# Optimizing a Trainium2 kernel written in Bass

```python
import math
import jax, jax.numpy as jnp
from jax import lax
import numpy as np

D_MODEL = 1024
BATCH = 1
SEQ = 256
DEPTH = 2

HEAD_DIM = 64
ROT_DIM = HEAD_DIM // 4
ROPE_THETA = 500000.0
DIFF_HEADS = 4
DIFF_VDIM = 2 * HEAD_DIM
SB_HEADS = 8
MOBA_HEADS = 8
MOBA_BLOCK = 256
MOBA_TOPK = 3
MOBA_Q_CHUNK = 64
Q_BLOCK = 128
FFN_DIM = 2816
NORM_EPS = 1e-6
DIFF_QK_W = DIFF_HEADS * 2 * HEAD_DIM
DIFF_W = DIFF_HEADS * DIFF_VDIM
SB_W = SB_HEADS * HEAD_DIM
MOBA_W = MOBA_HEADS * HEAD_DIM
IN_SIZES = (DIFF_QK_W, DIFF_QK_W, DIFF_W, SB_W, SB_W, SB_W, MOBA_W, MOBA_W, MOBA_W, D_MODEL, D_MODEL, D_MODEL)
IN_W = 3 * (DIFF_QK_W + DIFF_QK_W // 2) + 3 * SB_W + 3 * MOBA_W - 3 * (DIFF_QK_W // 2) + 3 * D_MODEL - 3 * DIFF_QK_W + DIFF_QK_W * 2 + DIFF_W


def rms_norm(x, gain):
    xf = x.astype(jnp.float32)
    y = xf * lax.rsqrt(jnp.mean(xf * xf, axis=-1, keepdims=True) + NORM_EPS)
    return (y * gain.astype(jnp.float32)).astype(x.dtype)

def swiglu(x, wg, wu, wd):
    return (jax.nn.silu(x @ wg) * (x @ wu)) @ wd

def rope_tables(seq_len):
    pos = jnp.arange(seq_len, dtype=jnp.float32)
    inv_freq = ROPE_THETA ** (-jnp.arange(0, ROT_DIM, 2, dtype=jnp.float32) / ROT_DIM)
    ang = pos[:, None] * inv_freq[None, :]
    return jnp.cos(ang), jnp.sin(ang)

def partial_rope(x, cos, sin):
    half = ROT_DIM // 2
    c = cos.astype(x.dtype)
    s = sin.astype(x.dtype)
    x1 = x[..., :half]
    x2 = x[..., half:ROT_DIM]
    return jnp.concatenate([x1 * c - x2 * s, x2 * c + x1 * s, x[..., ROT_DIM:]], axis=-1)

def split_heads(t, n_heads):
    b, s, _ = t.shape
    return t.reshape(b, s, n_heads, -1).transpose(0, 2, 1, 3)

def merge_heads(t):
    b, h, s, d = t.shape
    return t.transpose(0, 2, 1, 3).reshape(b, s, h * d)

def sweep_blocks(fn, n_blocks):
    out = lax.map(fn, jnp.arange(n_blocks))
    n, b, h, blk, d = out.shape
    return out.transpose(1, 2, 0, 3, 4).reshape(b, h, n * blk, d)

def diff_attention(q, k, v, lam, cos, sin):
    seq = q.shape[3]
    q = partial_rope(q, cos, sin)
    k = partial_rope(k, cos, sin)
    scale = HEAD_DIM ** -0.5
    kpos = jnp.arange(seq)
    lam = lam.astype(jnp.float32)

    def block(i):
        q0 = i * Q_BLOCK
        qb = lax.dynamic_slice_in_dim(q, q0, Q_BLOCK, axis=3)
        logits = jnp.einsum('bhmqd,bhmkd->bhmqk', qb, k).astype(jnp.float32) * scale
        qpos = q0 + jnp.arange(Q_BLOCK)
        causal = kpos[None, :] <= qpos[:, None]
        p = jax.nn.softmax(jnp.where(causal, logits, -jnp.inf), axis=-1)
        w = p[:, :, 0] - lam * p[:, :, 1]
        return jnp.einsum('bhqk,bhkd->bhqd', w.astype(v.dtype), v)

    return sweep_blocks(block, seq // Q_BLOCK)

def stick_breaking_attention(q, k, v):
    seq = q.shape[2]
    scale = HEAD_DIM ** -0.5
    kpos = jnp.arange(seq)

    def block(i):
        q0 = i * Q_BLOCK
        qb = lax.dynamic_slice_in_dim(q, q0, Q_BLOCK, axis=2)
        z = jnp.einsum('bhqd,bhkd->bhqk', qb, k).astype(jnp.float32) * scale
        qpos = q0 + jnp.arange(Q_BLOCK)
        strict = kpos[None, :] < qpos[:, None]
        log_keep = jnp.where(strict, jax.nn.log_sigmoid(-z), 0.0)
        shifted = jnp.concatenate([log_keep[..., 1:], jnp.zeros_like(log_keep[..., :1])], axis=-1)
        log_surv = lax.cumsum(shifted, axis=3, reverse=True)
        w = jnp.where(strict, jnp.exp(jax.nn.log_sigmoid(z) + log_surv), 0.0)
        return jnp.einsum('bhqk,bhkd->bhqd', w.astype(v.dtype), v)

    return sweep_blocks(block, seq // Q_BLOCK)

def moba_attention(q, k, v, cos, sin):
    b, h, seq, hd = q.shape
    q = partial_rope(q, cos, sin)
    k = partial_rope(k, cos, sin)
    nb = -(-seq // MOBA_BLOCK)
    pad = nb * MOBA_BLOCK - seq
    kp = jnp.pad(k, ((0, 0), (0, 0), (0, pad), (0, 0)))
    vp = jnp.pad(v, ((0, 0), (0, 0), (0, pad), (0, 0)))
    kblk = kp.reshape(b, h, nb, MOBA_BLOCK, hd)
    vblk = vp.reshape(b, h, nb, MOBA_BLOCK, hd)
    kmean = jnp.mean(kblk, axis=3)
    topk = min(MOBA_TOPK, nb)
    scale = hd ** -0.5
    blk_ids = jnp.arange(nb)
    gather = jax.vmap(jax.vmap(lambda a, idx: a[idx]))

    def chunk(i):
        q0 = i * MOBA_Q_CHUNK
        qb = lax.dynamic_slice_in_dim(q, q0, MOBA_Q_CHUNK, axis=2)
        qpos = q0 + jnp.arange(MOBA_Q_CHUNK)
        own = q0 // MOBA_BLOCK
        gate = jnp.einsum('bhqd,bhnd->bhqn', qb, kmean).astype(jnp.float32)
        gate = jnp.where(blk_ids < own, gate, -jnp.inf)
        _, idx = lax.top_k(gate, topk)
        ksel = gather(kblk, idx)
        vsel = gather(vblk, idx)
        past_ok = jnp.arange(topk) < own
        lp = jnp.einsum('bhqd,bhqrkd->bhqrk', qb, ksel).astype(jnp.float32) * scale
        lp = jnp.where(past_ok[:, None], lp, -jnp.inf).reshape(b, h, MOBA_Q_CHUNK, topk * MOBA_BLOCK)
        kown = lax.dynamic_slice_in_dim(kp, own * MOBA_BLOCK, MOBA_BLOCK, axis=2)
        vown = lax.dynamic_slice_in_dim(vp, own * MOBA_BLOCK, MOBA_BLOCK, axis=2)
        lo = jnp.einsum('bhqd,bhkd->bhqk', qb, kown).astype(jnp.float32) * scale
        own_pos = own * MOBA_BLOCK + jnp.arange(MOBA_BLOCK)
        lo = jnp.where(own_pos[None, :] <= qpos[:, None], lo, -jnp.inf)
        p = jax.nn.softmax(jnp.concatenate([lp, lo], axis=-1), axis=-1)
        pp = p[..., :topk * MOBA_BLOCK].reshape(b, h, MOBA_Q_CHUNK, topk, MOBA_BLOCK).astype(v.dtype)
        po = p[..., topk * MOBA_BLOCK:].astype(v.dtype)
        return (jnp.einsum('bhqrk,bhqrkd->bhqd', pp, vsel)
                + jnp.einsum('bhqk,bhkd->bhqd', po, vown))

    return sweep_blocks(chunk, seq // MOBA_Q_CHUNK)

def hybrid_mixer(h, w_in, w_diff_o, w_sb_o, w_moba_o, w_out,
                 lq1, lk1, lq2, lk2, diff_g, lambda_init, cos, sin):
    b, s, _ = h.shape
    proj = h @ w_in
    offsets = np.cumsum(IN_SIZES)[:-1].tolist()
    (dq, dk, dv, sq, sk, sv, mq, mk, mv, g_diff, g_sb, g_moba) = jnp.split(proj, offsets, axis=-1)

    dq = dq.reshape(b, s, DIFF_HEADS, 2, HEAD_DIM).transpose(0, 2, 3, 1, 4)
    dk = dk.reshape(b, s, DIFF_HEADS, 2, HEAD_DIM).transpose(0, 2, 3, 1, 4)
    lam = (jnp.exp(jnp.sum(lq1.astype(jnp.float32) * lk1.astype(jnp.float32)))
           - jnp.exp(jnp.sum(lq2.astype(jnp.float32) * lk2.astype(jnp.float32))) + lambda_init)
    a_out = diff_attention(dq, dk, split_heads(dv, DIFF_HEADS), lam, cos, sin)
    a_out = merge_heads(rms_norm(a_out, diff_g) * (1.0 - lambda_init))

    b_out = merge_heads(stick_breaking_attention(split_heads(sq, SB_HEADS),
                                                 split_heads(sk, SB_HEADS),
                                                 split_heads(sv, SB_HEADS)))
    c_out = merge_heads(moba_attention(split_heads(mq, MOBA_HEADS),
                                       split_heads(mk, MOBA_HEADS),
                                       split_heads(mv, MOBA_HEADS), cos, sin))

    merged = (jax.nn.sigmoid(g_diff) * (a_out @ w_diff_o)
              + jax.nn.sigmoid(g_sb) * (b_out @ w_sb_o)
              + jax.nn.sigmoid(g_moba) * (c_out @ w_moba_o))
    return merged @ w_out

def first_inputs(seed: int = 0) -> dict:
    key = jax.random.key(seed)
    ks = jax.random.split(key, 24)
    f32 = jnp.float32

    def nrm(k, shape, fan_in):
        return jax.random.normal(k, shape, f32) * (fan_in ** -0.5)

    def gain(k, shape):
        return 1.0 + 0.02 * jax.random.normal(k, shape, f32)

    L, D = DEPTH, D_MODEL
    return {
        "x": jax.random.normal(ks[0], (BATCH, SEQ, D), f32),
        "w_in": nrm(ks[1], (L, D, IN_W), D),
        "w_diff_o": nrm(ks[2], (L, DIFF_W, D), DIFF_W),
        "w_sb_o": nrm(ks[3], (L, SB_W, D), SB_W),
        "w_moba_o": nrm(ks[4], (L, MOBA_W, D), MOBA_W),
        "w_out": nrm(ks[5], (L, D, D), D),
        "lam_q1": 0.1 * jax.random.normal(ks[6], (L, HEAD_DIM), f32),
        "lam_k1": 0.1 * jax.random.normal(ks[7], (L, HEAD_DIM), f32),
        "lam_q2": 0.1 * jax.random.normal(ks[8], (L, HEAD_DIM), f32),
        "lam_k2": 0.1 * jax.random.normal(ks[9], (L, HEAD_DIM), f32),
        "diff_norm_g": gain(ks[10], (L, DIFF_VDIM)),
        "ffn1_wg": nrm(ks[11], (L, D, FFN_DIM), D),
        "ffn1_wu": nrm(ks[12], (L, D, FFN_DIM), D),
        "ffn1_wd": nrm(ks[13], (L, FFN_DIM, D), FFN_DIM),
        "ffn2_wg": nrm(ks[14], (L, D, FFN_DIM), D),
        "ffn2_wu": nrm(ks[15], (L, D, FFN_DIM), D),
        "ffn2_wd": nrm(ks[16], (L, FFN_DIM, D), FFN_DIM),
        "g_ffn1_pre": gain(ks[17], (L, D)),
        "g_ffn1_post": gain(ks[18], (L, D)),
        "g_mix_pre": gain(ks[19], (L, D)),
        "g_mix_post": gain(ks[20], (L, D)),
        "g_ffn2_pre": gain(ks[21], (L, D)),
        "g_ffn2_post": gain(ks[22], (L, D)),
    }

def first_block(x, w_in, w_diff_o, w_sb_o, w_moba_o, w_out, lam_q1, lam_k1, lam_q2, lam_k2,
              diff_norm_g, ffn1_wg, ffn1_wu, ffn1_wd, ffn2_wg, ffn2_wu, ffn2_wd,
              g_ffn1_pre, g_ffn1_post, g_mix_pre, g_mix_post, g_ffn2_pre, g_ffn2_post):
    cos, sin = rope_tables(x.shape[1])
    for l in range(DEPTH):
        lambda_init = 0.8 - 0.6 * math.exp(-0.3 * l)
        x = x + 0.5 * rms_norm(swiglu(rms_norm(x, g_ffn1_pre[l]), ffn1_wg[l], ffn1_wu[l], ffn1_wd[l]),
                               g_ffn1_post[l])
        mixed = hybrid_mixer(rms_norm(x, g_mix_pre[l]), w_in[l], w_diff_o[l], w_sb_o[l], w_moba_o[l],
                             w_out[l], lam_q1[l], lam_k1[l], lam_q2[l], lam_k2[l], diff_norm_g[l],
                             lambda_init, cos, sin)
        x = x + rms_norm(mixed, g_mix_post[l])
        x = x + 0.5 * rms_norm(swiglu(rms_norm(x, g_ffn2_pre[l]), ffn2_wg[l], ffn2_wu[l], ffn2_wd[l]),
                               g_ffn2_post[l])
    return x


D_FF = 2816
HG_DK = 128
HG_HEADS = D_MODEL // HG_DK
HG_DV = D_MODEL // HG_HEADS
HG_WK = HG_HEADS * HG_DK
HG_WV = HG_HEADS * HG_DV
HG_CHUNK = 64
ATT_PATTERNS = ((128, 1), (512, 4), (2048, 16))
ATT_GROUPS = 3
ATT_HEADS = 4
ATT_DH = 128
ATT_W = ATT_GROUPS * ATT_HEADS * ATT_DH
ATT_OUT = ATT_HEADS * ATT_DH
ROPE_THETA_2 = 10000.0
EPS = 1e-6
SPLIT_SIZES = (HG_WK, HG_WK, HG_WV, HG_WV, ATT_W, ATT_W, ATT_W, D_MODEL, D_MODEL)
P_IN = sum(SPLIT_SIZES)


def rms(x):
    xf = x.astype(jnp.float32)
    return xf * lax.rsqrt(jnp.mean(xf * xf, axis=-1, keepdims=True) + EPS)

def rmsnorm(x, g):
    return (rms(x) * g.astype(jnp.float32)).astype(x.dtype)

def swiglu_2(h, w_in, w_out):
    a, b = jnp.split(h @ w_in, 2, axis=-1)
    return (jax.nn.silu(a) * b) @ w_out

def rope_tables_2(t):
    pos = jnp.arange(t, dtype=jnp.float32)
    inv = ROPE_THETA_2 ** (-jnp.arange(0, ATT_DH, 2, dtype=jnp.float32) / ATT_DH)
    ang = pos[:, None] * inv[None, :]
    ang = jnp.concatenate([ang, ang], axis=-1)
    return jnp.cos(ang), jnp.sin(ang)

def apply_rope(x, cos, sin):
    x1, x2 = jnp.split(x, 2, axis=-1)
    return x * cos + jnp.concatenate([-x2, x1], axis=-1) * sin

def hgrn2_chunk_scan(q, k, v, log_f):
    b, t, h, dk = q.shape
    dv = v.shape[-1]
    n = t // HG_CHUNK

    def chunks(a):
        return a.reshape(b, n, HG_CHUNK, h, a.shape[-1]).transpose(1, 0, 3, 2, 4)

    causal = jnp.tril(jnp.ones((HG_CHUNK, HG_CHUNK), dtype=bool))[:, :, None]

    def step(state, inp):
        qc, kc, vc, gc = inp
        gcum = jnp.cumsum(gc, axis=2)
        diff = gcum[:, :, :, None, :] - gcum[:, :, None, :, :]
        decay = jnp.exp(jnp.where(causal, diff, -jnp.inf))
        attn = jnp.einsum('bhtk,bhsk,bhtsk->bhts', qc, kc, decay)
        o = jnp.einsum('bhts,bhsv->bhtv', attn, vc) + jnp.einsum(
            'bhtk,bhkv->bhtv', qc * jnp.exp(gcum), state)
        g_last = gcum[:, :, -1:, :]
        state = jnp.exp(g_last[:, :, 0, :, None]) * state + jnp.einsum(
            'bhsk,bhsv->bhkv', kc * jnp.exp(g_last - gcum), vc)
        return state, o

    s0 = jnp.zeros((b, h, dk, dv), jnp.float32)
    _, o = lax.scan(step, s0, (chunks(q), chunks(k), chunks(v), chunks(log_f)))
    return o.transpose(1, 0, 3, 2, 4).reshape(b, t, h * dv)

def dilated_window_attention(q, k, v, window, dilation):
    b, h, t, dh = q.shape
    back = window // dilation
    blk = back
    L = t // dilation
    nb = -(-L // blk)
    Lp = nb * blk

    def to_res(a):
        a = a.reshape(b, h, L, dilation, dh).transpose(0, 1, 3, 2, 4)
        return jnp.pad(a, ((0, 0), (0, 0), (0, 0), (0, Lp - L), (0, 0)))

    def kv_blocks(a):
        a = jnp.pad(a, ((0, 0), (0, 0), (0, 0), (blk, 0), (0, 0)))
        a = a.reshape(b, h, dilation, nb + 1, blk, dh)
        return jnp.concatenate([a[:, :, :, :-1], a[:, :, :, 1:]], axis=4)

    qb = to_res(q).reshape(b, h, dilation, nb, blk, dh)
    kb = kv_blocks(to_res(k))
    vb = kv_blocks(to_res(v))
    s = jnp.einsum('bhrnqd,bhrnkd->bhrnqk', qb, kb) * (dh ** -0.5)
    qi = jnp.arange(blk)[:, None]
    ki = jnp.arange(2 * blk)[None, :]
    band = (ki >= qi) & (ki <= qi + back)
    valid = (ki >= blk)[None] | (jnp.arange(nb)[:, None, None] > 0)
    mask = band[None] & valid
    s = jnp.where(mask, s, -jnp.inf)
    lse = jax.nn.logsumexp(s, axis=-1)
    p = jnp.exp(s - lse[..., None])
    o = jnp.einsum('bhrnqk,bhrnkd->bhrnqd', p, vb)
    o = o.reshape(b, h, dilation, Lp, dh)[:, :, :, :L].transpose(0, 1, 3, 2, 4)
    lse = lse.reshape(b, h, dilation, Lp)[:, :, :, :L].transpose(0, 1, 3, 2)
    return o.reshape(b, h, t, dh), lse.reshape(b, h, t)

def second_inputs(seed: int = 0) -> dict:
    key = jax.random.key(seed)
    ks = jax.random.split(key, 16)
    f32 = jnp.float32

    def nrm(k, shape, fan_in):
        return jax.random.normal(k, shape, f32) * (fan_in ** -0.5)

    def gain(k, shape):
        return 1.0 + 0.05 * jax.random.normal(k, shape, f32)

    return {
        "x": jax.random.normal(ks[0], (BATCH, SEQ, D_MODEL), f32),
        "ffn1_norm": gain(ks[1], (DEPTH, D_MODEL)),
        "ffn1_w_in": nrm(ks[2], (DEPTH, D_MODEL, 2 * D_FF), D_MODEL),
        "ffn1_w_out": nrm(ks[3], (DEPTH, D_FF, D_MODEL), D_FF),
        "mix_norm": gain(ks[4], (DEPTH, D_MODEL)),
        "w_in": nrm(ks[5], (DEPTH, D_MODEL, P_IN), D_MODEL),
        "hgrn_lb_logits": 0.5 * jax.random.normal(ks[6], (DEPTH, HG_WK), f32),
        "hgrn_out_norm": gain(ks[7], (DEPTH, HG_WV)),
        "attn_q_norm": gain(ks[8], (DEPTH, ATT_GROUPS, ATT_DH)),
        "attn_k_norm": gain(ks[9], (DEPTH, ATT_GROUPS, ATT_DH)),
        "w_branch_a": nrm(ks[10], (DEPTH, HG_WV, D_MODEL), HG_WV),
        "w_branch_b": nrm(ks[11], (DEPTH, ATT_OUT, D_MODEL), ATT_OUT),
        "w_out": nrm(ks[12], (DEPTH, D_MODEL, D_MODEL), D_MODEL),
        "ffn2_norm": gain(ks[13], (DEPTH, D_MODEL)),
        "ffn2_w_in": nrm(ks[14], (DEPTH, D_MODEL, 2 * D_FF), D_MODEL),
        "ffn2_w_out": nrm(ks[15], (DEPTH, D_FF, D_MODEL), D_FF),
    }

def second_block(x, ffn1_norm, ffn1_w_in, ffn1_w_out, mix_norm, w_in, hgrn_lb_logits,
              hgrn_out_norm, attn_q_norm, attn_k_norm, w_branch_a, w_branch_b, w_out,
              ffn2_norm, ffn2_w_in, ffn2_w_out):
    b, t, _ = x.shape
    f32 = jnp.float32
    cos, sin = rope_tables_2(t)
    lb_all = jnp.cumsum(jax.nn.softmax(hgrn_lb_logits.astype(f32), axis=0), axis=0)
    lb_all = lb_all - lb_all[0:1]
    split_idx = [int(s) for s in np.cumsum(SPLIT_SIZES)[:-1]]

    for l in range(DEPTH):
        x = x + 0.5 * swiglu_2(rmsnorm(x, ffn1_norm[l]), ffn1_w_in[l], ffn1_w_out[l])

        h = rmsnorm(x, mix_norm[l])
        hq, hf, hi, hg, aq, ak, av, ga, gb = jnp.split(h @ w_in[l], split_idx, axis=-1)

        lb = lb_all[l]
        f = lb + (1.0 - lb) * jax.nn.sigmoid(hf.astype(f32))
        q_a = jax.nn.silu(hq.astype(f32)).reshape(b, t, HG_HEADS, HG_DK)
        k_a = (1.0 - f).reshape(b, t, HG_HEADS, HG_DK)
        v_a = hi.astype(f32).reshape(b, t, HG_HEADS, HG_DV)
        log_f = jnp.log(f).reshape(b, t, HG_HEADS, HG_DK)
        o_a = hgrn2_chunk_scan(q_a, k_a, v_a, log_f)
        o_a = rms(o_a.reshape(b, t, HG_HEADS, HG_DV)).reshape(b, t, HG_WV)
        o_a = o_a * hgrn_out_norm[l].astype(f32) * jax.nn.silu(hg.astype(f32))
        y_a = o_a.astype(x.dtype) @ w_branch_a[l]

        def heads(a):
            return a.reshape(b, t, ATT_GROUPS, ATT_HEADS, ATT_DH).transpose(2, 0, 3, 1, 4).astype(f32)

        qn = attn_q_norm[l].astype(f32)[:, None, None, None, :]
        kn = attn_k_norm[l].astype(f32)[:, None, None, None, :]
        q_b = apply_rope(rms(heads(aq)) * qn, cos, sin)
        k_b = apply_rope(rms(heads(ak)) * kn, cos, sin)
        v_b = heads(av)
        outs, lses = [], []
        for g, (window, dilation) in enumerate(ATT_PATTERNS):
            o_g, lse_g = dilated_window_attention(q_b[g], k_b[g], v_b[g], window, dilation)
            outs.append(o_g)
            lses.append(lse_g)
        alpha = jax.nn.softmax(jnp.stack(lses, axis=0), axis=0)
        o_b = jnp.einsum('gbht,gbhtd->bthd', alpha, jnp.stack(outs, axis=0)).reshape(b, t, ATT_OUT)
        y_b = o_b.astype(x.dtype) @ w_branch_b[l]

        merged = jax.nn.sigmoid(ga) * y_a + jax.nn.sigmoid(gb) * y_b
        x = x + merged @ w_out[l]

        x = x + 0.5 * swiglu_2(rmsnorm(x, ffn2_norm[l]), ffn2_w_in[l], ffn2_w_out[l])
    return x


def setup_inputs(seed=0):
    out = dict(first_inputs(seed))
    for name, value in second_inputs(seed + 1).items():
        if name != "x":
            out[name + "_2"] = value
    return out


def reference(
    x, w_in, w_diff_o, w_sb_o, w_moba_o, w_out, lam_q1, lam_k1, lam_q2, lam_k2, diff_norm_g,
    ffn1_wg, ffn1_wu, ffn1_wd, ffn2_wg, ffn2_wu, ffn2_wd, g_ffn1_pre, g_ffn1_post, g_mix_pre,
    g_mix_post, g_ffn2_pre, g_ffn2_post, ffn1_norm_2, ffn1_w_in_2, ffn1_w_out_2, mix_norm_2,
    w_in_2, hgrn_lb_logits_2, hgrn_out_norm_2, attn_q_norm_2, attn_k_norm_2, w_branch_a_2,
    w_branch_b_2, w_out_2, ffn2_norm_2, ffn2_w_in_2, ffn2_w_out_2,
):
    x = first_block(
        x, w_in, w_diff_o, w_sb_o, w_moba_o, w_out, lam_q1, lam_k1, lam_q2, lam_k2, diff_norm_g,
        ffn1_wg, ffn1_wu, ffn1_wd, ffn2_wg, ffn2_wu, ffn2_wd, g_ffn1_pre, g_ffn1_post,
        g_mix_pre, g_mix_post, g_ffn2_pre, g_ffn2_post,
    )
    return second_block(
        x, ffn1_norm_2, ffn1_w_in_2, ffn1_w_out_2, mix_norm_2, w_in_2, hgrn_lb_logits_2,
        hgrn_out_norm_2, attn_q_norm_2, attn_k_norm_2, w_branch_a_2, w_branch_b_2, w_out_2,
        ffn2_norm_2, ffn2_w_in_2, ffn2_w_out_2,
    )


_drawn_inputs = setup_inputs


def setup_inputs(seed=0):
    import zlib

    import numpy as np

    out = dict(_drawn_inputs(seed))
    spreads = {}
    factors = {'lam_q2': 2.987,
     'diff_norm_g': 3.211,
     'g_ffn1_post': 3.541,
     'g_ffn2_pre': 4.063,
     'g_ffn2_post': 5.985,
     'ffn1_norm_2': 3.648,
     'mix_norm_2': 2.997,
     'hgrn_lb_logits_2': 7.728,
     'hgrn_out_norm_2': 4.934,
     'attn_q_norm_2': 8.0,
     'attn_k_norm_2': 8.0,
     'ffn2_norm_2': 3.778}
    for name, (base, spread) in spreads.items():
        noise = np.random.default_rng([zlib.crc32(name.encode()), seed]).standard_normal(out[name].shape)
        drawn = base * np.exp(spread * noise) if base else spread * noise
        out[name] = __import__('jax').numpy.asarray(drawn.astype(out[name].dtype))
    for name, factor in factors.items():
        out[name] = (out[name] * factor).astype(out[name].dtype)
    return out
```

```python
import math
from contextlib import ExitStack

import numpy as np
import concourse.bass as bass
from concourse import mybir

F32 = mybir.dt.float32
F32R = mybir.dt.float32r
U32 = mybir.dt.uint32
ALU = mybir.AluOpType
ACT = mybir.ActivationFunctionType
AX = mybir.AxisListType

P = 128
SEQ = 256
TT = SEQ // P
D = 1024
KT = D // P
LAYERS = 2
EPS = 1e-6
NEG = -1e30
FFN = 2816
FC = 256
FSTEPS = FFN // FC
UNIT = 2048
SLOTS = 3
FREE = 1
X_IN = 16
EXP_LN = "natural_log_exp_and_others"

HD = 64
ROT = HD // 4
DIFF_HEADS, SB_HEADS, MOBA_HEADS = 4, 8, 8
IN1 = 9 * 512 + 3 * D
CH1 = IN1 // 512
Q_DIFF, K_DIFF, V_DIFF, Q_SB, K_SB, V_SB, Q_MOBA, K_MOBA, V_MOBA = range(9)
PROJ1 = 2 * CH1
MIX1 = PROJ1 + 6 + 4

HG_HEADS = 8
ATT_GROUPS, ATT_HEADS, DH = 3, 4, 128
PATTERNS = ((128, 1), (512, 4), (2048, 16))
IN2 = 4 * D + 3 * 1536 + 2 * D
HQ, HF, HI, HG, AQ, AK, AV, GA, GB = 0, D, 2 * D, 3 * D, 4 * D, 4 * D + 1536, 4 * D + 3072, 4 * D + 4608, 5 * D + 4608
CHUNKS2 = [HQ, HF, HQ + 512, HF + 512, HI, HI + 512, HG, HG + 512, AV, AV + 512, AV + 1024,
           AQ, AQ + 512, AQ + 1024, AK, AK + 512, AK + 1024, GA, GA + 512, GB, GB + 512]
CH2 = len(CHUNKS2)
PROJ2 = 2 * CH2
MIX2 = PROJ2 + 4 + 2 + 4
LEVELS = 9

C_G = {0: 0, 1: KT, 2: 2 * KT}
C1_DIFF, C1_LAM0, C1_LAM1, C1_LQK = 24, 25, 26, 27
NC1 = C1_LQK + 4 * HD
C2_OUT, C2_LB, C2_LAYER, C2_QK = 24, 32, 48, 49
NC2 = C2_QK + 2 * ATT_GROUPS * DH
NCOL = max(NC1, NC2)
K_ID, K_ONES, K_TRI = 0, P, 2 * P
NK0 = 3 * P
K1_CAUSAL, K1_KEEP, K1_DROP, K1_COS, K1_SIN = 0, 384, 768, 1152, 1152 + TT * 8
NK1 = K1_SIN + TT * 8
K2_COS, K2_SIN, K2_MASK, K2_LEV = 0, TT * DH, 2 * TT * DH, 2 * TT * DH + 3 * 384
NK2 = K2_LEV + 8 * P
NKB = max(NK1 + D, NK2)


def slot_uses(units, slot):
    return (units - slot + SLOTS - 1) // SLOTS


U1 = [2 * FSTEPS + slot_uses(MIX1, s) for s in range(SLOTS)]
U2 = [2 * FSTEPS + slot_uses(MIX2, s) for s in range(SLOTS)]


def at(lay, per_layer, k):
    return lay * per_layer + k


def use(blk, slot, lay, k):
    if blk == 1:
        return lay * U1[slot] + (FREE + k)
    return lay * U2[slot] + (FREE + LAYERS * (U1[slot] - U2[slot]) + k)


def ffn_use(blk, f, slot):
    return 0 if f == 0 else FSTEPS + slot_uses(MIX1 if blk == 1 else MIX2, slot)


def mix_use(u):
    return FSTEPS + u // SLOTS


LINKS = {1: 46, 2: 42}


def build(nc, t):
    ctx = ExitStack()
    with ctx:
        def sb(name, shape, dt=F32):
            return ctx.enter_context(nc.sbuf_tensor(name, shape, dt))

        def sem(name):
            return ctx.enter_context(nc.semaphore(name))

        raw = [sb(f"raw{s}", [P, UNIT]) for s in range(SLOTS)]
        wh = [sb(f"w_high{s}", [P, UNIT], F32R) for s in range(SLOTS)]
        wl = [sb(f"w_low{s}", [P, UNIT], F32R) for s in range(SLOTS)]
        X = sb("x_res", [P, TT, D])
        xh = sb("xT_high", [P, KT, SEQ], F32R)
        xl = sb("xT_low", [P, KT, SEQ], F32R)
        konst = sb("konst", [P, NK0])
        kblk = sb("kblk", [P, NKB])
        cols = sb("cols", [P, NCOL])
        grow = kblk[:, NK1:NK1 + D]
        neghalf = sb("neghalf", [P, 16])
        ss = sb("ss", [P, TT]); ms = sb("ms", [P, TT]); rstd = sb("rstd", [P, TT])
        ssy = sb("ssy", [P, TT, 2]); msy = sb("msy", [P, TT]); rsy = sb("rsy", [P, TT])
        lamp = sb("lam_prod", [P, 2, HD]); lams = sb("lam_sum", [P, 2]); lame = sb("lam_exp", [P, 2])
        lam = sb("lam", [P, 1]); gdiff = sb("gain_diff", [P, 1])
        nmx = sb("neg_max", [P, 4]); lsum = sb("exp_sum", [P, 4]); rsum = sb("inv_sum", [P, 4])
        rsl = sb("inv_sum_lam", [P, 2])
        rmo = sb("inv_moba", [P, TT, MOBA_HEADS]); lmo = sb("sum_moba", [P, TT, MOBA_HEADS])
        ssd = sb("ss_diff", [P, 8]); msd = sb("ms_diff", [P, 8]); rsd = sb("rstd_diff", [P, 8])
        lbe = sb("lb_exp", [P, 2, HG_HEADS]); lbm = sb("lb_max", [P, HG_HEADS]); lbs = sb("lb_sum", [P, HG_HEADS])
        lb = sb("lb", [P, HG_HEADS]); omlb = sb("one_minus_lb", [P, HG_HEADS])
        sso = sb("ss_o", [P, 8]); mso = sb("ms_o", [P, 8]); rso = sb("rstd_o", [P, 8])
        ssa = sb("ss_a", [P, 8]); msa = sb("ms_a", [P, 8]); rsa = sb("rstd_a", [P, 8])
        rat = sb("inv_att", [P, ATT_HEADS, TT]); lat = sb("sum_att", [P, ATT_HEADS, TT]); nma = sb("neg_max_att", [P, TT])

        ARENA = 94 * 1024
        arena = sb("arena", [P, ARENA // 4])
        base = nc.sbuf_base - ARENA

        def over(name, shape, kib, dt=F32):
            size = 4 * int(np.prod(shape[1:]))
            assert kib * 1024 + size <= ARENA, name
            return nc.alloc_sbuf_tensor_at(name, shape, dt, offset=int(base + kib * 1024))

        hTh = over("hT_high", [P, 2, SEQ], 0, F32R)
        hTl = over("hT_low", [P, 2, SEQ], 2, F32R)
        sil = over("silu", [P, TT, FC], 4)
        hid = over("hidden", [P, TT, FC], 6)
        tpost = over("post", [P, TT, D], 8)
        junk = over("squares", [P, TT, D], 16)

        vnat = [over(f"v{b}", [P, TT, 512], 4 * b) for b in range(3)]
        gate1 = [over(f"gate{b}", [P, TT, D], 12 + 8 * b) for b in range(3)]
        stage = [over(f"stage{i}", [P, TT, 512], 36 + 4 * i) for i in range(2)]
        secT = {Q_DIFF: over("dqT", [P, 4, SEQ], 44), K_DIFF: over("dkT", [P, 4, SEQ], 48),
                Q_SB: over("sqT", [P, 4, SEQ], 52), K_SB: over("skT", [P, 4, SEQ], 56),
                Q_MOBA: over("mqT", [P, 4, SEQ], 44), K_MOBA: over("mkT", [P, 4, SEQ], 48)}
        oTh = [over(f"oT_high{b}", [P, 4, SEQ], k, F32R) for b, k in enumerate((60, 52, 0))]
        oTl = [over(f"oT_low{b}", [P, 4, SEQ], k, F32R) for b, k in enumerate((64, 56, 4))]
        onat = [over("o_diff", [P, TT, 512], 68), over("o_sb", [P, TT, 512], 72), over("o_moba", [P, TT, 512], 68)]
        smk = [over(f"masked{m}", [P, 384], 76 + 1.5 * m) for m in range(2)]
        ex = [over(f"expd{m}", [P, 384], 79 + 1.5 * m) for m in range(2)]
        osq = over("o_sq", [P, TT, 512], 76)
        wdf = over("w_diff", [P, 384], 82)
        wT = [over(f"wT{i}", [P, 384], 83.5 + 1.5 * i) for i in range(2)]
        saz = over("sb_abs", [P, 384], 86.5)
        sex = over("sb_exp", [P, 384], 88)
        slk = over("sb_keep", [P, 384], 89.5)
        sag = over("sb_arg", [P, 384], 91)
        smx = over("sb_max", [P, 384], 92.5)
        rt = [over(f"rope_t{i}", [P, TT, 8, 8], 76 + 0.5 * i) for i in range(4)]
        mrg = over("merged1", [P, TT, D], 36)
        mtm = over("merge_term", [P, TT, 512], 76)

        qT = over("hqT", [P, HG_HEADS, SEQ], 0)
        kT = over("hkT", [P, HG_HEADS, SEQ], 8)
        gc = over("log_decay", [P, HG_HEADS, SEQ], 16)
        dl = over("decay", [P, 4, SEQ], 24)
        Av = over("decayed", [P, 4, SEQ], 28)
        att = over("hg_att", [P, 4, 3, P], 32)
        hv = over("hg_v", [P, TT, D], 38)
        hgt = over("hg_gate", [P, TT, D], 46)
        stg = [over(f"stage2_{i}", [P, TT, 512], 54 + 4 * i) for i in range(2)]
        aqT = over("aqT", [P, 12, SEQ], 62)
        rsq = over("rope_sq", [P, TT, 512], 74)
        rtm = over("rope_tm", [P, TT, 512], 78)
        av = over("a_v", [P, 3, TT, 512], 82)
        akT = over("akT", [P, 12, SEQ], 0)
        ob = over("o_b", [P, TT, 512], 12)
        oaTh = over("oaT_high", [P, KT, SEQ], 16, F32R)
        oaTl = over("oaT_low", [P, KT, SEQ], 24, F32R)
        gate2 = [over(f"gate2_{b}", [P, TT, D], 32 + 8 * b) for b in range(2)]
        sma = over("masked_att", [P, 3, 384], 48)
        wTa = over("wT_att", [P, 3, 384], 54)
        exa = over("exp_att", [P, 3, 384], 74)
        obTh = over("obT_high", [P, 4, SEQ], 62, F32R)
        obTl = over("obT_low", [P, 4, SEQ], 66, F32R)
        mrg2 = over("merged2", [P, TT, D], 0)
        mtm2 = over("merge_term2", [P, TT, 512], 74)
        osb = [over("o_half0", [P, 4, TT, P], 74), over("o_half1", [P, 4, TT, P], 24)]
        oq = [over("o_sq0", [P, 4, TT, P], 78), over("o_sq1", [P, 4, TT, P], 28)]

        ps = [ctx.enter_context(nc.psum_tensor(f"bank{b}", [P, 512], F32)) for b in range(8)]
        acc = [[ps[0], ps[1]], [ps[2], ps[3]]]
        wk = ps[4:8]
        DOWN = [[ps[4], ps[5]], [ps[6], ps[7]]]
        YMIX = [[ps[2], ps[0]], [ps[3], ps[1]]]

        ident = konst[:, K_ID:K_ID + P]
        ones = konst[:, K_ONES:K_ONES + P]
        tri = konst[:, K_TRI:K_TRI + P]

        konst_in = sem("konst_in"); kblk_in = sem("kblk_in"); cols_in = sem("cols_in"); grow_in = sem("grow_in")
        out_sent = sem("out_sent"); const_set = sem("const_set")
        raw_in = [sem(f"raw_in{s}") for s in range(SLOTS)]
        high_done = [sem(f"high_done{s}") for s in range(SLOTS)]
        low_done = [sem(f"low_done{s}") for s in range(SLOTS)]
        slot_used = [sem(f"slot_used{s}") for s in range(SLOTS)]
        x_ready = sem("x_ready"); xT_done = sem("xT_done"); xh_done = sem("xh_done"); xl_done = sem("xl_done")
        ss_done = sem("ss_done"); ms_done = sem("ms_done"); rstd_done = sem("rstd_done")
        silu_done = sem("silu_done"); hid_done = sem("hid_done")
        hT_done = sem("hT_done"); hTh_done = sem("hTh_done"); hTl_done = sem("hTl_done")
        ssy_done = sem("ssy_done"); msy_done = sem("msy_done"); rsy_done = sem("rsy_done")
        dve_link = sem("dve_link"); lam_sum = sem("lam_sum_done"); lam_exp = sem("lam_exp_done")
        chunk_out = sem("chunk_out")
        rope_done = sem("rope_done"); sec_T = sem("sec_T"); sec_out = sem("sec_out")
        score_done = sem("score_done"); mask_done = sem("mask_done"); max_done = sem("max_done"); exp_done = sem("exp_done")
        wdf_done = sem("wdf_done"); wT_done = sem("wT_done"); wT_out = sem("wT_out")
        z_done = sem("z_done"); abs_done = sem("abs_done"); sbe_done = sem("sbe_done"); ln_done = sem("ln_done")
        keep_done = sem("keep_done"); cum_done = sem("cum_done"); arg_done = sem("arg_done"); sbw_done = sem("sbw_done")
        pv_done = sem("pv_done"); o_out = sem("o_out")
        osq_done = sem("osq_done"); od_ms = sem("od_ms"); od_pow = sem("od_pow"); od_done = sem("od_done")
        oT_done = sem("oT_done"); oTh_done = sem("oTh_done"); oTl_done = sem("oTl_done")
        proj_out = sem("proj_out"); sig_done = sem("sig_done"); merged = sem("merged")
        mT_done = sem("mT_done"); mTh_done = sem("mTh_done"); mTl_done = sem("mTl_done")
        lbx = sem("lb_exp_done"); lbw = sem("lb_max_done")
        f_done = sem("f_done"); lnf_done = sem("lnf_done"); g_done = sem("g_done"); k_done = sem("k_done")
        diff_ready = sem("diff_ready"); dec_done = sem("dec_done"); A_done = sem("A_done")
        lev_done = sem("lev_done"); lev_out = sem("lev_out")
        pvh_done = sem("pvh_done"); oh_out = sem("oh_out"); oh_sq = sem("oh_sq"); oh_ms = sem("oh_ms"); oh_pow = sem("oh_pow")
        hgs_done = sem("hgs_done"); oa_done = sem("oa_done")
        asq_done = sem("asq_done"); ams_done = sem("ams_done"); apow_done = sem("apow_done")
        
        chunk_out2 = sem("chunk_out2"); dT_done = sem("dT_done"); dexp_done = sem("dexp_done"); dmax_done = sem("dmax_done"); dpv_done = sem("dpv_done")
        dsc_done = sem("dsc_done"); hq_out = sem("hq_out"); mT_done2 = sem("mT_done2"); mTh_done2 = sem("mTh_done2"); mTl_done2 = sem("mTl_done2")
        merged2 = sem("merged2"); oaT_done = sem("oaT_done"); oaTh_done = sem("oaTh_done"); oaTl_done = sem("oaTl_done"); obT_done = sem("obT_done")
        obTh_done = sem("obTh_done"); obTl_done = sem("obTl_done"); ob_out = sem("ob_out"); proj_out2 = sem("proj_out2"); rope_done2 = sem("rope_done2")
        sec_T2 = sem("sec_T2"); sec_out2 = sem("sec_out2"); sig_done2 = sem("sig_done2"); wTa_out = sem("wTa_out")
        links = {}

        def split_high(act, blk, slot, lay, k):
            act.wait_ge(raw_in[slot], use(blk, slot, lay, k + 1 - FREE) * 32)
            act.wait_ge(slot_used[slot], use(blk, slot, lay, k))
            nc.scalar.activation(wh[slot][:], raw[slot][:], ACT.Copy).then_inc(high_done[slot], 1)

        def split_low(eng, ops, blk, slot, lay, k):
            eng.wait_ge(high_done[slot], use(blk, slot, lay, k + 1 - FREE))
            ops.tensor_tensor(wl[slot][:], raw[slot][:], wh[slot][:].bitcast(F32), ALU.subtract).then_inc(low_done[slot], 1)

        def product(pe, outs, xhi, xlo, slot, col, n, start, stop):
            for tt in range(TT):
                rows = slice(tt * P, (tt + 1) * P)
                for x, w, first, last in ((xhi, wh, True, False), (xhi, wl, False, False), (xlo, wh, False, True)):
                    for j, o in enumerate(outs[tt]):
                        mm = pe.matmul(o[:, 0:n], x[:, rows], w[slot][:, col + j * n:col + (j + 1) * n],
                                       start=start and first, stop=stop and last)
            return mm

        def norm_pe(pe, lay, n):
            pe.wait_ge(konst_in, 16)
            pe.wait_ge(x_ready, at(lay, 6, X_IN + 2 * n))
            for tt in range(TT):
                for kt in range(KT):
                    tr = pe.transpose(wk[kt // 2][:, (kt % 2) * SEQ + tt * P:(kt % 2) * SEQ + (tt + 1) * P],
                                      X[:, tt, kt * P:(kt + 1) * P], ident)
                    if tt == TT - 1 and kt % 2:
                        tr.then_inc(xT_done, 1)

        def norm_act(act, lay, n):
            for kt in range(KT):
                if kt % 2 == 0:
                    act.wait_ge(xT_done, at(lay, 12, 4 * n + kt // 2 + 1))
                if n == 0 and kt == 0:
                    act.wait_ge(cols_in, 16 * (lay + 1))
                nc.scalar.activation(xh[:, kt, :], wk[kt // 2][:, (kt % 2) * SEQ:(kt % 2 + 1) * SEQ], ACT.Copy,
                                     scale=cols[:, C_G[n] + kt:C_G[n] + kt + 1]).then_inc(xh_done, 1)
            for tt in range(TT):
                nc.scalar.activation(junk[:, tt, :], X[:, tt, :], ACT.Square, accum_out=ss[:, tt:tt + 1]).then_inc(ss_done, 1)

        def norm_dve(dve, lay, n):
            for kt in range(KT):
                dve.wait_ge(xh_done, at(lay, 24, 8 * n + kt + 1))
                if kt % 2 == 0:
                    dve.wait_ge(xh_done, at(lay, 24, 8 * n + kt + 2))
                nc.vector.scalar_tensor_tensor(xl[:, kt, :], wk[kt // 2][:, (kt % 2) * SEQ:(kt % 2 + 1) * SEQ],
                                               cols[:, C_G[n] + kt:C_G[n] + kt + 1], xh[:, kt, :].bitcast(F32),
                                               ALU.mult, ALU.subtract).then_inc(xl_done, 1)
            dve.wait_ge(ss_done, at(lay, 6, 2 * n + 2))
            nc.vector.tensor_scalar(ms[:], ss[:], 1.0 / D, EPS, ALU.mult, ALU.add).then_inc(ms_done, 1)

        def norm_pool(pool, lay, n):
            pool.wait_ge(ms_done, at(lay, 3, n + 1))
            nc.gpsimd.tensor_tensor(rstd[:], ms[:], neghalf[:, 0:TT], ALU.pow).then_inc(rstd_done, 1)

        def ffn_pe(pe, blk, lay, f):
            def up(i):
                for s in range(2):
                    if isinstance(i, int) and i == 0:
                        pe.wait_ge(xl_done, at(lay, 24, 16 * f + 4 * s + 4))
                    pe.wait_ge(low_done[s], use(blk, s, lay, ffn_use(blk, f, s) + 1) + i)
                    for k in range(4):
                        mm = product(pe, [[acc[0][tt]] for tt in range(TT)], xh[:, 4 * s + k, :], xl[:, 4 * s + k, :],
                                     s, k * 512, 512, s == 0 and k == 0, s == 1 and k == 3)
                    mm.then_inc(slot_used[s], 1)

            def down(i, start, stop):
                pe.wait_ge(hTl_done, at(lay, 22, FSTEPS * f + 1) + i)
                pe.wait_ge(low_done[2], use(blk, 2, lay, ffn_use(blk, f, 2) + 1) + i)
                for k in range(2):
                    mm = product(pe, DOWN, hTh[:, k, :], hTl[:, k, :], 2, k * D, 512, start and k == 0, stop and k == 1)
                mm.then_inc(slot_used[2], 1)

            def turn(i):
                pe.wait_ge(hid_done, at(lay, 22, FSTEPS * f + 1) + i)
                for k in range(2):
                    for tt in range(TT):
                        tr = pe.transpose(ps[2][:, k * SEQ + tt * P:k * SEQ + (tt + 1) * P],
                                          hid[:, tt, k * P:(k + 1) * P], ident)
                tr.then_inc(hT_done, 1)

            norm_pe(pe, lay, 2 * f)
            up(0)
            turn(0)
            up(1)
            down(0, True, False)
            turn(1)
            with pe.Fori(2, FSTEPS) as i:
                up(i)
                down(i - 1, False, False)
                turn(i)
            down(FSTEPS - 1, False, True)

        def ffn_act(act, blk, lay, f):
            b = [ffn_use(blk, f, s) for s in range(SLOTS)]

            def silu(i):
                act.wait_ge(slot_used[1], use(blk, 1, lay, b[1] + 1) + i)
                for tt in range(TT):
                    a = nc.scalar.activation(sil[:, tt, :], acc[0][tt][:, 0:FC], ACT.Silu, scale=rstd[:, tt:tt + 1])
                a.then_inc(silu_done, 1)

            def turn_high(i):
                act.wait_ge(hT_done, at(lay, 22, FSTEPS * f + 1) + i)
                nc.scalar.activation(hTh[:], ps[2][:].rearrange("p (k n) -> p k n", k=2), ACT.Copy).then_inc(hTh_done, 1)

            for s in range(2):
                split_high(act, blk, s, lay, b[s])
            norm_act(act, lay, 2 * f)
            act.preload_act_table(ACT.Silu)
            act.wait_ge(rstd_done, at(lay, 3, 2 * f + 1))
            with act.Fori(0, FSTEPS - 1) as i:
                silu(i)
                for s in range(2):
                    split_high(act, blk, s, lay, b[s] + 1 + i)
                turn_high(i)
                split_high(act, blk, 2, lay, b[2] + i)
            silu(FSTEPS - 1)
            turn_high(FSTEPS - 1)
            split_high(act, blk, 2, lay, b[2] + FSTEPS - 1)

        def ffn_dve(dve, blk, lay, f):
            b = [ffn_use(blk, f, s) for s in range(SLOTS)]

            def hidden(i):
                dve.wait_ge(silu_done, at(lay, 22, FSTEPS * f + 1) + i)
                for tt in range(TT):
                    h = nc.vector.scalar_tensor_tensor(hid[:, tt, :], acc[0][tt][:, FC:2 * FC], rstd[:, tt:tt + 1],
                                                       sil[:, tt, :], ALU.mult, ALU.mult)
                h.then_inc(hid_done, 1)

            def turn_low(i):
                dve.wait_ge(hTh_done, at(lay, 22, FSTEPS * f + 1) + i)
                nc.vector.tensor_tensor(hTl[:], ps[2][:].rearrange("p (k n) -> p k n", k=2), hTh[:].bitcast(F32),
                                        ALU.subtract).then_inc(hTl_done, 1)

            for s in range(2):
                split_low(dve, nc.vector, blk, s, lay, b[s])
            norm_dve(dve, lay, 2 * f)
            with dve.Fori(0, FSTEPS - 1) as i:
                hidden(i)
                for s in range(2):
                    split_low(dve, nc.vector, blk, s, lay, b[s] + 1 + i)
                turn_low(i)
            hidden(FSTEPS - 1)
            turn_low(FSTEPS - 1)

        def ffn_pool(pool, blk, lay, f):
            norm_pool(pool, lay, 2 * f)
            with pool.Fori(0, FSTEPS) as i:
                split_low(pool, nc.gpsimd, blk, 2, lay, ffn_use(blk, f, 2) + i)

        def ffn_sp(sp, blk, lay, f):
            gate_w, up_w, down_w, up_col = t["ffn"][blk][f]
            row = lay * D if blk == 1 else lay * D - LAYERS * D
            drow = lay * FFN if blk == 1 else lay * FFN - LAYERS * FFN
            with sp.Fori(0, FSTEPS) as i:
                for s in range(2):
                    sp.wait_ge(low_done[s], use(blk, s, lay, ffn_use(blk, f, s)) + i)
                    dst = raw[s][:].rearrange("p (k g n) -> p k g n", k=4, g=2)
                    for g, (w, c0) in enumerate(((gate_w, 0), (up_w, up_col))):
                        sp.dma_start(dst[:, :, g, :], w[bass.ds(row + 4 * s * P, 4 * P), bass.ds(i * FC + c0, FC)]
                                     .rearrange("(k p) n -> p k n", p=P)).then_inc(raw_in[s], 16)
                sp.wait_ge(low_done[2], use(blk, 2, lay, ffn_use(blk, f, 2)) + i)
                for k in range(2):
                    sp.dma_start(raw[2][:, k * D:(k + 1) * D], down_w[bass.ds(drow + i * FC + k * P, P), :]).then_inc(raw_in[2], 16)

        def y_wait(eng, blk, lay, f):
            if f == 1:
                u = (MIX1 if blk == 1 else MIX2) - 1
                eng.wait_ge(slot_used[u % SLOTS], use(blk, u % SLOTS, lay, mix_use(u) + 1))
            else:
                eng.wait_ge(slot_used[2], use(blk, 2, lay, ffn_use(blk, f // 2, 2) + FSTEPS))

        def post_act(act, blk, lay, f):
            if blk == 2:
                return
            Y = YMIX if f == 1 else DOWN
            y_wait(act, blk, lay, f)
            for tt in range(TT):
                for j in range(2):
                    nc.scalar.activation(junk[:, tt, j * 512:(j + 1) * 512], Y[tt][j][:], ACT.Square,
                                         accum_out=ssy[:, tt, j:j + 1]).then_inc(ssy_done, 1)

        def post_dve(dve, blk, lay, f):
            Y = YMIX if f == 1 else DOWN
            weight = 1.0 if f == 1 else 0.5
            if blk == 2:
                y_wait(dve, blk, lay, f)
                for tt in range(TT):
                    for j in range(2):
                        xs = X[:, tt, j * 512:(j + 1) * 512]
                        r = nc.vector.scalar_tensor_tensor(xs, Y[tt][j][:], weight, xs, ALU.mult, ALU.add)
                    r.then_inc(x_ready, 1)
                return
            dve.wait_ge(ssy_done, at(lay, 12, 4 * f + 4))
            link(dve, nc.vector.tensor_tensor(msy[:], ssy[:, :, 0], ssy[:, :, 1], ALU.add))
            nc.vector.tensor_scalar(msy[:], msy[:], 1.0 / D, EPS, ALU.mult, ALU.add).then_inc(msy_done, 1)
            dve.wait_ge(rsy_done, at(lay, 3, f + 1))
            dve.wait_ge(grow_in, 16 * at(lay, 3, f + 1))
            for tt in range(TT):
                for j in range(2):
                    c = slice(j * 512, (j + 1) * 512)
                    a = nc.vector.scalar_tensor_tensor(tpost[:, tt, c], Y[tt][j][:], rsy[:, tt:tt + 1], grow[:, c], ALU.mult, ALU.mult)
            link(dve, a)
            for tt in range(TT):
                nc.vector.scalar_tensor_tensor(X[:, tt, :], tpost[:, tt, :], weight, X[:, tt, :], ALU.mult, ALU.add).then_inc(x_ready, 1)

        def post_pool(pool, blk, lay, f):
            if blk == 2:
                return
            pool.wait_ge(msy_done, at(lay, 3, f + 1))
            nc.gpsimd.tensor_tensor(rsy[:], msy[:], neghalf[:, 0:TT], ALU.pow).then_inc(rsy_done, 1)

        def post_sp(sp, blk, lay, f):
            if blk == 2:
                return
            sp.wait_ge(x_ready, at(lay, 6, X_IN + 2 * f))
            sp.dma_start(grow, t["post"][f][bass.ds(lay, 1), :].broadcast_to((P, D))).then_inc(grow_in, 16)

        chain = {"n": 0, "lay": 0, "per": 0, "off": 0}

        def link(dve, ins):
            chain["n"] += 1
            ins.then_inc(dve_link, 1)
            dve.wait_ge(dve_link, chain["lay"] * chain["per"] + (chain["off"] + chain["n"]))

        SECTIONS = (Q_DIFF, K_DIFF, Q_SB, K_SB, Q_MOBA, K_MOBA)
        DIFF0, SB0, MOBA0 = 6, 12, 20
        V_CHUNKS = {V_DIFF: 0, V_SB: 1, V_MOBA: 2}
        BRANCH = [(u, (u - PROJ1) % 3, (u - PROJ1) // 3) for u in range(PROJ1, PROJ1 + 6)]
        NDI, NSB, NMO = DIFF_HEADS, SB_HEADS, MOBA_HEADS
        NPV = NDI + NSB + NMO

        def halves(k):
            return slice(k * 512, (k + 1) * 512)

        def unit1_done(eng, lay, u):
            eng.wait_ge(slot_used[u % SLOTS], use(1, u % SLOTS, lay, mix_use(u) + 1))

        def load_unit(sp, s, weights, row, col):
            for k in range(2):
                sp.dma_start(raw[s][:, k * D:(k + 1) * D].rearrange("p (k n) -> p k n", k=2),
                             weights[bass.ds(row + k * SEQ, SEQ), col].rearrange("(k p) n -> p k n", p=P)).then_inc(raw_in[s], 16)

        def mix1_sp(sp, lay):
            for u in range(MIX1):
                s = u % SLOTS
                if u < PROJ1:
                    weights, row, col = t["w_in"], lay * D + (u % 2) * 512, halves(u // 2)
                elif u < PROJ1 + 6:
                    _, b, half = BRANCH[u - PROJ1]
                    weights, row, col = t["w_o"][b], lay * 512, halves(half)
                else:
                    kh, half = divmod(u - PROJ1 - 6, 2)
                    weights, row, col = t["w_out"], lay * D + kh * 512, halves(half)
                sp.wait_ge(low_done[s], use(1, s, lay, mix_use(u)))
                load_unit(sp, s, weights, row, col)

        def scores1(pe, bank, q, k, lo, blk):
            rows = slice(lo, lo + HD)
            pe.matmul(bank[:, 0:P], q[rows, blk, 0:P], k[rows, blk, 0:P], start=True, stop=True)
            return pe.matmul(bank[:, P:384], q[rows, blk, P:SEQ], k[rows, blk, 0:SEQ], start=True, stop=True)

        def values(pe, out0, out1, w, v0, v1):
            pe.matmul(out0, w[:, 0:P], v0, start=True, stop=True)
            pe.matmul(out1, w[:, P:2 * P], v0, start=True, stop=False)
            return pe.matmul(out1, w[:, 2 * P:384], v1, start=False, stop=True)

        def turn_tokens(pe, bank, src, kt):
            for k in range(2):
                for tt in range(TT):
                    tr = pe.transpose(bank[:, k * SEQ + tt * P:k * SEQ + (tt + 1) * P], src[:, tt, (kt + k) * P:(kt + k + 1) * P], ident)
            return tr

        def mix1_pe(pe, lay):
            norm_pe(pe, lay, 1)
            for u in range(MIX1):
                s = u % SLOTS
                if u < PROJ1:
                    c, half = divmod(u, 2)
                    if c == 0:
                        pe.wait_ge(xl_done, at(lay, 24, 8 + 4 * half + 4))
                    if half == 0 and c >= 2:
                        pe.wait_ge(chunk_out, at(lay, CH1, c - 1))
                    lhs = [(xh[:, 4 * half + k, :], xl[:, 4 * half + k, :]) for k in range(4)]
                    out, first, last = acc[c % 2], half == 0, half == 1
                elif u < PROJ1 + 6:
                    _, b, half = BRANCH[u - PROJ1]
                    c = CH1 + u - PROJ1
                    if u < PROJ1 + 2:
                        pe.wait_ge(chunk_out, at(lay, CH1, c - 1))
                    else:
                        pe.wait_ge(proj_out, at(lay, 6, u - PROJ1 - 1))
                    pe.wait_ge(oTl_done, at(lay, 6, 2 * b + 2))
                    lhs = [(oTh[b][:, k, :], oTl[b][:, k, :]) for k in range(4)]
                    out, first, last = acc[c % 2], True, True
                else:
                    kh, half = divmod(u - PROJ1 - 6, 2)
                    if kh == 0:
                        pe.wait_ge(proj_out, at(lay, 6, 5 + half))
                    pe.wait_ge(mTl_done, at(lay, 4, 2 * kh + 2))
                    lhs = [(xh[:, 4 * kh + k, :], xl[:, 4 * kh + k, :]) for k in range(4)]
                    out, first, last = [YMIX[tt][half] for tt in range(TT)], kh == 0, kh == 1
                pe.wait_ge(low_done[s], use(1, s, lay, mix_use(u) + 1))
                for k in range(4):
                    mm = product(pe, [[o] for o in out], lhs[k][0], lhs[k][1], s, k * 512, 512, first and k == 0, last and k == 3)
                mm.then_inc(slot_used[s], 1)
                mix1_tail(pe, lay, u)

        def mix1_tail(pe, lay, u):
            h = u - DIFF0 - 2
            if 0 <= h < NDI:
                pe.wait_ge(wT_out, at(lay, NDI + NMO, h + 1))
                if h == 0:
                    pe.wait_ge(chunk_out, at(lay, CH1, V_DIFF + 1))
                if h == 2:
                    pe.wait_ge(o_out, at(lay, 6, 1))
                o = wk[3][:, (h % 2) * 256:(h % 2 + 1) * 256]
                v = vnat[0][:, :, h * P:(h + 1) * P]
                values(pe, o[:, 0:P], o[:, P:256], wT[h % 2], v[:, 0, :], v[:, 1, :]).then_inc(pv_done, 1)
            j = u - SB0 - 2
            if 0 <= j < NSB:
                pe.wait_ge(sbw_done, at(lay, NSB, j + 1))
                if j % 4 == 0:
                    pe.wait_ge(o_out, at(lay, 6, 2 + j // 4))
                if j == 0:
                    pe.wait_ge(chunk_out, at(lay, CH1, V_SB + 1))
                o = wk[3][:, (j % 4) * P:(j % 4 + 1) * P]
                v = vnat[1][:, :, j * HD:(j + 1) * HD]
                values(pe, o[:, 0:HD], o[:, HD:P], wT[j % 2], v[:, 0, :], v[:, 1, :]).then_inc(pv_done, 1)
            j = u - MOBA0 - 2
            if 0 <= j < NMO:
                pe.wait_ge(wT_out, at(lay, NDI + NMO, NDI + j + 1))
                if j % 4 == 0:
                    pe.wait_ge(o_out, at(lay, 6, 4 + j // 4))
                if j == 0:
                    pe.wait_ge(chunk_out, at(lay, CH1, V_MOBA + 1))
                o = wk[3][:, (j % 4) * P:(j % 4 + 1) * P]
                v = vnat[2][:, :, j * HD:(j + 1) * HD]
                values(pe, o[:, 0:HD], o[:, HD:P], wT[j % 2], v[:, 0, :], v[:, 1, :]).then_inc(pv_done, 1)
            h = u - DIFF0 - 1
            if 0 <= h < NDI:
                pe.wait_ge(wdf_done, at(lay, NDI, h + 1))
                if h > 0:
                    pe.wait_ge(wT_out, at(lay, NDI + NMO, h))
                for b in range(3):
                    tr = pe.transpose(wk[2][:, b * P:(b + 1) * P], wdf[:, b * P:(b + 1) * P], ident)
                tr.then_inc(wT_done, 1)
            j = u - MOBA0 - 1
            if 0 <= j < NMO:
                pe.wait_ge(exp_done, at(lay, NDI + NMO, NDI + j + 1))
                if j == 0:
                    pe.wait_ge(sec_out, at(lay, 12, 12))
                else:
                    pe.wait_ge(wT_out, at(lay, NDI + NMO, NDI + j))
                for b in range(3):
                    tr = pe.transpose(wk[2][:, b * P:(b + 1) * P], ex[j % 2][:, b * P:(b + 1) * P], ident)
                tr.then_inc(wT_done, 1)
            j = u - SB0 - 1
            if 0 <= j < NSB:
                pe.wait_ge(keep_done, at(lay, NSB, j + 1))
                bank = wk[j % 2]
                pe.matmul(bank[:, 0:384], tri, slk[:], start=False, stop=False, skip_group_check=True)
                pe.matmul(bank[:, P:2 * P], ones, slk[:, 2 * P:384], start=False, stop=True, skip_group_check=True).then_inc(cum_done, 1)
            if u in (13, 14):
                pe.wait_ge(od_done, at(lay, 1, 1))
                if u == 13:
                    pe.wait_ge(wT_out, at(lay, NDI + NMO, NDI))
                else:
                    pe.wait_ge(oTl_done, at(lay, 6, 1))
                turn_tokens(pe, wk[2], onat[0], 2 * (u - 13)).then_inc(oT_done, 1)
            if u == 28:
                pe.wait_ge(mask_done, at(lay, 2 * NDI + NMO, 2 * NDI + NMO))
                pe.wait_ge(o_out, at(lay, 6, 4))
                for i in range(2):
                    turn_tokens(pe, wk[i], onat[1], 2 * i).then_inc(oT_done, 1)
            if u == 30:
                pe.wait_ge(oTl_done, at(lay, 6, 4))
                pe.wait_ge(o_out, at(lay, 6, 6))
                for i in range(2):
                    turn_tokens(pe, wk[i], onat[2], 2 * i).then_inc(oT_done, 1)
            if u in (34, 36):
                half = (u - 34) // 2
                pe.wait_ge(merged, at(lay, 2, half + 1))
                if half == 0:
                    pe.wait_ge(oTl_done, at(lay, 6, 6))
                else:
                    pe.wait_ge(wT_out, at(lay, NDI + NMO, NDI + NMO))
                    pe.wait_ge(o_out, at(lay, 6, 6))
                for i in range(2):
                    turn_tokens(pe, wk[2 * half + i], mrg, 4 * half + 2 * i).then_inc(mT_done, 1)
            for si, (first, second, b0, b1) in enumerate(((3, 3, 0, 1), (5, 5, 0, 1), (10, 10, 0, 1), (11, 11, 0, 1), (15, 16, 2, 2), (17, 18, 2, 2))):
                for half, (step, b) in enumerate(((first, b0), (second, b1))):
                    if u != step:
                        continue
                    src = stage[si % 2]
                    if half == 0:
                        if si in (2, 3):
                            pe.wait_ge(chunk_out, at(lay, CH1, SECTIONS[si] + 1))
                        else:
                            pe.wait_ge(rope_done, at(lay, 4, si + 1 if si < 2 else si - 1))
                        if si == 2:
                            pe.wait_ge(mask_done, at(lay, 2 * NDI + NMO, 2 * NDI))
                        elif si == 4:
                            pe.wait_ge(oTl_done, at(lay, 6, 2))
                        elif si > 0:
                            pe.wait_ge(sec_out, at(lay, 12, 2 * si))
                    elif si >= 4:
                        pe.wait_ge(sec_out, at(lay, 12, 2 * si + 1))
                    turn_tokens(pe, wk[b], src, 2 * half).then_inc(sec_T, 1)
            h = u - DIFF0
            if 0 <= h < NDI:
                if h == 0:
                    pe.wait_ge(sec_out, at(lay, 12, 4))
                else:
                    pe.wait_ge(mask_done, at(lay, 2 * NDI + NMO, 2 * h))
                for m in range(2):
                    scores1(pe, wk[m], secT[Q_DIFF], secT[K_DIFF], HD * m, h).then_inc(score_done, 1)
            j = u - SB0
            if 0 <= j < NSB:
                if j == 0:
                    pe.wait_ge(sec_out, at(lay, 12, 8))
                if j >= 2:
                    pe.wait_ge(arg_done, at(lay, NSB, j - 1))
                q, k, rows, blk, bank = secT[Q_SB], secT[K_SB], slice(HD * (j % 2), HD * (j % 2) + HD), j // 2, wk[j % 2]
                pe.matmul(bank[:, 0:SEQ], k[rows, blk, 0:P], q[rows, blk, :], start=True, stop=False, skip_group_check=True)
                pe.matmul(bank[:, SEQ:384], k[rows, blk, P:SEQ], q[rows, blk, P:SEQ], start=False, stop=True, skip_group_check=True).then_inc(z_done, 1)
            j = u - MOBA0
            if 0 <= j < NMO:
                if j < 2:
                    pe.wait_ge(sec_out, at(lay, 12, 12))
                    pe.wait_ge(arg_done, at(lay, NSB, NSB - 1 + j))
                else:
                    pe.wait_ge(mask_done, at(lay, 2 * NDI + NMO, 2 * NDI + j - 1))
                scores1(pe, wk[j % 2], secT[Q_MOBA], secT[K_MOBA], HD * (j % 2), j // 2).then_inc(score_done, 1)

        def mix1_act(act, lay):
            for u in range(2):
                split_high(act, 1, u % SLOTS, lay, mix_use(u))
            norm_act(act, lay, 1)
            act.preload_act_table_set(EXP_LN)
            act.wait_ge(rstd_done, at(lay, 3, 2))
            for u in range(MIX1 + 1):
                if u + 2 < MIX1:
                    split_high(act, 1, (u + 2) % SLOTS, lay, mix_use(u + 2))
                c = u // 2 - 1
                if u % 2 == 0 and 0 <= c < CH1:
                    unit1_done(act, lay, u - 1)
                    if c in SECTIONS:
                        si = SECTIONS.index(c)
                        if si >= 2:
                            act.wait_ge(sec_T, at(lay, 12, 2 * si - 2))
                        dst = stage[si % 2]
                    elif c in V_CHUNKS:
                        dst = vnat[V_CHUNKS[c]]
                    else:
                        dst = gate1[(c - 9) // 2][:, :, halves((c - 9) % 2)]
                    for tt in range(TT):
                        a = nc.scalar.activation(dst[:, tt, :], acc[c % 2][tt][:], ACT.Copy, scale=rstd[:, tt:tt + 1])
                    a.then_inc(chunk_out, 1)
                if u == 4:
                    act.wait_ge(lam_sum, at(lay, 1, 1))
                    nc.scalar.activation(lame[:], lams[:], ACT.Exp).then_inc(lam_exp, 1)
                for si, steps in enumerate(((4, 4), (6, 6), (11, 11), (12, 12), (16, 17), (18, 19))):
                    for half, step in enumerate(steps):
                        if u == step:
                            act.wait_ge(sec_T, at(lay, 12, 2 * si + half + 1))
                            nc.scalar.activation(secT[SECTIONS[si]][:, 2 * half:2 * half + 2, :],
                                                 wk[half if si < 4 else 2][:].rearrange("p (k n) -> p k n", k=2), ACT.Copy,
                                                 scale=HD ** -0.5 if si % 2 == 0 else 1.0).then_inc(sec_out, 1)
                for first, n, i0, pv0 in ((DIFF0 + 2, NDI, 0, 0), (MOBA0 + 2, NMO, NDI, NDI + NSB)):
                    j = u - first
                    if 0 <= j < n:
                        act.wait_ge(wT_done, at(lay, NDI + NMO, i0 + j + 1))
                        if pv0 + j >= 2:
                            act.wait_ge(pv_done, at(lay, NPV, pv0 + j - 1))
                        nc.scalar.activation(wT[j % 2][:], wk[2][:, 0:384], ACT.Copy).then_inc(wT_out, 1)
                for step, n, g in ((DIFF0 + 4, 2, 0), (DIFF0 + 6, 4, 1)):
                    if u == step:
                        act.wait_ge(pv_done, at(lay, NPV, n))
                        nc.scalar.activation(onat[0][:].rearrange("p t (h d) -> p h t d", d=P)[:, 2 * g:2 * g + 2],
                                             wk[3][:].rearrange("p (h t d) -> p h t d", h=2, t=TT), ACT.Copy).then_inc(o_out, 1)
                for step, n, g in ((SB0 + 6, 4, 0), (SB0 + 10, 8, 1)):
                    if u == step:
                        act.wait_ge(pv_done, at(lay, NPV, NDI + n))
                        nc.scalar.activation(onat[1][:].rearrange("p t (h d) -> p h t d", d=HD)[:, 4 * g:4 * g + 4],
                                             wk[3][:].rearrange("p (h t d) -> p h t d", h=4, t=TT), ACT.Copy).then_inc(o_out, 1)
                j = u - SB0 - 2
                if 0 <= j < NSB:
                    act.wait_ge(arg_done, at(lay, NSB, j + 1))
                    act.wait_ge(pv_done, at(lay, NPV, NDI + j - 1))
                    nc.scalar.activation(wT[j % 2][:], sag[:], ACT.Exp).then_inc(sbw_done, 1)
                j = u - SB0 - 1
                if 0 <= j < NSB:
                    act.wait_ge(abs_done, at(lay, NSB, j + 1))
                    if j > 0:
                        act.wait_ge(keep_done, at(lay, NSB, j))
                    nc.scalar.activation(sex[:], saz[:], ACT.Exp).then_inc(sbe_done, 1)
                    act.wait_ge(sbe_done, at(lay, NSB, j + 1))
                    nc.scalar.activation(sex[:], sex[:], ACT.Ln, bias=1.0).then_inc(ln_done, 1)
                h = u - DIFF0 - 1
                if 0 <= h < NDI:
                    act.wait_ge(max_done, at(lay, NDI + NMO, h + 1))
                    if h > 0:
                        act.wait_ge(wdf_done, at(lay, NDI, h))
                    for m in range(2):
                        for tt, seg in enumerate((slice(0, P), slice(P, 384))):
                            a = nc.scalar.activation(ex[m][:, seg], smk[m][:, seg], ACT.Exp, bias=nmx[:, 2 * m + tt:2 * m + tt + 1],
                                                     accum_out=lsum[:, 2 * m + tt:2 * m + tt + 1])
                    a.then_inc(exp_done, 1)
                j = u - MOBA0 - 1
                if 0 <= j < NMO:
                    act.wait_ge(max_done, at(lay, NDI + NMO, NDI + j + 1))
                    if j < 2:
                        act.wait_ge(wdf_done, at(lay, NDI, NDI))
                    else:
                        act.wait_ge(wT_done, at(lay, NDI + NMO, NDI + j - 1))
                    for tt, seg in enumerate((slice(0, P), slice(P, 384))):
                        a = nc.scalar.activation(ex[j % 2][:, seg], smk[j % 2][:, seg], ACT.Exp, bias=nmx[:, 2 * (j % 2) + tt:2 * (j % 2) + tt + 1],
                                                 accum_out=lmo[:, tt, j:j + 1])
                    a.then_inc(exp_done, 1)
                for step, b, i, bank in ((14, 0, 0, 2), (15, 0, 1, 2), (29, 1, 0, 0), (29, 1, 1, 1), (31, 2, 0, 0), (31, 2, 1, 1)):
                    if u == step:
                        act.wait_ge(oT_done, at(lay, 6, 2 * b + i + 1))
                        nc.scalar.activation(oTh[b][:, 2 * i:2 * i + 2, :], wk[bank][:].rearrange("p (k n) -> p k n", k=2), ACT.Copy,
                                             scale=gdiff[:] if b == 0 else 1.0).then_inc(oTh_done, 1)
                k = u - PROJ1
                if 0 <= k < 6:
                    _, b, half = BRANCH[k]
                    if k == 0:
                        act.wait_ge(chunk_out, at(lay, CH1, CH1))
                    g = gate1[b][:, :, halves(half)]
                    nc.scalar.activation(g, g, ACT.Sigmoid).then_inc(sig_done, 1)
                if u in (35, 37):
                    half = (u - 35) // 2
                    for i in range(2):
                        act.wait_ge(mT_done, at(lay, 4, 2 * half + i + 1))
                        nc.scalar.activation(xh[:, 4 * half + 2 * i:4 * half + 2 * i + 2, :],
                                             wk[2 * half + i][:].rearrange("p (k n) -> p k n", k=2), ACT.Copy).then_inc(mTh_done, 1)

        def mix1_dve(dve, lay):
            causal = kblk[:, K1_CAUSAL:K1_CAUSAL + 384]
            keep = kblk[:, K1_KEEP:K1_KEEP + 384]
            drop = kblk[:, K1_DROP:K1_DROP + 384]

            def table(col):
                return kblk[:, col:col + TT * 8].rearrange("p (t e) -> p t e", t=TT).unsqueeze(2).broadcast_to((P, TT, 8, 8))

            for u in range(2):
                split_low(dve, nc.vector, 1, u % SLOTS, lay, mix_use(u))
            norm_dve(dve, lay, 1)
            dve.wait_ge(kblk_in, 16)
            for u in range(MIX1 + 1):
                if u + 2 < MIX1 and (u + 2) % SLOTS != 2:
                    split_low(dve, nc.vector, 1, (u + 2) % SLOTS, lay, mix_use(u + 2))
                if u == 0:
                    qk = cols[:, C1_LQK:C1_LQK + 4 * HD].rearrange("p (a b d) -> p a b d", a=2, b=2)
                    link(dve, nc.vector.tensor_tensor(lamp[:], qk[:, :, 0, :], qk[:, :, 1, :], ALU.mult))
                    nc.vector.tensor_reduce(lams[:], lamp[:], AX.X, ALU.add).then_inc(lam_sum, 1)
                if u == 4:
                    dve.wait_ge(lam_exp, at(lay, 1, 1))
                    link(dve, nc.vector.tensor_tensor(lam[:], lame[:, 0:1], lame[:, 1:2], ALU.subtract))
                    nc.vector.tensor_tensor(lam[:], lam[:], cols[:, C1_LAM0:C1_LAM0 + 1], ALU.add)
                    link(dve, nc.vector.tensor_tensor(gdiff[:], cols[:, C1_DIFF:C1_DIFF + 1], cols[:, C1_LAM1:C1_LAM1 + 1], ALU.mult))
                for n, (si, step) in enumerate(((0, 2), (1, 4), (4, 14), (5, 16))):
                    if u == step:
                        dve.wait_ge(chunk_out, at(lay, CH1, SECTIONS[si] + 1))
                        v = stage[si % 2][:].rearrange("p t (h d) -> p t h d", d=HD)
                        x1, x2 = v[:, :, :, 0:8], v[:, :, :, 8:16]
                        for i, (x, col) in enumerate(((x1, K1_COS), (x2, K1_SIN), (x2, K1_COS), (x1, K1_SIN))):
                            a = nc.vector.tensor_tensor(rt[i][:], x, table(col), ALU.mult)
                        link(dve, a)
                        nc.vector.tensor_tensor(x1, rt[0][:], rt[1][:], ALU.subtract)
                        nc.vector.tensor_tensor(x2, rt[2][:], rt[3][:], ALU.add).then_inc(rope_done, 1)
                j = u - SB0 - 2
                if 0 <= j < NSB:
                    dve.wait_ge(cum_done, at(lay, NSB, j + 1))
                    if j > 0:
                        dve.wait_ge(sbw_done, at(lay, NSB, j))
                    nc.vector.tensor_tensor(sag[:], wk[j % 2][:, 0:384], drop, ALU.add).then_inc(arg_done, 1)
                j = u - SB0 - 1
                if 0 <= j < NSB:
                    bank = wk[j % 2]
                    dve.wait_ge(z_done, at(lay, NSB, j + 1))
                    link(dve, nc.vector.tensor_scalar(smx[:], bank[:, 0:384], 0.0, None, ALU.max))
                    nc.vector.scalar_tensor_tensor(saz[:], smx[:], -2.0, bank[:, 0:384], ALU.mult, ALU.add).then_inc(abs_done, 1)
                    dve.wait_ge(ln_done, at(lay, NSB, j + 1))
                    link(dve, nc.vector.tensor_tensor(saz[:], smx[:], sex[:], ALU.add))
                    if j > 0:
                        dve.wait_ge(cum_done, at(lay, NSB, j))
                    nc.vector.scalar_tensor_tensor(slk[:], saz[:], -1.0, keep, ALU.mult, ALU.mult).then_inc(keep_done, 1)
                h = u - DIFF0 - 1
                if 0 <= h < NDI:
                    if h > 0:
                        dve.wait_ge(exp_done, at(lay, NDI + NMO, h))
                    for m in range(2):
                        dve.wait_ge(score_done, at(lay, 2 * NDI + NMO, 2 * h + m + 1))
                        nc.vector.tensor_tensor(smk[m][:], wk[m][:, 0:384], causal, ALU.add).then_inc(mask_done, 1)
                    dve.wait_ge(mask_done, at(lay, 2 * NDI + NMO, 2 * h + 2))
                    for m in range(2):
                        nc.vector.tensor_reduce(nmx[:, 2 * m:2 * m + 1], smk[m][:, 0:P], AX.X, ALU.max, negate=True)
                        a = nc.vector.tensor_reduce(nmx[:, 2 * m + 1:2 * m + 2], smk[m][:, P:384], AX.X, ALU.max, negate=True)
                    a.then_inc(max_done, 1)
                    dve.wait_ge(exp_done, at(lay, NDI + NMO, h + 1))
                    link(dve, nc.vector.reciprocal(rsum[:], lsum[:]))
                    link(dve, nc.vector.tensor_scalar(rsl[:], rsum[:, 2:4], lam[:], None, ALU.mult))
                    if h > 0:
                        dve.wait_ge(wT_done, at(lay, NDI + NMO, h))
                    for tt, seg in enumerate((slice(0, P), slice(P, 384))):
                        a = nc.vector.tensor_scalar(wdf[:, seg], ex[1][:, seg], rsl[:, tt:tt + 1], None, ALU.mult)
                    link(dve, a)
                    for tt, seg in enumerate((slice(0, P), slice(P, 384))):
                        a = nc.vector.scalar_tensor_tensor(wdf[:, seg], ex[0][:, seg], rsum[:, tt:tt + 1], wdf[:, seg], ALU.mult, ALU.subtract)
                    a.then_inc(wdf_done, 1)
                j = u - MOBA0 - 1
                if 0 <= j < NMO:
                    m = j % 2
                    dve.wait_ge(score_done, at(lay, 2 * NDI + NMO, 2 * NDI + j + 1))
                    if j >= 2:
                        dve.wait_ge(exp_done, at(lay, NDI + NMO, NDI + j - 1))
                    nc.vector.tensor_tensor(smk[m][:], wk[m][:, 0:384], causal, ALU.add).then_inc(mask_done, 1)
                    dve.wait_ge(mask_done, at(lay, 2 * NDI + NMO, 2 * NDI + j + 1))
                    nc.vector.tensor_reduce(nmx[:, 2 * m:2 * m + 1], smk[m][:, 0:P], AX.X, ALU.max, negate=True)
                    nc.vector.tensor_reduce(nmx[:, 2 * m + 1:2 * m + 2], smk[m][:, P:384], AX.X, ALU.max, negate=True).then_inc(max_done, 1)
                for step, g in ((MOBA0 + 6, 0), (MOBA0 + 10, 1)):
                    if u == step:
                        hs = slice(4 * g, 4 * g + 4)
                        dve.wait_ge(pv_done, at(lay, NPV, NDI + NSB + 4 * g + 4))
                        link(dve, nc.vector.reciprocal(rmo[:, :, hs], lmo[:, :, hs]))
                        for tt in range(TT):
                            a = nc.vector.tensor_tensor(onat[2][:, tt, :].rearrange("p (h d) -> p h d", d=HD)[:, hs],
                                                        wk[3][:].rearrange("p (h t d) -> p h t d", h=4, t=TT)[:, :, tt, :],
                                                        rmo[:, tt, hs].unsqueeze(2).broadcast_to((P, 4, HD)), ALU.mult)
                        a.then_inc(o_out, 1)
                if u == 12:
                    dve.wait_ge(osq_done, at(lay, 1, 1))
                    link(dve, nc.vector.tensor_reduce(ssd[:], osq[:].rearrange("p t (h d) -> p (t h) d", d=P), AX.X, ALU.add))
                    nc.vector.tensor_scalar(msd[:], ssd[:], 1.0 / P, EPS, ALU.mult, ALU.add).then_inc(od_ms, 1)
                if u == 13:
                    dve.wait_ge(od_pow, at(lay, 1, 1))
                    o = onat[0][:].rearrange("p t (h d) -> p (t h) d", d=P)
                    nc.vector.tensor_tensor(o, o, rsd[:].unsqueeze(2).broadcast_to((P, 8, P)), ALU.mult).then_inc(od_done, 1)
                for step, b, i, bank in ((14, 0, 0, 2), (15, 0, 1, 2), (29, 1, 0, 0), (29, 1, 1, 1), (31, 2, 0, 0), (31, 2, 1, 1)):
                    if u == step:
                        dve.wait_ge(oTh_done, at(lay, 6, 2 * b + i + 1))
                        nc.vector.scalar_tensor_tensor(oTl[b][:, 2 * i:2 * i + 2, :], wk[bank][:].rearrange("p (k n) -> p k n", k=2),
                                                       gdiff[:] if b == 0 else 1.0, oTh[b][:, 2 * i:2 * i + 2, :].bitcast(F32),
                                                       ALU.mult, ALU.subtract).then_inc(oTl_done, 1)
                k = u - PROJ1 - 1
                if 0 <= k < 6:
                    _, b, half = BRANCH[k]
                    c = CH1 + k
                    unit1_done(dve, lay, PROJ1 + k)
                    dve.wait_ge(sig_done, at(lay, 6, k + 1))
                    dst = mrg[:, :, halves(half)] if b == 0 else mtm[:]
                    if k == 4:
                        dve.wait_ge(merged, at(lay, 2, 1))
                    for tt in range(TT):
                        a = nc.vector.tensor_tensor(dst[:, tt, :], acc[c % 2][tt][:], gate1[b][:, tt, halves(half)], ALU.mult)
                    a.then_inc(proj_out, 1)
                    if b > 0:
                        dve.wait_ge(proj_out, at(lay, 6, k + 1))
                        a = nc.vector.tensor_tensor(mrg[:, :, halves(half)], mrg[:, :, halves(half)], mtm[:], ALU.add)
                        if b == 2:
                            a.then_inc(merged, 1)
                        else:
                            link(dve, a)
                if u in (35, 37):
                    half = (u - 35) // 2
                    for i in range(2):
                        kt = 4 * half + 2 * i
                        dve.wait_ge(mTh_done, at(lay, 4, 2 * half + i + 1))
                        nc.vector.tensor_tensor(xl[:, kt:kt + 2, :], wk[2 * half + i][:].rearrange("p (k n) -> p k n", k=2),
                                                xh[:, kt:kt + 2, :].bitcast(F32), ALU.subtract).then_inc(mTl_done, 1)

        def mix1_pool(pool, lay):
            norm_pool(pool, lay, 1)
            for u in range(MIX1):
                if u % SLOTS == 2:
                    split_low(pool, nc.gpsimd, 1, 2, lay, mix_use(u))
                if u == 12:
                    pool.wait_ge(o_out, at(lay, 6, 2))
                    nc.gpsimd.tensor_tensor(osq[:], onat[0][:], onat[0][:], ALU.mult).then_inc(osq_done, 1)
                    pool.wait_ge(od_ms, at(lay, 1, 1))
                    nc.gpsimd.tensor_tensor(rsd[:], msd[:], neghalf[:, 0:8], ALU.pow).then_inc(od_pow, 1)

        NHG = 2 * LEVELS
        HG0, AQ0, ATT0 = 9, 24, 36
        EARLY = ((2, 0), (4, 1), (6, 2), (8, 3))
        NSEC = 4 + 6

        def at2(lay, per_layer, k):
            return lay * per_layer + (k - LAYERS * per_layer)

        def unit2_done(eng, lay, u):
            eng.wait_ge(slot_used[u % SLOTS], use(2, u % SLOTS, lay, mix_use(u) + 1))

        def mix2_sp(sp, lay):
            for u in range(MIX2):
                s = u % SLOTS
                if u < PROJ2:
                    weights, row, col = t["w_in2"], lay * D + ((u % 2) * 512 - LAYERS * D), slice(CHUNKS2[u // 2], CHUNKS2[u // 2] + 512)
                elif u < PROJ2 + 4:
                    half, kh = divmod(u - PROJ2, 2)
                    weights, row, col = t["w_a"], lay * D + (kh * 512 - LAYERS * D), halves(half)
                elif u < PROJ2 + 6:
                    weights, row, col = t["w_b"], lay * 512 - LAYERS * 512, halves(u - PROJ2 - 4)
                else:
                    kh, half = divmod(u - PROJ2 - 6, 2)
                    weights, row, col = t["w_out2"], lay * D + (kh * 512 - LAYERS * D), halves(half)
                sp.wait_ge(low_done[s], use(2, s, lay, mix_use(u)))
                load_unit(sp, s, weights, row, col)

        def mix2_pe(pe, lay):
            norm_pe(pe, lay, 1)
            for u in range(MIX2):
                s = u % SLOTS
                if u < PROJ2:
                    c, half = divmod(u, 2)
                    if c == 0:
                        pe.wait_ge(xl_done, at(lay, 24, 8 + 4 * half + 4))
                    if half == 0 and c >= 2:
                        pe.wait_ge(chunk_out2, at2(lay, CH2, c - 1))
                    lhs = [(xh[:, 4 * half + k, :], xl[:, 4 * half + k, :]) for k in range(4)]
                    out, first, last = acc[c % 2], half == 0, half == 1
                elif u < PROJ2 + 4:
                    half, kh = divmod(u - PROJ2, 2)
                    if kh == 0:
                        pe.wait_ge(chunk_out2, at2(lay, CH2, CH2 - 1 + half))
                    pe.wait_ge(oaTl_done, at2(lay, 8, 4 * kh + 4))
                    lhs = [(oaTh[:, 4 * kh + k, :], oaTl[:, 4 * kh + k, :]) for k in range(4)]
                    out, first, last = acc[(CH2 + half) % 2], kh == 0, kh == 1
                elif u < PROJ2 + 6:
                    half = u - PROJ2 - 4
                    pe.wait_ge(proj_out2, at2(lay, 4, half + 1))
                    pe.wait_ge(obTl_done, at2(lay, 2, 2))
                    lhs = [(obTh[:, k, :], obTl[:, k, :]) for k in range(4)]
                    out, first, last = acc[(CH2 + half) % 2], True, True
                else:
                    kh, half = divmod(u - PROJ2 - 6, 2)
                    if kh == 0:
                        pe.wait_ge(proj_out2, at2(lay, 4, 3 + half))
                    pe.wait_ge(mTl_done2, at2(lay, 4, 2 * kh + 2))
                    lhs = [(xh[:, 4 * kh + k, :], xl[:, 4 * kh + k, :]) for k in range(4)]
                    out, first, last = [YMIX[tt][half] for tt in range(TT)], kh == 0, kh == 1
                pe.wait_ge(low_done[s], use(2, s, lay, mix_use(u) + 1))
                for k in range(4):
                    mm = product(pe, [[o] for o in out], lhs[k][0], lhs[k][1], s, k * 512, 512, first and k == 0, last and k == 3)
                mm.then_inc(slot_used[s], 1)
                mix2_tail(pe, lay, u)

        def mix2_tail(pe, lay, u):
            for hf, step, b0 in ((0, HG0 + LEVELS, 2), (1, HG0 + NHG, 0)):
                if u == step:
                    pe.wait_ge(lev_out, at2(lay, NHG, LEVELS * (hf + 1)))
                    pe.wait_ge(chunk_out2, at2(lay, CH2, 5 + hf))
                    if hf == 0:
                        pe.wait_ge(f_done, at2(lay, 2, 2))
                    for h in range(4):
                        o = wk[b0 + h // 2][:, (h % 2) * SEQ:(h % 2 + 1) * SEQ]
                        v = hv[:, :, (4 * hf + h) * P:(4 * hf + h + 1) * P]
                        pe.matmul(o[:, 0:P], att[:, h, 0, :], v[:, 0, :], start=True, stop=True)
                        pe.matmul(o[:, P:SEQ], att[:, h, 2, :], v[:, 0, :], start=True, stop=False)
                        mm = pe.matmul(o[:, P:SEQ], att[:, h, 1, :], v[:, 1, :], start=False, stop=True)
                    mm.then_inc(pvh_done, 1)
            n = u - HG0
            if 0 <= n < NHG:
                hf, lev = divmod(n, LEVELS)
                if n == 0:
                    pe.wait_ge(hq_out, at2(lay, 2, 2))
                else:
                    pe.wait_ge(lev_out, at2(lay, NHG, n))
                if lev == 0:
                    pe.wait_ge(k_done, at2(lay, 2, hf + 1))
                else:
                    pe.wait_ge(A_done, at2(lay, 2 * (LEVELS - 1), (LEVELS - 1) * hf + lev))
                for h in range(4):
                    hd = 4 * hf + h
                    if lev == LEVELS - 1:
                        mm = pe.matmul(wk[0][:, h * P:(h + 1) * P], Av[:, h, 0:P], Av[:, h, P:SEQ], start=True, stop=True)
                        continue
                    for tl in range(TT):
                        cs = slice(tl * P, (tl + 1) * P)
                        k, q = (kT[:, hd, cs], qT[:, hd, cs]) if lev == 0 else (Av[:, h, cs], Av[:, h, cs])
                        mm = pe.matmul(wk[h // 2][:, (h % 2) * SEQ + tl * P:(h % 2) * SEQ + (tl + 1) * P], k, q, start=True, stop=True)
                mm.then_inc(lev_done, 1)
            if u in (29, 30):
                i0 = u - 29
                pe.wait_ge(oa_done, at2(lay, 2, i0 + 1))
                if i0 == 0:
                    pe.wait_ge(oh_out, at2(lay, 2, 2))
                else:
                    pe.wait_ge(oaTl_done, at2(lay, 8, 4))
                for i in range(2):
                    turn_tokens(pe, wk[i], hgt, 4 * i0 + 2 * i).then_inc(oaT_done, 1)
            hd, odd = divmod(u - ATT0 - 2, 2)
            if odd == 0 and 0 <= hd < ATT_HEADS:
                pe.wait_ge(wTa_out, at2(lay, ATT_HEADS, hd + 1))
                if hd == 0:
                    pe.wait_ge(sec_out2, at2(lay, 6, 6))
                if hd == 2:
                    pe.wait_ge(ob_out, at2(lay, 2, 1))
                o = wk[3][:, (hd % 2) * SEQ:(hd % 2 + 1) * SEQ]
                for g in range(ATT_GROUPS):
                    pe.matmul(o[:, 0:P], wTa[:, g, 0:P], av[:, g, 0, hd * P:(hd + 1) * P], start=g == 0, stop=g == ATT_GROUPS - 1)
                for g in range(ATT_GROUPS):
                    pe.matmul(o[:, P:SEQ], wTa[:, g, P:2 * P], av[:, g, 0, hd * P:(hd + 1) * P], start=g == 0, stop=False)
                    mm = pe.matmul(o[:, P:SEQ], wTa[:, g, 2 * P:384], av[:, g, 1, hd * P:(hd + 1) * P], start=False, stop=g == ATT_GROUPS - 1)
                mm.then_inc(dpv_done, 1)
            hd, odd = divmod(u - ATT0 - 1, 2)
            if odd == 0 and 0 <= hd < ATT_HEADS:
                pe.wait_ge(dexp_done, at2(lay, ATT_HEADS, hd + 1))
                for g in range(ATT_GROUPS):
                    for b in range(3):
                        tr = pe.transpose(wk[g][:, b * P:(b + 1) * P], exa[:, g, b * P:(b + 1) * P], ident)
                tr.then_inc(dT_done, 1)
            for step, s in EARLY:
                if u == step:
                    pe.wait_ge(chunk_out2, at2(lay, CH2, s + 1))
                    if s == 2:
                        pe.wait_ge(hq_out, at2(lay, 2, 1))
                    if s == 3:
                        pe.wait_ge(f_done, at2(lay, 2, 1))
                    for i in range(2):
                        tr = turn_tokens(pe, wk[2 * (s % 2) + i], stg[s % 2], 2 * i)
                    tr.then_inc(sec_T2, 1)
            a, odd = divmod(u - AQ0 - 1, 2)
            if odd == 0 and 0 <= a < 6:
                pe.wait_ge(rope_done2, at2(lay, 6, a + 1))
                if a == 0:
                    pe.wait_ge(oh_out, at2(lay, 2, 1))
                else:
                    pe.wait_ge(sec_out2, at2(lay, 6, a))
                for i in range(2):
                    tr = turn_tokens(pe, wk[2 + i], stg[a % 2], 2 * i)
                tr.then_inc(sec_T2, 1)
            if u == 45:
                pe.wait_ge(ob_out, at2(lay, 2, 2))
                pe.wait_ge(wTa_out, at2(lay, ATT_HEADS, ATT_HEADS))
                for i in range(2):
                    turn_tokens(pe, wk[i], ob, 2 * i).then_inc(obT_done, 1)
            if u in (47, 48):
                half = u - 47
                pe.wait_ge(merged2, at2(lay, 2, half + 1))
                if half == 0:
                    pe.wait_ge(obTl_done, at2(lay, 2, 2))
                for i in range(2):
                    turn_tokens(pe, wk[2 * half + i], mrg2, 4 * half + 2 * i).then_inc(mT_done2, 1)
            hd, odd = divmod(u - ATT0, 2)
            if odd == 0 and 0 <= hd < ATT_HEADS:
                if hd == 0:
                    pe.wait_ge(sec_out2, at2(lay, 6, 6))
                    pe.wait_ge(oaTl_done, at2(lay, 8, 8))
                else:
                    pe.wait_ge(wTa_out, at2(lay, ATT_HEADS, hd))
                for g in range(ATT_GROUPS):
                    q, k = aqT[:, 4 * g + hd, :], akT[:, 4 * g + hd, :]
                    pe.matmul(wk[g][:, 0:P], q[:, 0:P], k[:, 0:P], start=True, stop=True)
                    pe.matmul(wk[g][:, P:384], q[:, P:SEQ], k[:, 0:SEQ], start=True, stop=True).then_inc(dsc_done, 1)

        def mix2_act(act, lay):
            for u in range(2):
                split_high(act, 2, u % SLOTS, lay, mix_use(u))
            norm_act(act, lay, 1)
            act.wait_ge(lbw, at2(lay, 1, 1))
            nc.scalar.activation(lbe[:], lbe[:], ACT.Exp).then_inc(lbx, 1)
            act.wait_ge(rstd_done, at(lay, 3, 2))
            for u in range(MIX2 + 1):
                if u + 2 < MIX2:
                    split_high(act, 2, (u + 2) % SLOTS, lay, mix_use(u + 2))
                c = u // 2 - 1
                if u % 2 == 0 and 0 <= c < CH2:
                    unit2_done(act, lay, u - 1)
                    func = ACT.Copy
                    if c < 4:
                        func, dst = (ACT.Silu, ACT.Sigmoid)[c % 2], stg[c % 2]
                        if c >= 2:
                            act.wait_ge(sec_T2, at2(lay, NSEC, c - 1))
                    elif c < 8:
                        dst = (hv, hgt)[(c - 4) // 2][:, :, halves(c % 2)]
                    elif c < 11:
                        dst = av[:, c - 8]
                    elif c < 17:
                        act.wait_ge(sec_T2, at2(lay, NSEC, 4 + c - 11 - 1))
                        dst = stg[(c - 11) % 2]
                    else:
                        dst = gate2[(c - 17) // 2][:, :, halves((c - 17) % 2)]
                    for tt in range(TT):
                        a = nc.scalar.activation(dst[:, tt, :], acc[c % 2][tt][:], func, scale=rstd[:, tt:tt + 1])
                    a.then_inc(chunk_out2, 1)
                for hf, step in ((0, 3), (1, 7)):
                    if u == step:
                        act.wait_ge(sec_T2, at2(lay, NSEC, 2 * hf + 1))
                        for i in range(2):
                            a = nc.scalar.activation(qT[:, 4 * hf + 2 * i:4 * hf + 2 * i + 2, :], wk[i][:].rearrange("p (k n) -> p k n", k=2), ACT.Copy)
                        a.then_inc(hq_out, 1)
                for hf, step in ((0, 5), (1, 9)):
                    if u == step:
                        act.preload_act_table_set(EXP_LN)
                        act.wait_ge(k_done, at2(lay, 2, hf + 1))
                        g = gc[:, 4 * hf:4 * hf + 4, :]
                        nc.scalar.activation(g, g, ACT.Ln).then_inc(lnf_done, 1)
                n = u - HG0
                if 0 <= n < NHG and n % LEVELS:
                    hf, lev = divmod(n, LEVELS)
                    i = (LEVELS - 1) * hf + lev
                    if lev < LEVELS - 1:
                        L = 1 << (lev - 1)
                        d = dl[:].rearrange("p h (b l) -> p (h b) l", l=2 * L)
                        act.wait_ge(diff_ready, at2(lay, 2 * (LEVELS - 2), (LEVELS - 2) * hf + lev))
                        nc.scalar.activation(d[:, :, L:2 * L], d[:, :, L:2 * L], ACT.Exp)
                        nc.scalar.activation(d[:, :, 0:L], d[:, :, 0:L], ACT.Exp, scale=-1.0).then_inc(dec_done, 1)
                    else:
                        act.wait_ge(A_done, at2(lay, 2 * (LEVELS - 1), i - 1))
                        for h in range(4):
                            hd = 4 * hf + h
                            nc.scalar.activation(dl[:, h, 0:P], gc[:, hd, 0:P], ACT.Exp, bias=gc[:, hd, P - 1:P], scale=-1.0)
                        nc.scalar.activation(dl[:, :, P:SEQ], gc[:, 4 * hf:4 * hf + 4, P:SEQ], ACT.Exp).then_inc(dec_done, 1)
                if u == 28:
                    act.wait_ge(chunk_out2, at2(lay, CH2, 8))
                    nc.scalar.activation(hgt[:], hgt[:], ACT.Silu).then_inc(hgs_done, 1)
                a, odd = divmod(u - AQ0, 2)
                if odd == 0 and 0 <= a < 6:
                    act.wait_ge(chunk_out2, at2(lay, CH2, 12 + a))
                    if a > 0:
                        act.wait_ge(rope_done2, at2(lay, 6, a))
                    nc.scalar.activation(rsq[:], stg[a % 2][:], ACT.Square).then_inc(asq_done, 1)
                a, odd = divmod(u - AQ0 - 2, 2)
                if odd == 0 and 0 <= a < 6:
                    act.wait_ge(sec_T2, at2(lay, NSEC, 4 + a + 1))
                    for i in range(2):
                        r = nc.scalar.activation((aqT, akT)[a // 3][:, 4 * (a % 3) + 2 * i:4 * (a % 3) + 2 * i + 2, :],
                                                 wk[2 + i][:].rearrange("p (k n) -> p k n", k=2), ACT.Copy)
                    r.then_inc(sec_out2, 1)
                if u in (30, 31):
                    for kt in range(4 * (u - 30), 4 * (u - 30) + 4):
                        if kt % 2 == 0:
                            act.wait_ge(oaT_done, at2(lay, 4, kt // 2 + 1))
                        nc.scalar.activation(oaTh[:, kt, :], wk[kt // 2 % 2][:, (kt % 2) * SEQ:(kt % 2 + 1) * SEQ], ACT.Copy,
                                             scale=cols[:, C2_OUT + kt:C2_OUT + kt + 1]).then_inc(oaTh_done, 1)
                hd, odd = divmod(u - ATT0 - 2, 2)
                if odd == 0 and 0 <= hd < ATT_HEADS:
                    act.wait_ge(dT_done, at2(lay, ATT_HEADS, hd + 1))
                    if hd > 0:
                        act.wait_ge(dpv_done, at2(lay, ATT_HEADS, hd))
                    for g in range(ATT_GROUPS):
                        a = nc.scalar.activation(wTa[:, g, :], wk[g][:, 0:384], ACT.Copy)
                    a.then_inc(wTa_out, 1)
                hd, odd = divmod(u - ATT0 - 1, 2)
                if odd == 0 and 0 <= hd < ATT_HEADS:
                    act.wait_ge(dmax_done, at2(lay, ATT_HEADS, hd + 1))
                    if hd > 0:
                        act.wait_ge(dT_done, at2(lay, ATT_HEADS, hd))
                    for tt, seg in enumerate((slice(0, P), slice(P, 384))):
                        a = nc.scalar.activation(exa[:, :, seg], sma[:, :, seg], ACT.Exp, bias=nma[:, tt:tt + 1], accum_out=lat[:, hd, tt:tt + 1])
                    a.then_inc(dexp_done, 1)
                k = u - 44
                if 0 <= k < 4:
                    if k == 0:
                        act.wait_ge(chunk_out2, at2(lay, CH2, CH2))
                    g = gate2[k // 2][:, :, halves(k % 2)]
                    nc.scalar.activation(g, g, ACT.Sigmoid).then_inc(sig_done2, 1)
                if u == 46:
                    for i in range(2):
                        act.wait_ge(obT_done, at2(lay, 2, i + 1))
                        nc.scalar.activation(obTh[:, 2 * i:2 * i + 2, :], wk[i][:].rearrange("p (k n) -> p k n", k=2), ACT.Copy).then_inc(obTh_done, 1)
                if u in (48, 49):
                    half = u - 48
                    for i in range(2):
                        act.wait_ge(mT_done2, at2(lay, 4, 2 * half + i + 1))
                        nc.scalar.activation(xh[:, 4 * half + 2 * i:4 * half + 2 * i + 2, :],
                                             wk[2 * half + i][:].rearrange("p (k n) -> p k n", k=2), ACT.Copy).then_inc(mTh_done2, 1)

        def mix2_dve(dve, lay):
            def per_head(x, n):
                return x.unsqueeze(2).broadcast_to((P, n, P))

            for u in range(2):
                split_low(dve, nc.vector, 2, u % SLOTS, lay, mix_use(u))
            norm_dve(dve, lay, 1)
            dve.wait_ge(kblk_in, 32)
            l2 = cols[:, C2_LB:C2_LB + 2 * HG_HEADS].rearrange("p (l h) -> p l h", l=2)
            link(dve, nc.vector.tensor_tensor(lbm[:], l2[:, 0, :], l2[:, 1, :], ALU.max))
            nc.vector.tensor_tensor(lbe[:], l2, lbm[:].unsqueeze(1).broadcast_to((P, 2, HG_HEADS)), ALU.subtract).then_inc(lbw, 1)
            for u in range(MIX2 + 1):
                if u + 2 < MIX2 and (u + 2) % SLOTS != 2:
                    split_low(dve, nc.vector, 2, (u + 2) % SLOTS, lay, mix_use(u + 2))
                if u == 1:
                    dve.wait_ge(lbx, at2(lay, 1, 1))
                    link(dve, nc.vector.tensor_tensor(lbs[:], lbe[:, 0, :], lbe[:, 1, :], ALU.add))
                    link(dve, nc.vector.reciprocal(lbm[:], lbs[:]))
                    link(dve, nc.vector.tensor_tensor(lbe[:], lbe[:], lbm[:].unsqueeze(1).broadcast_to((P, 2, HG_HEADS)), ALU.mult))
                    link(dve, nc.vector.tensor_tensor(lbs[:], lbe[:, 0, :], lbe[:, 1, :], ALU.add))
                    link(dve, nc.vector.tensor_tensor(lbs[:], lbs[:], lbe[:, 0, :], ALU.subtract))
                    link(dve, nc.vector.tensor_scalar(lb[:], lbs[:], cols[:, C2_LAYER:C2_LAYER + 1], None, ALU.mult))
                    link(dve, nc.vector.tensor_scalar(omlb[:], lb[:], -1.0, 1.0, ALU.mult, ALU.add))
                for hf, step in ((0, 5), (1, 9)):
                    if u == step:
                        dve.wait_ge(sec_T2, at2(lay, NSEC, 2 * hf + 2))
                        for h in range(4):
                            hd = 4 * hf + h
                            a = nc.vector.tensor_scalar(gc[:, hd, :], wk[2 + h // 2][:, (h % 2) * SEQ:(h % 2 + 1) * SEQ],
                                                        omlb[:, hd:hd + 1], lb[:, hd:hd + 1], ALU.mult, ALU.add)
                        a.then_inc(f_done, 1)
                        dve.wait_ge(f_done, at2(lay, 2, hf + 1))
                        hs = slice(4 * hf, 4 * hf + 4)
                        nc.vector.tensor_scalar(kT[:, hs, :], gc[:, hs, :], -1.0, 1.0, ALU.mult, ALU.add).then_inc(k_done, 1)
                        dve.wait_ge(lnf_done, at2(lay, 2, hf + 1))
                        for h in range(4):
                            for tl in range(TT):
                                g = gc[:, 4 * hf + h, tl * P:(tl + 1) * P]
                                a = nc.vector.tensor_tensor_scan(g, ones, g, 0.0, ALU.mult, ALU.add)
                        a.then_inc(g_done, 1)
                n = u - HG0
                if 0 <= n < NHG and n % LEVELS:
                    hf, lev = divmod(n, LEVELS)
                    L = 1 << (lev - 1)
                    dve.wait_ge(dec_done, at2(lay, 2 * (LEVELS - 1), (LEVELS - 1) * hf + lev))
                    if lev == 1:
                        dve.wait_ge(hq_out, at2(lay, 2, hf + 1))
                    dve.wait_ge(lev_done, at2(lay, NHG, n))
                    view = [x.rearrange("p h (b l) -> p (h b) l", l=2 * L)
                            for x in (Av[:], dl[:], qT[:, 4 * hf:4 * hf + 4, :], kT[:, 4 * hf:4 * hf + 4, :])]
                    nc.vector.tensor_tensor(view[0][:, :, L:2 * L], view[1][:, :, L:2 * L], view[2][:, :, L:2 * L], ALU.mult)
                    nc.vector.tensor_tensor(view[0][:, :, 0:L], view[1][:, :, 0:L], view[3][:, :, 0:L], ALU.mult).then_inc(A_done, 1)
                n = u - HG0 - 1
                if 0 <= n < NHG:
                    hf, lev = divmod(n, LEVELS)
                    if lev == LEVELS - 1:
                        dve.wait_ge(lev_done, at2(lay, NHG, n + 1))
                    if lev == LEVELS - 1:
                        a = nc.vector.tensor_copy(att[:, :, 2, :], wk[0][:].rearrange("p (h s) -> p h s", h=4))
                    else:
                        mask = kblk[:, K2_LEV + lev * P:K2_LEV + (lev + 1) * P].unsqueeze(1).broadcast_to((P, 2, P))
                        if n == LEVELS:
                            dve.wait_ge(pvh_done, at2(lay, 2, 1))
                        for h in range(4):
                            src = wk[h // 2][:, (h % 2) * SEQ:(h % 2 + 1) * SEQ].rearrange("p (t s) -> p t s", t=TT)
                            if lev == 0:
                                a = nc.vector.tensor_tensor(att[:, h, 0:2, :], src, mask, ALU.mult)
                            else:
                                a = nc.vector.copy_predicated(att[:, h, 0:2, :], mask.bitcast(U32), src)
                    a.then_inc(lev_out, 1)
                for hf, step, b0 in ((0, HG0 + LEVELS + 1, 2), (1, HG0 + NHG + 1, 0)):
                    if u == step:
                        o = osb[hf][:].rearrange("p h t d -> p (h t d)")
                        dve.wait_ge(pvh_done, at2(lay, 2, hf + 1))
                        for i in range(2):
                            a = nc.vector.tensor_copy(o[:, i * 512:(i + 1) * 512], wk[b0 + i][:])
                        a.then_inc(oh_out, 1)
                        dve.wait_ge(oh_sq, at2(lay, 2, hf + 1))
                        link(dve, nc.vector.tensor_reduce(sso[:], oq[hf][:].rearrange("p h t d -> p (h t) d"), AX.X, ALU.add))
                        nc.vector.tensor_scalar(mso[:], sso[:], 1.0 / P, EPS, ALU.mult, ALU.add).then_inc(oh_ms, 1)
                        dve.wait_ge(oh_pow, at2(lay, 2, hf + 1))
                        for tt in range(TT):
                            a = nc.vector.tensor_tensor(hv[:, tt, halves(hf)].rearrange("p (h d) -> p h d", d=P), osb[hf][:, :, tt, :],
                                                        per_head(rso[:].rearrange("p (h t) -> p h t", t=TT)[:, :, tt], 4), ALU.mult)
                        link(dve, a)
                if u == HG0 + NHG + 1:
                    dve.wait_ge(hgs_done, at2(lay, 1, 1))
                    for hf in range(2):
                        g = hgt[:, :, halves(hf)]
                        nc.vector.tensor_tensor(g, g, hv[:, :, halves(hf)], ALU.mult).then_inc(oa_done, 1)
                if u in (30, 31):
                    for kt in range(4 * (u - 30), 4 * (u - 30) + 4):
                        dve.wait_ge(oaTh_done, at2(lay, 8, kt + 2 - kt % 2))
                        nc.vector.scalar_tensor_tensor(oaTl[:, kt, :], wk[kt // 2 % 2][:, (kt % 2) * SEQ:(kt % 2 + 1) * SEQ],
                                                       cols[:, C2_OUT + kt:C2_OUT + kt + 1], oaTh[:, kt, :].bitcast(F32),
                                                       ALU.mult, ALU.subtract).then_inc(oaTl_done, 1)
                a, odd = divmod(u - AQ0, 2)
                if odd == 0 and 0 <= a < 6:
                    x = stg[a % 2][:].rearrange("p t (h d) -> p t h d", d=DH)
                    x8 = stg[a % 2][:].rearrange("p t (h d) -> p (t h) d", d=DH)
                    r8 = rtm[:].rearrange("p t (h d) -> p t h d", d=DH)
                    dve.wait_ge(asq_done, at2(lay, 6, a + 1))
                    link(dve, nc.vector.tensor_reduce(ssa[:], rsq[:].rearrange("p t (h d) -> p (t h) d", d=DH), AX.X, ALU.add))
                    nc.vector.tensor_scalar(msa[:], ssa[:], 1.0 / DH, EPS, ALU.mult, ALU.add).then_inc(ams_done, 1)
                    dve.wait_ge(apow_done, at2(lay, 6, a + 1))
                    link(dve, nc.vector.tensor_tensor(x8, x8, per_head(rsa[:], 8), ALU.mult))
                    gain = cols[:, C2_QK + a * DH:C2_QK + (a + 1) * DH]
                    link(dve, nc.vector.tensor_tensor(x8, x8, gain.unsqueeze(1).broadcast_to((P, 8, DH)), ALU.mult))
                    H = DH // 2
                    for tt in range(TT):
                        sin = kblk[:, K2_SIN + tt * DH:K2_SIN + (tt + 1) * DH].unsqueeze(1).broadcast_to((P, ATT_HEADS, DH))
                        nc.vector.tensor_tensor(r8[:, tt, :, 0:H], x[:, tt, :, H:DH], sin[:, :, 0:H], ALU.mult)
                        nc.vector.tensor_tensor(r8[:, tt, :, H:DH], x[:, tt, :, 0:H], sin[:, :, H:DH], ALU.mult)
                    for tt in range(TT):
                        cos = kblk[:, K2_COS + tt * DH:K2_COS + (tt + 1) * DH].unsqueeze(1).broadcast_to((P, ATT_HEADS, DH))
                        r = nc.vector.tensor_tensor(rsq[:, tt, :].rearrange("p (h d) -> p h d", d=DH), x[:, tt, :, :], cos, ALU.mult)
                    link(dve, r)
                    nc.vector.tensor_tensor(stg[a % 2][:], rsq[:], rtm[:], ALU.add).then_inc(rope_done2, 1)
                for step, p in ((ATT0 + 5, 0), (ATT0 + 9, 1)):
                    if u == step:
                        hs = slice(2 * p, 2 * p + 2)
                        dve.wait_ge(dpv_done, at2(lay, ATT_HEADS, 2 * p + 2))
                        link(dve, nc.vector.reciprocal(rat[:, hs, :], lat[:, hs, :]))
                        for tt in range(TT):
                            r = nc.vector.tensor_tensor(ob[:, tt, :].rearrange("p (h d) -> p h d", d=DH)[:, hs],
                                                        wk[3][:].rearrange("p (h t d) -> p h t d", h=2, t=TT)[:, :, tt, :],
                                                        per_head(rat[:, hs, tt], 2), ALU.mult)
                        r.then_inc(ob_out, 1)
                hd, odd = divmod(u - ATT0 - 1, 2)
                if odd == 0 and 0 <= hd < ATT_HEADS:
                    if hd > 0:
                        dve.wait_ge(dexp_done, at2(lay, ATT_HEADS, hd))
                    for g in range(ATT_GROUPS):
                        dve.wait_ge(dsc_done, at2(lay, 3 * ATT_HEADS, 3 * hd + g + 1))
                        a = nc.vector.scalar_tensor_tensor(sma[:, g, :], wk[g][:, 0:384], DH ** -0.5,
                                                           kblk[:, K2_MASK + 384 * g:K2_MASK + 384 * (g + 1)], ALU.mult, ALU.add)
                    link(dve, a)
                    nc.vector.tensor_reduce(nma[:, 0:1], sma[:, :, 0:P], AX.XY, ALU.max, negate=True)
                    nc.vector.tensor_reduce(nma[:, 1:2], sma[:, :, P:384], AX.XY, ALU.max, negate=True).then_inc(dmax_done, 1)
                for k, (step, b, half, unit) in enumerate(((44, 0, 0, 43), (46, 0, 1, 45), (47, 1, 0, 46), (48, 1, 1, 47))):
                    if u == step:
                        unit2_done(dve, lay, unit)
                        dve.wait_ge(sig_done2, at2(lay, 4, k + 1))
                        dst = mrg2[:, :, halves(half)] if b == 0 else mtm2[:]
                        if k == 3:
                            dve.wait_ge(merged2, at2(lay, 2, 1))
                        for tt in range(TT):
                            a = nc.vector.tensor_tensor(dst[:, tt, :], acc[(CH2 + half) % 2][tt][:], gate2[b][:, tt, halves(half)], ALU.mult)
                        a.then_inc(proj_out2, 1)
                        if b == 1:
                            dve.wait_ge(proj_out2, at2(lay, 4, k + 1))
                            m = mrg2[:, :, halves(half)]
                            nc.vector.tensor_tensor(m, m, mtm2[:], ALU.add).then_inc(merged2, 1)
                if u == 46:
                    for i in range(2):
                        dve.wait_ge(obTh_done, at2(lay, 2, i + 1))
                        nc.vector.tensor_tensor(obTl[:, 2 * i:2 * i + 2, :], wk[i][:].rearrange("p (k n) -> p k n", k=2),
                                                obTh[:, 2 * i:2 * i + 2, :].bitcast(F32), ALU.subtract).then_inc(obTl_done, 1)
                if u in (48, 49):
                    half = u - 48
                    for i in range(2):
                        kt = 4 * half + 2 * i
                        dve.wait_ge(mTh_done2, at2(lay, 4, 2 * half + i + 1))
                        nc.vector.tensor_tensor(xl[:, kt:kt + 2, :], wk[2 * half + i][:].rearrange("p (k n) -> p k n", k=2),
                                                xh[:, kt:kt + 2, :].bitcast(F32), ALU.subtract).then_inc(mTl_done2, 1)

        def mix2_pool(pool, lay):
            norm_pool(pool, lay, 1)
            for u in range(MIX2):
                if u % SLOTS == 2:
                    split_low(pool, nc.gpsimd, 2, 2, lay, mix_use(u))
                n = u - HG0
                if 0 <= n < NHG and 0 < n % LEVELS < LEVELS - 1:
                    hf, lev = divmod(n, LEVELS)
                    L = 1 << (lev - 1)
                    g = gc[:, 4 * hf:4 * hf + 4, :].rearrange("p h (b l) -> p (h b) l", l=2 * L)
                    if lev == 1:
                        pool.wait_ge(g_done, at2(lay, 2, hf + 1))
                    if (LEVELS - 1) * hf + lev > 1:
                        pool.wait_ge(A_done, at2(lay, 2 * (LEVELS - 1), (LEVELS - 1) * hf + lev - 1))
                    nc.gpsimd.tensor_tensor(dl[:].rearrange("p h (b l) -> p (h b) l", l=2 * L), g,
                                            g[:, :, L - 1:L].broadcast_to((P, 4 * SEQ // (2 * L), 2 * L)), ALU.subtract).then_inc(diff_ready, 1)
                for hf, step in ((0, HG0 + LEVELS + 1), (1, HG0 + NHG + 1)):
                    if u == step:
                        pool.wait_ge(oh_out, at2(lay, 2, hf + 1))
                        nc.gpsimd.tensor_tensor(oq[hf][:], osb[hf][:], osb[hf][:], ALU.mult).then_inc(oh_sq, 1)
                        pool.wait_ge(oh_ms, at2(lay, 2, hf + 1))
                        nc.gpsimd.tensor_tensor(rso[:], mso[:], neghalf[:, 0:8], ALU.pow).then_inc(oh_pow, 1)
                a, odd = divmod(u - AQ0, 2)
                if odd == 0 and 0 <= a < 6:
                    pool.wait_ge(ams_done, at2(lay, 6, a + 1))
                    nc.gpsimd.tensor_tensor(rsa[:], msa[:], neghalf[:, 0:8], ALU.pow).then_inc(apow_done, 1)

        t_mix = {1: dict(sp=mix1_sp, pe=mix1_pe, act=mix1_act, dve=mix1_dve, pool=mix1_pool),
                 2: dict(sp=mix2_sp, pe=mix2_pe, act=mix2_act, dve=mix2_dve, pool=mix2_pool)}


        block = ctx.enter_context(nc.Block())

        @block.sync
        def _(sp):
            sp.dma_start(X[:], t["x"].rearrange("(t p) d -> p t d", p=P)).then_inc(x_ready, X_IN)
            sp.dma_start(konst[:], t["konst"]).then_inc(konst_in, 16)
            for blk in (1, 2):
                if blk == 2:
                    sp.wait_ge(x_ready, X_IN + 6 * LAYERS)
                sp.dma_start(kblk[:, 0:(NK1, NK2)[blk - 1]], t["kblk"][blk]).then_inc(kblk_in, 16)
                with sp.Fori((blk - 1) * LAYERS, blk * LAYERS) as lay:
                    sp.wait_ge(x_ready, at(lay, 6, X_IN))
                    l = lay if blk == 1 else lay - LAYERS
                    sp.dma_start(cols[:, 0:(NC1, NC2)[blk - 1]], t["cols"][blk][bass.ds(l * P, P), :]).then_inc(cols_in, 16)
                    post_sp(sp, blk, lay, 0)
                    ffn_sp(sp, blk, lay, 0)
                    post_sp(sp, blk, lay, 1)
                    t_mix[blk]["sp"](sp, lay)
                    post_sp(sp, blk, lay, 2)
                    ffn_sp(sp, blk, lay, 1)
            sp.wait_ge(x_ready, X_IN + 6 * 2 * LAYERS)
            sp.dma_start(t["out"].rearrange("(t p) d -> p t d", p=P), X[:]).then_inc(out_sent, 16)
            sp.wait_ge(out_sent, 16)

        @block.tensor
        def _(pe):
            for s in range(SLOTS):
                pe.sem_inc(slot_used[s], FREE)
            for blk in (1, 2):
                with pe.Fori((blk - 1) * LAYERS, blk * LAYERS) as lay:
                    ffn_pe(pe, blk, lay, 0)
                    t_mix[blk]["pe"](pe, lay)
                    ffn_pe(pe, blk, lay, 1)

        @block.scalar
        def _(act):
            for blk in (1, 2):
                with act.Fori((blk - 1) * LAYERS, blk * LAYERS) as lay:
                    ffn_act(act, blk, lay, 0)
                    post_act(act, blk, lay, 0)
                    t_mix[blk]["act"](act, lay)
                    post_act(act, blk, lay, 1)
                    ffn_act(act, blk, lay, 1)
                    post_act(act, blk, lay, 2)

        @block.vector
        def _(dve):
            for s in range(2):
                dve.sem_inc(low_done[s], FREE)
            for blk in (1, 2):
                with dve.Fori((blk - 1) * LAYERS, blk * LAYERS) as lay:
                    per = LINKS[blk]
                    chain.update(n=0, lay=lay, per=per, off=0 if blk == 1 else LAYERS * (LINKS[1] - LINKS[2]))
                    ffn_dve(dve, blk, lay, 0)
                    post_dve(dve, blk, lay, 0)
                    t_mix[blk]["dve"](dve, lay)
                    post_dve(dve, blk, lay, 1)
                    ffn_dve(dve, blk, lay, 1)
                    post_dve(dve, blk, lay, 2)
                links[blk] = chain["n"]

        @block.gpsimd
        def _(pool):
            nc.gpsimd.memset(neghalf[:], -0.5).then_inc(const_set, 1)
            pool.sem_inc(low_done[2], FREE)
            pool.wait_ge(const_set, 1)
            for blk in (1, 2):
                with pool.Fori((blk - 1) * LAYERS, blk * LAYERS) as lay:
                    ffn_pool(pool, blk, lay, 0)
                    post_pool(pool, blk, lay, 0)
                    t_mix[blk]["pool"](pool, lay)
                    post_pool(pool, blk, lay, 1)
                    ffn_pool(pool, blk, lay, 1)
                    post_pool(pool, blk, lay, 2)
        assert links == LINKS, links


def constants():
    i = np.arange(P)
    konst = np.concatenate([np.eye(P), np.ones((P, P)), i[:, None] >= i[None, :]], 1).astype(np.float32)

    def logit_blocks(ok):
        return np.concatenate([ok[0:P, 0:P], ok[P:SEQ, 0:SEQ]], 1)

    tok = np.arange(SEQ)
    gap = tok[:, None] - tok[None, :]
    causal = np.where(logit_blocks(gap >= 0), 0.0, NEG)
    before = (gap > 0).T
    keep = np.concatenate([before[0:P, :], before[P:SEQ, P:SEQ]], 1)

    def angles(theta, width):
        inv = (np.float32(theta) ** (-np.arange(0, width, 2, dtype=np.float32) / np.float32(width))).astype(np.float32)
        a = (tok.astype(np.float32)[:, None] * inv[None, :]).astype(np.float32)
        return np.cos(a), np.sin(a)

    def by_tile(a):
        return a.reshape(TT, P, -1).transpose(1, 0, 2).reshape(P, -1)

    c1, s1 = angles(500000.0, ROT)
    kb1 = np.concatenate([causal, keep, np.where(keep, 0.0, NEG), by_tile(c1), by_tile(s1)], 1).astype(np.float32)
    c2, s2 = angles(10000.0, DH)
    masks = [np.where(logit_blocks((gap >= 0) & (gap <= w) & (gap % d == 0)), 0.0, NEG) for w, d in PATTERNS]
    levels = [np.eye(P)]
    for n in range(7):
        L = 1 << n
        same = i[:, None] // (2 * L) == i[None, :] // (2 * L)
        levels.append(same & (i[:, None] % (2 * L) < L) & (i[None, :] % (2 * L) >= L))
    kb2 = np.concatenate([by_tile(np.concatenate([c2, c2], 1)), by_tile(np.concatenate([-s2, s2], 1))] + masks + levels, 1).astype(np.float32)
    assert konst.shape[1] == NK0 and kb1.shape[1] == NK1 and kb2.shape[1] == NK2
    return konst, kb1, kb2


WEIGHTS = ["w_in", "w_diff_o", "w_sb_o", "w_moba_o", "w_out", "ffn1_wg", "ffn1_wu", "ffn1_wd", "ffn2_wg", "ffn2_wu", "ffn2_wd",
           "ffn1_w_in_2", "ffn1_w_out_2", "w_in_2", "w_branch_a_2", "w_branch_b_2", "w_out_2", "ffn2_w_in_2", "ffn2_w_out_2",
           "g_ffn1_post", "g_mix_post", "g_ffn2_post"]


def laid_out(inputs):
    arrays = {n: np.ascontiguousarray(inputs[n]) for n in WEIGHTS}
    arrays["x"] = np.ascontiguousarray(inputs["x"]).reshape(SEQ, D)

    def column(a):
        return np.asarray(a).reshape(-1, P).T

    def repeated(a):
        return np.tile(np.asarray(a).reshape(1, -1), (P, 1))

    def const(v):
        return np.full((P, 1), v, np.float32)

    one, two = [], []
    for l in range(LAYERS):
        start = 0.8 - 0.6 * math.exp(-0.3 * l)
        one.append(np.concatenate([column(inputs[n][l]) for n in ("g_ffn1_pre", "g_mix_pre", "g_ffn2_pre", "diff_norm_g")]
                                  + [const(start), const(1.0 - start)]
                                  + [repeated(inputs[n][l]) for n in ("lam_q1", "lam_k1", "lam_q2", "lam_k2")], 1))
        two.append(np.concatenate([column(inputs[n][l]) for n in ("ffn1_norm_2", "mix_norm_2", "ffn2_norm_2", "hgrn_out_norm_2")]
                                  + [column(inputs["hgrn_lb_logits_2"][m]) for m in range(LAYERS)]
                                  + [const(float(l))]
                                  + [repeated(inputs[n][l]) for n in ("attn_q_norm_2", "attn_k_norm_2")], 1))
    arrays["cols1"] = np.ascontiguousarray(np.concatenate(one, 0))
    arrays["cols2"] = np.ascontiguousarray(np.concatenate(two, 0))
    arrays["konst"], arrays["kblk1"], arrays["kblk2"] = constants()
    return arrays


def program(nc, shapes):
    dram = {n: nc.dram_tensor(f"in_{n}", s, F32, kind="ExternalInput").ap() for n, s in shapes.items()}
    out = nc.dram_tensor("out_x", (SEQ, D), F32, kind="ExternalOutput").ap()
    rows = {n: dram[n].rearrange("l k n -> (l k) n") for n in WEIGHTS if len(shapes[n]) == 3}
    build(nc, {
        "x": dram["x"], "out": out, "konst": dram["konst"], "kblk": {1: dram["kblk1"], 2: dram["kblk2"]},
        "cols": {1: dram["cols1"], 2: dram["cols2"]},
        "post": [dram["g_ffn1_post"], dram["g_mix_post"], dram["g_ffn2_post"]],
        "ffn": {1: [(rows["ffn1_wg"], rows["ffn1_wu"], rows["ffn1_wd"], 0), (rows["ffn2_wg"], rows["ffn2_wu"], rows["ffn2_wd"], 0)],
                2: [(rows["ffn1_w_in_2"], rows["ffn1_w_in_2"], rows["ffn1_w_out_2"], FFN),
                    (rows["ffn2_w_in_2"], rows["ffn2_w_in_2"], rows["ffn2_w_out_2"], FFN)]},
        "w_in": rows["w_in"], "w_o": [rows["w_diff_o"], rows["w_sb_o"], rows["w_moba_o"]], "w_out": rows["w_out"],
        "w_in2": rows["w_in_2"], "w_a": rows["w_branch_a_2"], "w_b": rows["w_branch_b_2"], "w_out2": rows["w_out_2"],
    })


def kernel(**inputs):
    import concourse.bacc as _bacc
    from concourse.bass_utils import run_bass_kernel_spmd as _run

    arrays = laid_out(inputs)
    nc = _bacc.Bacc("TRN2", target_bir_lowering=False, num_devices=1)
    program(nc, {n: a.shape for n, a in arrays.items()})
    r = _run(nc, [{f"in_{n}": a for n, a in arrays.items()}], core_ids=[0])
    return r.results[0]["out_x"].reshape(1, SEQ, D)
```

```python
import math
from contextlib import ExitStack

import numpy as np
import concourse.bass as bass
from concourse import mybir

F32 = mybir.dt.float32
F32R = mybir.dt.float32r
U32 = mybir.dt.uint32
ALU = mybir.AluOpType
ACT = mybir.ActivationFunctionType
AX = mybir.AxisListType

P = 128
SEQ = 256
TT = SEQ // P
D = 1024
KT = D // P
LAYERS = 2
EPS = 1e-6
NEG = -1e30
FFN = 2816
FC = 256
FSTEPS = FFN // FC
UNIT = 2048
SLOTS = 3
FREE = 1
LOADED = TT
EXP_LN = "natural_log_exp_and_others"

HD = 64
ROT = HD // 4
DIFF_HEADS, SB_HEADS, MOBA_HEADS = 4, 8, 8
IN1 = 9 * 512 + 3 * D
CH1 = IN1 // 512
Q_DIFF, K_DIFF, V_DIFF, Q_SB, K_SB, V_SB, Q_MOBA, K_MOBA, V_MOBA = range(9)
PROJ1 = 2 * CH1
MIX1 = PROJ1 + 6 + 4

HG_HEADS = 8
ATT_GROUPS, ATT_HEADS, DH = 3, 4, 128
PATTERNS = ((128, 1), (512, 4), (2048, 16))
IN2 = 4 * D + 3 * 1536 + 2 * D
HQ, HF, HI, HG, AQ, AK, AV, GA, GB = 0, D, 2 * D, 3 * D, 4 * D, 4 * D + 1536, 4 * D + 3072, 4 * D + 4608, 5 * D + 4608
CHUNKS2 = [HQ, HF, HQ + 512, HF + 512, HI, HI + 512, HG, HG + 512, AV, AV + 512, AV + 1024,
           AQ, AQ + 512, AQ + 1024, AK, AK + 512, AK + 1024, GA, GA + 512, GB, GB + 512]
CH2 = len(CHUNKS2)
PROJ2 = 2 * CH2
MIX2 = PROJ2 + 4 + 2 + 4
LEVELS = 9

C_G = {0: 0, 1: KT, 2: 2 * KT}
C1_DIFF, C1_LAM0, C1_LAM1, C1_LQK = 24, 25, 26, 27
NC1 = C1_LQK + 4 * HD
C2_OUT, C2_LB, C2_LAYER, C2_QK = 24, 32, 48, 49
NC2 = C2_QK + 2 * ATT_GROUPS * DH
NCOL = max(NC1, NC2)
K_ID, K_ONES, K_TRI = 0, P, 2 * P
NK0 = 3 * P
K1_CAUSAL, K1_KEEP, K1_DROP, K1_COS, K1_SIN = 0, 384, 768, 1152, 1152 + TT * 8
NK1 = K1_SIN + TT * 8
K2_COS, K2_SIN, K2_MASK, K2_LEV = 0, TT * DH, 2 * TT * DH, 2 * TT * DH + 3 * 384
NK2 = K2_LEV + 8 * P
NKB = max(NK1 + D, NK2)


LEAD = ((0, 1), (0, 2))
UP = ((2, 0), (1, 0))
DN = (1, 2)
AHEAD = (0, 2)
POOLS = 2
EDGE = 1


def slot_of(u):
    return u % SLOTS if u < SLOTS else (1, 0, 2)[u % SLOTS]


def slot_uses(units, slot):
    return sum(slot_of(u) == slot for u in range(units))


U1 = [2 * FSTEPS + slot_uses(MIX1, s) for s in range(SLOTS)]
U2 = [2 * FSTEPS + slot_uses(MIX2, s) for s in range(SLOTS)]


def at(lay, per_layer, k):
    return lay * per_layer + k


def use(blk, slot, lay, k):
    if blk == 1:
        return lay * U1[slot] + (FREE + k)
    return lay * U2[slot] + (FREE + LAYERS * (U1[slot] - U2[slot]) + k)


def ffn_use(blk, f, slot):
    return 0 if f == 0 else FSTEPS + slot_uses(MIX1 if blk == 1 else MIX2, slot)


def mix_use(u):
    return FSTEPS + u // SLOTS


LINKS = {1: 52, 2: 42}


def build(nc, t):
    ctx = ExitStack()
    with ctx:
        def sb(name, shape, dt=F32):
            return ctx.enter_context(nc.sbuf_tensor(name, shape, dt))

        def sem(name):
            return ctx.enter_context(nc.semaphore(name))

        raw = [sb(f"raw{s}", [P, UNIT]) for s in range(SLOTS)]
        wh = [sb(f"w_high{s}", [P, UNIT], F32R) for s in range(SLOTS)]
        wl = [sb(f"w_low{s}", [P, UNIT], F32R) for s in range(SLOTS)]
        X = sb("x_res", [P, TT, D])
        xh = sb("xT_high", [P, KT, SEQ], F32R)
        xl = sb("xT_low", [P, KT, SEQ], F32R)
        konst = sb("konst", [P, NK0])
        kblk = sb("kblk", [P, NKB])
        cols = sb("cols", [P, NCOL])
        gain0 = sb("gain0", [P, KT])
        grow = kblk[:, NK1:NK1 + D]
        neghalf = sb("neghalf", [P, 16])
        ss = sb("ss", [P, TT]); ms = sb("ms", [P, TT]); rstd = sb("rstd", [P, TT])
        ssy = sb("ssy", [P, TT, 2]); msy = sb("msy", [P, TT]); rsy = sb("rsy", [P, TT])
        lamp = sb("lam_prod", [P, 2, HD]); lams = sb("lam_sum", [P, 2]); lame = sb("lam_exp", [P, 2])
        lam = sb("lam", [P, 1]); gdiff = sb("gain_diff", [P, 1])
        nmx = sb("neg_max", [P, 4]); lsum = sb("exp_sum", [P, 4]); rsum = sb("inv_sum", [P, 4])
        rsl = sb("inv_sum_lam", [P, 2])
        rmo = sb("inv_moba", [P, TT, MOBA_HEADS]); lmo = sb("sum_moba", [P, TT, MOBA_HEADS])
        ssd = sb("ss_diff", [P, 8]); msd = sb("ms_diff", [P, 8]); rsd = sb("rstd_diff", [P, 8])
        lbe = sb("lb_exp", [P, 2, HG_HEADS]); lbm = sb("lb_max", [P, HG_HEADS]); lbs = sb("lb_sum", [P, HG_HEADS])
        lb = sb("lb", [P, HG_HEADS]); omlb = sb("one_minus_lb", [P, HG_HEADS])
        sso = sb("ss_o", [P, 8]); mso = sb("ms_o", [P, 8]); rso = sb("rstd_o", [P, 8])
        ssa = sb("ss_a", [P, 8]); msa = sb("ms_a", [P, 8]); rsa = sb("rstd_a", [P, 8])
        rat = sb("inv_att", [P, ATT_HEADS, TT]); lat = sb("sum_att", [P, ATT_HEADS, TT]); nma = sb("neg_max_att", [P, TT])

        ARENA = 94 * 1024
        arena = sb("arena", [P, ARENA // 4])
        base = nc.sbuf_base - ARENA

        def over(name, shape, kib, dt=F32):
            size = 4 * int(np.prod(shape[1:]))
            assert kib * 1024 + size <= ARENA, name
            return nc.alloc_sbuf_tensor_at(name, shape, dt, offset=int(base + kib * 1024))

        hTh = over("hT_high", [P, 2, SEQ], 0, F32R)
        hTl = over("hT_low", [P, 2, SEQ], 2, F32R)
        sil = over("silu", [P, TT, FC], 4)
        hid = over("hidden", [P, TT, FC], 6)
        tpost = over("post", [P, TT, D], 8)
        junk = over("squares", [P, TT, D], 16)

        vnat = [over(f"v{b}", [P, TT, 512], 4 * b) for b in range(3)]
        gate1 = [over(f"gate{b}", [P, TT, D], 12 + 8 * b) for b in range(3)]
        stage = [over(f"stage{i}", [P, TT, 512], 36 + 4 * i) for i in range(2)]
        secT = {Q_DIFF: over("dqT", [P, 4, SEQ], 44), K_DIFF: over("dkT", [P, 4, SEQ], 48),
                Q_SB: over("sqT", [P, 4, SEQ], 52), K_SB: over("skT", [P, 4, SEQ], 56),
                Q_MOBA: over("mqT", [P, 4, SEQ], 44), K_MOBA: over("mkT", [P, 4, SEQ], 48)}
        oTh = [over(f"oT_high{b}", [P, 4, SEQ], k, F32R) for b, k in enumerate((60, 52, 0))]
        oTl = [over(f"oT_low{b}", [P, 4, SEQ], k, F32R) for b, k in enumerate((64, 56, 4))]
        onat = [over("o_diff", [P, TT, 512], 68), over("o_sb", [P, TT, 512], 72), over("o_moba", [P, TT, 512], 68)]
        smk = [over(f"masked{m}", [P, 384], 76 + 1.5 * m) for m in range(2)]
        ex = [over(f"expd{m}", [P, 384], 79 + 1.5 * m) for m in range(2)]
        osq = over("o_sq", [P, TT, 512], 76)
        wdf = over("w_diff", [P, 384], 82)
        wT = [over(f"wT{i}", [P, 384], 83.5 + 1.5 * i) for i in range(2)]
        saz = over("sb_abs", [P, 384], 86.5)
        sex = over("sb_exp", [P, 384], 88)
        slk = over("sb_keep", [P, 384], 89.5)
        sag = over("sb_arg", [P, 384], 91)
        smx = over("sb_max", [P, 384], 92.5)
        rt = [over(f"rope_t{i}", [P, TT, 8, 8], 76 + 0.5 * i) for i in range(4)]
        mrg = over("merged1", [P, TT, D], 36)
        mtm = over("merge_term", [P, TT, 512], 76)

        qT = over("hqT", [P, HG_HEADS, SEQ], 0)
        kT = over("hkT", [P, HG_HEADS, SEQ], 8)
        gc = over("log_decay", [P, HG_HEADS, SEQ], 16)
        dl = over("decay", [P, 4, SEQ], 24)
        Av = over("decayed", [P, 4, SEQ], 28)
        att = over("hg_att", [P, 4, 3, P], 32)
        hv = over("hg_v", [P, TT, D], 38)
        hgt = over("hg_gate", [P, TT, D], 46)
        stg = [over(f"stage2_{i}", [P, TT, 512], 54 + 4 * i) for i in range(2)]
        aqT = over("aqT", [P, 12, SEQ], 62)
        rsq = over("rope_sq", [P, TT, 512], 74)
        rtm = over("rope_tm", [P, TT, 512], 78)
        av = over("a_v", [P, 3, TT, 512], 82)
        akT = over("akT", [P, 12, SEQ], 0)
        ob = over("o_b", [P, TT, 512], 12)
        oaTh = over("oaT_high", [P, KT, SEQ], 16, F32R)
        oaTl = over("oaT_low", [P, KT, SEQ], 24, F32R)
        gate2 = [over(f"gate2_{b}", [P, TT, D], 32 + 8 * b) for b in range(2)]
        sma = over("masked_att", [P, 3, 384], 48)
        wTa = over("wT_att", [P, 3, 384], 54)
        exa = over("exp_att", [P, 3, 384], 74)
        obTh = over("obT_high", [P, 4, SEQ], 62, F32R)
        obTl = over("obT_low", [P, 4, SEQ], 66, F32R)
        mrg2 = over("merged2", [P, TT, D], 0)
        mtm2 = over("merge_term2", [P, TT, 512], 74)
        osb = [over("o_half0", [P, 4, TT, P], 74), over("o_half1", [P, 4, TT, P], 24)]
        oq = [over("o_sq0", [P, 4, TT, P], 78), over("o_sq1", [P, 4, TT, P], 28)]

        ps = [ctx.enter_context(nc.psum_tensor(f"bank{b}", [P, 512], F32)) for b in range(8)]
        acc = [[ps[0], ps[1]], [ps[2], ps[3]]]
        wk = ps[4:8]
        DOWN = [[ps[4], ps[5]], [ps[6], ps[7]]]
        YMIX = [[ps[2], ps[0]], [ps[3], ps[1]]]

        ident = konst[:, K_ID:K_ID + P]
        ones = konst[:, K_ONES:K_ONES + P]
        tri = konst[:, K_TRI:K_TRI + P]

        konst_in = sem("konst_in"); kblk_in = sem("kblk_in"); cols_in = sem("cols_in"); grow_in = sem("grow_in")
        out_sent = sem("out_sent"); const_set = sem("const_set")
        raw_in = [sem(f"raw_in{s}") for s in range(SLOTS)]
        high_done = [sem(f"high_done{s}") for s in range(SLOTS)]
        low_done = [sem(f"low_done{s}") for s in range(SLOTS)]
        slot_used = [sem(f"slot_used{s}") for s in range(SLOTS)]
        x_in = sem("x_in"); x_ready = sem("x_ready"); y_half = sem("y_half"); gain0_in = sem("gain0_in"); xT_done = sem("xT_done"); xh_done = sem("xh_done"); xl_done = sem("xl_done")
        ss_done = sem("ss_done"); ms_done = sem("ms_done"); rstd_done = sem("rstd_done")
        silu_done = sem("silu_done"); hid_done = sem("hid_done")
        hT_done = sem("hT_done"); hTh_done = sem("hTh_done"); hTl_done = sem("hTl_done")
        ssy_done = sem("ssy_done"); msy_done = sem("msy_done"); rsy_done = sem("rsy_done")
        dve_link = sem("dve_link"); lam_sum = sem("lam_sum_done"); lam_exp = sem("lam_exp_done")
        chunk_out = sem("chunk_out")
        rope_done = sem("rope_done"); sec_T = sem("sec_T"); sec_out = sem("sec_out")
        score_done = sem("score_done"); mask_done = sem("mask_done"); max_done = sem("max_done"); exp_done = sem("exp_done")
        wdf_done = sem("wdf_done"); wT_done = sem("wT_done"); wT_out = sem("wT_out")
        z_done = sem("z_done"); abs_done = sem("abs_done"); sbe_done = sem("sbe_done"); ln_done = sem("ln_done")
        keep_done = sem("keep_done"); cum_done = sem("cum_done"); arg_done = sem("arg_done"); sbw_done = sem("sbw_done")
        pv_done = sem("pv_done"); o_out = sem("o_out")
        osq_done = sem("osq_done"); od_ms = sem("od_ms"); od_pow = sem("od_pow"); od_done = sem("od_done")
        oT_done = sem("oT_done"); oTh_done = sem("oTh_done"); oTl_done = sem("oTl_done")
        proj_out = sem("proj_out"); sig_done = sem("sig_done"); merged = sem("merged")
        mT_done = sem("mT_done"); mTh_done = sem("mTh_done"); mTl_done = sem("mTl_done")
        lbx = sem("lb_exp_done"); lbw = sem("lb_max_done")
        f_done = sem("f_done"); lnf_done = sem("lnf_done"); g_done = sem("g_done"); k_done = sem("k_done")
        diff_ready = sem("diff_ready"); dec_done = sem("dec_done"); A_done = sem("A_done")
        lev_done = sem("lev_done"); lev_out = sem("lev_out")
        pvh_done = sem("pvh_done"); oh_out = sem("oh_out"); oh_sq = sem("oh_sq"); oh_ms = sem("oh_ms"); oh_pow = sem("oh_pow")
        hgs_done = sem("hgs_done"); oa_done = sem("oa_done")
        asq_done = sem("asq_done"); ams_done = sem("ams_done"); apow_done = sem("apow_done")
        
        chunk_out2 = sem("chunk_out2"); dT_done = sem("dT_done"); dexp_done = sem("dexp_done"); dmax_done = sem("dmax_done"); dpv_done = sem("dpv_done")
        dsc_done = sem("dsc_done"); hq_out = sem("hq_out"); mT_done2 = sem("mT_done2"); mTh_done2 = sem("mTh_done2"); mTl_done2 = sem("mTl_done2")
        merged2 = sem("merged2"); oaT_done = sem("oaT_done"); oaTh_done = sem("oaTh_done"); oaTl_done = sem("oaTl_done"); obT_done = sem("obT_done")
        obTh_done = sem("obTh_done"); obTl_done = sem("obTl_done"); ob_out = sem("ob_out"); proj_out2 = sem("proj_out2"); rope_done2 = sem("rope_done2")
        sec_T2 = sem("sec_T2"); sec_out2 = sem("sec_out2"); sig_done2 = sem("sig_done2"); wTa_out = sem("wTa_out")
        links = {}

        def split_high(act, blk, slot, lay, k):
            act.wait_ge(raw_in[slot], use(blk, slot, lay, k + 1 - FREE) * 32)
            act.wait_ge(slot_used[slot], use(blk, slot, lay, k))
            nc.scalar.activation(wh[slot][:], raw[slot][:], ACT.Copy).then_inc(high_done[slot], 1)

        def split_low(eng, ops, blk, slot, lay, k):
            eng.wait_ge(high_done[slot], use(blk, slot, lay, k + 1 - FREE))
            ops.tensor_tensor(wl[slot][:], raw[slot][:], wh[slot][:].bitcast(F32), ALU.subtract).then_inc(low_done[slot], 1)

        def product(pe, outs, xhi, xlo, slot, col, n, start, stop, tiles=range(TT)):
            for tt in tiles:
                rows = slice(tt * P, (tt + 1) * P)
                for x, w, first, last in ((xhi, wh, True, False), (xhi, wl, False, False), (xlo, wh, False, True)):
                    for j, o in enumerate(outs[tt]):
                        mm = pe.matmul(o[:, 0:n], x[:, rows], w[slot][:, col + j * n:col + (j + 1) * n],
                                       start=start and first, stop=stop and last)
            return mm

        def gain(n, kt):
            return gain0[:, kt:kt + 1] if n == 0 else cols[:, C_G[n] + kt:C_G[n] + kt + 1]

        def norm_pe(pe, lay, n, tt):
            pe.wait_ge(konst_in, 16)
            pe.wait_ge(x_in, 16)
            pe.wait_ge(x_ready, at(lay, 6, LOADED + 2 * n - 1 + tt))
            for kt in range(KT):
                tr = pe.transpose(wk[2 * tt + kt // 4][:, (kt % 4) * P:(kt % 4 + 1) * P], X[:, tt, kt * P:(kt + 1) * P], ident)
                if kt % 4 == 3:
                    tr.then_inc(xT_done, 1)

        def norm_act(act, lay, n):
            for tt in range(TT):
                for kt in range(KT):
                    if kt % 4 == 0:
                        act.wait_ge(xT_done, at(lay, 12, 4 * n + 2 * tt + kt // 4 + 1))
                    if tt == 0 and kt == 0 and n == 0:
                        act.wait_ge(gain0_in, at(lay, 16, 16))
                    if tt == 0 and kt == 0 and n == 1:
                        act.wait_ge(cols_in, at(lay, 16, 16))
                    nc.scalar.activation(xh[:, kt, tt * P:(tt + 1) * P], wk[2 * tt + kt // 4][:, (kt % 4) * P:(kt % 4 + 1) * P],
                                         ACT.Copy, scale=gain(n, kt)).then_inc(xh_done, 1)
            for tt in range(TT):
                nc.scalar.activation(junk[:, tt, :], X[:, tt, :], ACT.Square, accum_out=ss[:, tt:tt + 1]).then_inc(ss_done, 1)

        def norm_dve(dve, lay, n, tt):
            for kt in range(KT):
                if kt % 4 == 0:
                    dve.wait_ge(xh_done, at(lay, 48, 16 * n + 8 * tt + kt + 4))
                nc.vector.scalar_tensor_tensor(xl[:, kt, tt * P:(tt + 1) * P], wk[2 * tt + kt // 4][:, (kt % 4) * P:(kt % 4 + 1) * P],
                                               gain(n, kt), xh[:, kt, tt * P:(tt + 1) * P].bitcast(F32),
                                               ALU.mult, ALU.subtract).then_inc(xl_done, 1)
            if tt == TT - 1:
                dve.wait_ge(ss_done, at(lay, 6, 2 * n + 2))
                nc.vector.tensor_scalar(ms[:], ss[:], 1.0 / D, EPS, ALU.mult, ALU.add).then_inc(ms_done, 1)

        def lead_in(pe, blk, lay, n, slots, used):
            norm_pe(pe, lay, n, 0)
            for tt in range(TT):
                for half, s in enumerate(slots):
                    if tt == 0:
                        pe.wait_ge(low_done[s], use(blk, s, lay, used(s) + 1))
                    for k in range(4):
                        kt = 4 * half + k
                        pe.wait_ge(xl_done, at(lay, 48, 16 * n + 8 * tt + kt + 1))
                        mm = product(pe, [[acc[0][0]], [acc[0][1]]], xh[:, kt, :], xl[:, kt, :], s, k * 512, 512,
                                     kt == 0, kt == KT - 1, tiles=(tt,))
                    if tt == TT - 1:
                        mm.then_inc(slot_used[s], 1)
                    if tt == 0 and half == 0:
                        norm_pe(pe, lay, n, 1)

        def norm_pool(pool, lay, n):
            pool.wait_ge(ms_done, at(lay, 3, n + 1))
            nc.gpsimd.tensor_tensor(rstd[:], ms[:], neghalf[:, 0:TT], ALU.pow).then_inc(rstd_done, 1)

        def ffn_pe(pe, blk, lay, f):
            (sa, sb), sd = UP[f], DN[f]
            b = [ffn_use(blk, f, s) for s in range(SLOTS)]

            def up(i):
                for half, s, before in ((0, sa, b[sa] - 1), (1, sb, b[sb])):
                    pe.wait_ge(low_done[s], use(blk, s, lay, before + 1) + i)
                    for k in range(4):
                        kt = 4 * half + k
                        mm = product(pe, [[acc[0][tt]] for tt in range(TT)], xh[:, kt, :], xl[:, kt, :],
                                     s, k * 512, 512, kt == 0, kt == KT - 1)
                    mm.then_inc(slot_used[s], 1)

            def down(i, k, slot, start, stop, tiles=range(TT)):
                pe.wait_ge(hTl_done, at(lay, 44, 2 * FSTEPS * f + k + 1) + i * 2)
                if k == 0:
                    before = b[sd] + 1 if slot == sd else b[sa]
                    pe.wait_ge(low_done[slot], use(blk, slot, lay, before + 1) + i)
                return product(pe, DOWN, hTh[:, k, :], hTl[:, k, :], slot, k * D, 512, start and k == 0, stop and k == 1, tiles)

            def turn(i):
                pe.wait_ge(hid_done, at(lay, 22, FSTEPS * f + 1) + i)
                for k in range(2):
                    for tt in range(TT):
                        tr = pe.transpose(ps[2 + k][:, tt * P:(tt + 1) * P],
                                          hid[:, tt, k * P:(k + 1) * P], ident)
                tr.then_inc(hT_done, 1)

            lead_in(pe, blk, lay, 2 * f, LEAD[f], lambda s: b[s])
            turn(0)
            up(1)
            down(0, 0, sd, True, False)
            turn(1)
            down(0, 1, sd, True, False).then_inc(slot_used[sd], 1)
            with pe.Fori(2, FSTEPS) as i:
                up(i)
                down(i - 1, 0, sd, False, False)
                turn(i)
                down(i - 1, 1, sd, False, False).then_inc(slot_used[sd], 1)
            for tt in range(TT):
                for k in range(2):
                    mm = down(FSTEPS - 1, k, sa, False, True, tiles=(tt,))
                mm.then_inc(y_half if tt == 0 else slot_used[sa], 1)

        def ffn_act(act, blk, lay, f):
            (sa, sb), sd = UP[f], DN[f]
            b = [ffn_use(blk, f, s) for s in range(SLOTS)]

            def silu(i):
                if isinstance(i, int):
                    s = LEAD[f][1]
                    act.wait_ge(slot_used[s], use(blk, s, lay, b[s] + 1))
                else:
                    act.wait_ge(slot_used[sb], use(blk, sb, lay, b[sb] + 1) + i)
                for tt in range(TT):
                    a = nc.scalar.activation(sil[:, tt, :], acc[0][tt][:, 0:FC], ACT.Silu, scale=rstd[:, tt:tt + 1])
                a.then_inc(silu_done, 1)

            def turn_high(i):
                act.wait_ge(hT_done, at(lay, 22, FSTEPS * f + 1) + i)
                for k in range(2):
                    if k == 1:
                        act.wait_ge(slot_used[sd], use(blk, sd, lay, b[sd] + (LEAD[f][1] == sd)) + i)
                    nc.scalar.activation(hTh[:, k, :], ps[2 + k][:, 0:SEQ], ACT.Copy).then_inc(hTh_done, 1)

            split_high(act, blk, EDGE, lay, b[EDGE])
            norm_act(act, lay, 2 * f)
            act.preload_act_table(ACT.Silu)
            act.wait_ge(rstd_done, at(lay, 3, 2 * f + 1))
            silu(0)
            split_high(act, blk, sb, lay, b[sb] + 1)
            turn_high(0)
            split_high(act, blk, sd, lay, b[sd] + 1)
            with act.Fori(1, FSTEPS) as i:
                split_high(act, blk, sa, lay, b[sa] + i)
                silu(i)
                split_high(act, blk, sb, lay, b[sb] + 1 + i)
                turn_high(i)
                split_high(act, blk, sd, lay, b[sd] + 1 + i)

        def ffn_dve(dve, blk, lay, f):
            (sa, sb), sd = UP[f], DN[f]
            b = [ffn_use(blk, f, s) for s in range(SLOTS)]

            def low(slot, k):
                if slot != POOLS:
                    split_low(dve, nc.vector, blk, slot, lay, b[slot] + k)

            def hidden(i):
                dve.wait_ge(silu_done, at(lay, 22, FSTEPS * f + 1) + i)
                for tt in range(TT):
                    h = nc.vector.scalar_tensor_tensor(hid[:, tt, :], acc[0][tt][:, FC:2 * FC], rstd[:, tt:tt + 1],
                                                       sil[:, tt, :], ALU.mult, ALU.mult)
                h.then_inc(hid_done, 1)

            def turn_low(i):
                for k in range(2):
                    dve.wait_ge(hTh_done, at(lay, 44, 2 * FSTEPS * f + k + 1) + i * 2)
                    nc.vector.tensor_tensor(hTl[:, k, :], ps[2 + k][:, 0:SEQ], hTh[:, k, :].bitcast(F32),
                                            ALU.subtract).then_inc(hTl_done, 1)

            norm_dve(dve, lay, 2 * f, 0)
            low(EDGE, 0)
            norm_dve(dve, lay, 2 * f, 1)
            hidden(0)
            low(sb, 1)
            turn_low(0)
            low(sd, 1)
            with dve.Fori(1, FSTEPS) as i:
                low(sa, i)
                hidden(i)
                low(sb, i + 1)
                turn_low(i)
                low(sd, i + 1)

        def ffn_pool(pool, blk, lay, f):
            norm_pool(pool, lay, 2 * f)
            first = 1 if POOLS == UP[f][0] else 0
            with pool.Fori(0, FSTEPS - first) as i:
                split_low(pool, nc.gpsimd, blk, POOLS, lay, ffn_use(blk, f, POOLS) + 1 + i)

        def ffn_sp(sp, blk, lay, f):
            gate_w, up_w, down_w, up_col = t["ffn"][blk][f]
            (sa, sb), sd = UP[f], DN[f]
            row = lay * D if blk == 1 else lay * D - LAYERS * D
            drow = lay * FFN if blk == 1 else lay * FFN - LAYERS * FFN

            def free(slot, k):
                sp.wait_ge(low_done[slot], use(blk, slot, lay, ffn_use(blk, f, slot)) + k)

            def up(col, slots, uses):
                for half, (s, k) in enumerate(zip(slots, uses)):
                    free(s, k)
                    dst = raw[s][:].rearrange("p (k g n) -> p k g n", k=4, g=2)
                    for g, (w, c0) in enumerate(((gate_w, 0), (up_w, up_col))):
                        sp.dma_start(dst[:, :, g, :], w[bass.ds(row + 4 * half * P, 4 * P), bass.ds(col + c0, FC)]
                                     .rearrange("(k p) n -> p k n", p=P)).then_inc(raw_in[s], 16)

            def down(i, s, k):
                free(s, k)
                for h in range(2):
                    sp.dma_start(raw[s][:, h * D:(h + 1) * D], down_w[bass.ds(drow + i * FC + h * P, P), :]).then_inc(raw_in[s], 16)

            up(0, LEAD[f], (0, 0))
            with sp.Fori(0, FSTEPS - 1) as i:
                up(i * FC + FC, UP[f], (i, i + 1))
                down(i, sd, i + 1)
            down(FSTEPS - 1, sa, FSTEPS - 1)

        def y_wait(eng, blk, lay, f, tt):
            if tt == 0:
                eng.wait_ge(y_half, at(lay, 3, f + 1))
            elif f == 1:
                u = (MIX1 if blk == 1 else MIX2) - 1
                eng.wait_ge(slot_used[slot_of(u)], use(blk, slot_of(u), lay, mix_use(u) + 1))
            else:
                s = UP[f // 2][0]
                eng.wait_ge(slot_used[s], use(blk, s, lay, ffn_use(blk, f // 2, s) + FSTEPS))

        def post_act(act, blk, lay, f):
            Y = YMIX if f == 1 else DOWN
            for tt in range(TT if blk == 1 else 0):
                y_wait(act, blk, lay, f, tt)
                for j in range(2):
                    a = nc.scalar.activation(junk[:, tt, j * 512:(j + 1) * 512], Y[tt][j][:], ACT.Square, accum_out=ssy[:, tt, j:j + 1])
                a.then_inc(ssy_done, 1)

        def post_dve(dve, blk, lay, f):
            Y = YMIX if f == 1 else DOWN
            weight = 1.0 if f == 1 else 0.5
            for tt in range(TT):
                if blk == 2:
                    y_wait(dve, blk, lay, f, tt)
                    for j in range(2):
                        xs = X[:, tt, j * 512:(j + 1) * 512]
                        r = nc.vector.scalar_tensor_tensor(xs, Y[tt][j][:], weight, xs, ALU.mult, ALU.add)
                    r.then_inc(x_ready, 1)
                    continue
                dve.wait_ge(ssy_done, at(lay, 6, 2 * f + tt + 1))
                link(dve, nc.vector.tensor_tensor(msy[:, tt:tt + 1], ssy[:, tt, 0:1], ssy[:, tt, 1:2], ALU.add))
                nc.vector.tensor_scalar(msy[:, tt:tt + 1], msy[:, tt:tt + 1], 1.0 / D, EPS, ALU.mult, ALU.add).then_inc(msy_done, 1)
                if tt == 0:
                    dve.wait_ge(grow_in, at(lay, 48, 16 * (f + 1)))
                dve.wait_ge(rsy_done, at(lay, 6, 2 * f + tt + 1))
                for j in range(2):
                    c = slice(j * 512, (j + 1) * 512)
                    a = nc.vector.scalar_tensor_tensor(tpost[:, tt, c], Y[tt][j][:], rsy[:, tt:tt + 1], grow[:, c], ALU.mult, ALU.mult)
                link(dve, a)
                nc.vector.scalar_tensor_tensor(X[:, tt, :], tpost[:, tt, :], weight, X[:, tt, :], ALU.mult, ALU.add).then_inc(x_ready, 1)

        def post_pool(pool, blk, lay, f):
            for tt in range(TT if blk == 1 else 0):
                pool.wait_ge(msy_done, at(lay, 6, 2 * f + tt + 1))
                nc.gpsimd.tensor_tensor(rsy[:, tt:tt + 1], msy[:, tt:tt + 1], neghalf[:, 0:1], ALU.pow).then_inc(rsy_done, 1)

        def post_sp(sp, blk, lay, f):
            if blk == 1:
                sp.dma_start(grow, t["post"][bass.ds(lay * 3 + f, 1), :].broadcast_to((P, D))).then_inc(grow_in, 16)

        chain = {"n": 0, "lay": 0, "per": 0, "off": 0}

        def link(dve, ins):
            chain["n"] += 1
            ins.then_inc(dve_link, 1)
            dve.wait_ge(dve_link, chain["lay"] * chain["per"] + (chain["off"] + chain["n"]))

        SECTIONS = (Q_DIFF, K_DIFF, Q_SB, K_SB, Q_MOBA, K_MOBA)
        DIFF0, SB0, MOBA0 = 6, 12, 20
        V_CHUNKS = {V_DIFF: 0, V_SB: 1, V_MOBA: 2}
        BRANCH = [(u, (u - PROJ1) % 3, (u - PROJ1) // 3) for u in range(PROJ1, PROJ1 + 6)]
        NDI, NSB, NMO = DIFF_HEADS, SB_HEADS, MOBA_HEADS
        NPV = NDI + NSB + NMO

        def halves(k):
            return slice(k * 512, (k + 1) * 512)

        def unit1_done(eng, lay, u):
            eng.wait_ge(slot_used[slot_of(u)], use(1, slot_of(u), lay, mix_use(u) + 1))

        def load_unit(sp, s, weights, row, col):
            for k in range(2):
                sp.dma_start(raw[s][:, k * D:(k + 1) * D].rearrange("p (k n) -> p k n", k=2),
                             weights[bass.ds(row + k * SEQ, SEQ), col].rearrange("(k p) n -> p k n", p=P)).then_inc(raw_in[s], 16)

        def mix1_sp(sp, lay):
            for u in range(MIX1):
                s = slot_of(u)
                if u < PROJ1:
                    weights, row, col = t["w_in"], lay * D + (u % 2) * 512, halves(u // 2)
                elif u < PROJ1 + 6:
                    _, b, half = BRANCH[u - PROJ1]
                    weights, row, col = t["w_o"][b], lay * 512, halves(half)
                else:
                    kh, half = divmod(u - PROJ1 - 6, 2)
                    weights, row, col = t["w_out"], lay * D + kh * 512, halves(half)
                sp.wait_ge(low_done[s], use(1, s, lay, mix_use(u)))
                load_unit(sp, s, weights, row, col)

        def scores1(pe, bank, q, k, lo, blk):
            rows = slice(lo, lo + HD)
            pe.matmul(bank[:, 0:P], q[rows, blk, 0:P], k[rows, blk, 0:P], start=True, stop=True)
            return pe.matmul(bank[:, P:384], q[rows, blk, P:SEQ], k[rows, blk, 0:SEQ], start=True, stop=True)

        def values(pe, out0, out1, w, v0, v1):
            pe.matmul(out0, w[:, 0:P], v0, start=True, stop=True)
            pe.matmul(out1, w[:, P:2 * P], v0, start=True, stop=False)
            return pe.matmul(out1, w[:, 2 * P:384], v1, start=False, stop=True)

        def turn_tokens(pe, bank, src, kt):
            for k in range(2):
                for tt in range(TT):
                    tr = pe.transpose(bank[:, k * SEQ + tt * P:k * SEQ + (tt + 1) * P], src[:, tt, (kt + k) * P:(kt + k + 1) * P], ident)
            return tr

        def mix1_pe(pe, lay):
            lead_in(pe, 1, lay, 1, (0, 1), lambda s: FSTEPS)
            for u in range(2, MIX1 - 2):
                s = slot_of(u)
                if u < PROJ1:
                    c, half = divmod(u, 2)
                    if half == 0 and c >= 2:
                        pe.wait_ge(chunk_out, at(lay, CH1, c - 1))
                    lhs = [(xh[:, 4 * half + k, :], xl[:, 4 * half + k, :]) for k in range(4)]
                    out, first, last = acc[c % 2], half == 0, half == 1
                elif u < PROJ1 + 6:
                    _, b, half = BRANCH[u - PROJ1]
                    c = CH1 + u - PROJ1
                    if u < PROJ1 + 2:
                        pe.wait_ge(chunk_out, at(lay, CH1, c - 1))
                    else:
                        pe.wait_ge(proj_out, at(lay, 6, u - PROJ1 - 1))
                    pe.wait_ge(oTl_done, at(lay, 6, 2 * b + 2))
                    lhs = [(oTh[b][:, k, :], oTl[b][:, k, :]) for k in range(4)]
                    out, first, last = acc[c % 2], True, True
                else:
                    half = u - PROJ1 - 6
                    pe.wait_ge(proj_out, at(lay, 6, 5 + half))
                    pe.wait_ge(mTl_done, at(lay, 4, 2))
                    lhs = [(xh[:, k, :], xl[:, k, :]) for k in range(4)]
                    out, first, last = [YMIX[tt][half] for tt in range(TT)], True, False
                pe.wait_ge(low_done[s], use(1, s, lay, mix_use(u) + 1))
                for k in range(4):
                    mm = product(pe, [[o] for o in out], lhs[k][0], lhs[k][1], s, k * 512, 512, first and k == 0, last and k == 3)
                mm.then_inc(slot_used[s], 1)
                mix1_tail(pe, lay, u)
            pe.wait_ge(mTl_done, at(lay, 4, 4))
            mixer_end(pe, 1, lay, MIX1)

        def mixer_end(pe, blk, lay, units):
            for tt in range(TT):
                for half in range(2):
                    u = units - 2 + half
                    s = slot_of(u)
                    if tt == 0:
                        pe.wait_ge(low_done[s], use(blk, s, lay, mix_use(u) + 1))
                    for k in range(4):
                        mm = product(pe, [[YMIX[t][half]] for t in range(TT)], xh[:, 4 + k, :], xl[:, 4 + k, :], s, k * 512, 512,
                                     False, k == 3, tiles=(tt,))
                    if tt == TT - 1:
                        mm.then_inc(slot_used[s], 1)
                if tt == 0:
                    mm.then_inc(y_half, 1)

        def mix1_tail(pe, lay, u):
            h = u - DIFF0 - 2
            if 0 <= h < NDI:
                pe.wait_ge(wT_out, at(lay, NDI + NMO, h + 1))
                if h == 0:
                    pe.wait_ge(chunk_out, at(lay, CH1, V_DIFF + 1))
                if h == 2:
                    pe.wait_ge(o_out, at(lay, 6, 1))
                o = wk[3][:, (h % 2) * 256:(h % 2 + 1) * 256]
                v = vnat[0][:, :, h * P:(h + 1) * P]
                values(pe, o[:, 0:P], o[:, P:256], wT[h % 2], v[:, 0, :], v[:, 1, :]).then_inc(pv_done, 1)
            j = u - SB0 - 2
            if 0 <= j < NSB:
                pe.wait_ge(sbw_done, at(lay, NSB, j + 1))
                if j % 4 == 0:
                    pe.wait_ge(o_out, at(lay, 6, 2 + j // 4))
                if j == 0:
                    pe.wait_ge(chunk_out, at(lay, CH1, V_SB + 1))
                o = wk[3][:, (j % 4) * P:(j % 4 + 1) * P]
                v = vnat[1][:, :, j * HD:(j + 1) * HD]
                values(pe, o[:, 0:HD], o[:, HD:P], wT[j % 2], v[:, 0, :], v[:, 1, :]).then_inc(pv_done, 1)
            j = u - MOBA0 - 2
            if 0 <= j < NMO:
                pe.wait_ge(wT_out, at(lay, NDI + NMO, NDI + j + 1))
                if j % 4 == 0:
                    pe.wait_ge(o_out, at(lay, 6, 4 + j // 4))
                if j == 0:
                    pe.wait_ge(chunk_out, at(lay, CH1, V_MOBA + 1))
                o = wk[3][:, (j % 4) * P:(j % 4 + 1) * P]
                v = vnat[2][:, :, j * HD:(j + 1) * HD]
                values(pe, o[:, 0:HD], o[:, HD:P], wT[j % 2], v[:, 0, :], v[:, 1, :]).then_inc(pv_done, 1)
            h = u - DIFF0 - 1
            if 0 <= h < NDI:
                pe.wait_ge(wdf_done, at(lay, NDI, h + 1))
                if h > 0:
                    pe.wait_ge(wT_out, at(lay, NDI + NMO, h))
                for b in range(3):
                    tr = pe.transpose(wk[2][:, b * P:(b + 1) * P], wdf[:, b * P:(b + 1) * P], ident)
                tr.then_inc(wT_done, 1)
            j = u - MOBA0 - 1
            if 0 <= j < NMO:
                pe.wait_ge(exp_done, at(lay, NDI + NMO, NDI + j + 1))
                if j == 0:
                    pe.wait_ge(sec_out, at(lay, 12, 12))
                else:
                    pe.wait_ge(wT_out, at(lay, NDI + NMO, NDI + j))
                for b in range(3):
                    tr = pe.transpose(wk[2][:, b * P:(b + 1) * P], ex[j % 2][:, b * P:(b + 1) * P], ident)
                tr.then_inc(wT_done, 1)
            j = u - SB0 - 1
            if 0 <= j < NSB:
                pe.wait_ge(keep_done, at(lay, NSB, j + 1))
                bank = wk[j % 2]
                pe.matmul(bank[:, 0:384], tri, slk[:], start=False, stop=False, skip_group_check=True)
                pe.matmul(bank[:, P:2 * P], ones, slk[:, 2 * P:384], start=False, stop=True, skip_group_check=True).then_inc(cum_done, 1)
            if u in (13, 14):
                pe.wait_ge(od_done, at(lay, 1, 1))
                if u == 13:
                    pe.wait_ge(wT_out, at(lay, NDI + NMO, NDI))
                else:
                    pe.wait_ge(oTl_done, at(lay, 6, 1))
                turn_tokens(pe, wk[2], onat[0], 2 * (u - 13)).then_inc(oT_done, 1)
            if u == 28:
                pe.wait_ge(mask_done, at(lay, 2 * NDI + NMO, 2 * NDI + NMO))
                pe.wait_ge(o_out, at(lay, 6, 4))
                for i in range(2):
                    turn_tokens(pe, wk[i], onat[1], 2 * i).then_inc(oT_done, 1)
            if u == 30:
                pe.wait_ge(oTl_done, at(lay, 6, 4))
                pe.wait_ge(o_out, at(lay, 6, 6))
                for i in range(2):
                    turn_tokens(pe, wk[i], onat[2], 2 * i).then_inc(oT_done, 1)
            if u in (34, 36):
                half = (u - 34) // 2
                pe.wait_ge(merged, at(lay, 2, half + 1))
                if half == 0:
                    pe.wait_ge(oTl_done, at(lay, 6, 6))
                else:
                    pe.wait_ge(wT_out, at(lay, NDI + NMO, NDI + NMO))
                    pe.wait_ge(o_out, at(lay, 6, 6))
                for i in range(2):
                    turn_tokens(pe, wk[2 * half + i], mrg, 4 * half + 2 * i).then_inc(mT_done, 1)
            for si, (first, second, b0, b1) in enumerate(((3, 3, 0, 1), (5, 5, 0, 1), (10, 10, 0, 1), (11, 11, 0, 1), (15, 16, 2, 2), (17, 18, 2, 2))):
                for half, (step, b) in enumerate(((first, b0), (second, b1))):
                    if u != step:
                        continue
                    src = stage[si % 2]
                    if half == 0:
                        if si in (2, 3):
                            pe.wait_ge(chunk_out, at(lay, CH1, SECTIONS[si] + 1))
                        else:
                            pe.wait_ge(rope_done, at(lay, 4, si + 1 if si < 2 else si - 1))
                        if si == 2:
                            pe.wait_ge(mask_done, at(lay, 2 * NDI + NMO, 2 * NDI))
                        elif si == 4:
                            pe.wait_ge(oTl_done, at(lay, 6, 2))
                        elif si > 0:
                            pe.wait_ge(sec_out, at(lay, 12, 2 * si))
                    elif si >= 4:
                        pe.wait_ge(sec_out, at(lay, 12, 2 * si + 1))
                    turn_tokens(pe, wk[b], src, 2 * half).then_inc(sec_T, 1)
            h = u - DIFF0
            if 0 <= h < NDI:
                if h == 0:
                    pe.wait_ge(sec_out, at(lay, 12, 4))
                else:
                    pe.wait_ge(mask_done, at(lay, 2 * NDI + NMO, 2 * h))
                for m in range(2):
                    scores1(pe, wk[m], secT[Q_DIFF], secT[K_DIFF], HD * m, h).then_inc(score_done, 1)
            j = u - SB0
            if 0 <= j < NSB:
                if j == 0:
                    pe.wait_ge(sec_out, at(lay, 12, 8))
                if j >= 2:
                    pe.wait_ge(arg_done, at(lay, NSB, j - 1))
                q, k, rows, blk, bank = secT[Q_SB], secT[K_SB], slice(HD * (j % 2), HD * (j % 2) + HD), j // 2, wk[j % 2]
                pe.matmul(bank[:, 0:SEQ], k[rows, blk, 0:P], q[rows, blk, :], start=True, stop=False, skip_group_check=True)
                pe.matmul(bank[:, SEQ:384], k[rows, blk, P:SEQ], q[rows, blk, P:SEQ], start=False, stop=True, skip_group_check=True).then_inc(z_done, 1)
            j = u - MOBA0
            if 0 <= j < NMO:
                if j < 2:
                    pe.wait_ge(sec_out, at(lay, 12, 12))
                    pe.wait_ge(arg_done, at(lay, NSB, NSB - 1 + j))
                else:
                    pe.wait_ge(mask_done, at(lay, 2 * NDI + NMO, 2 * NDI + j - 1))
                scores1(pe, wk[j % 2], secT[Q_MOBA], secT[K_MOBA], HD * (j % 2), j // 2).then_inc(score_done, 1)

        def mix1_act(act, lay):
            norm_act(act, lay, 1)
            act.preload_act_table_set(EXP_LN)
            act.wait_ge(rstd_done, at(lay, 3, 2))
            for u in range(MIX1 + 1):
                if u < MIX1:
                    split_high(act, 1, slot_of(u + 2), lay, mix_use(u + 2))
                c = u // 2 - 1
                if u % 2 == 0 and 0 <= c < CH1:
                    unit1_done(act, lay, u - 1)
                    if c in SECTIONS:
                        si = SECTIONS.index(c)
                        if si >= 2:
                            act.wait_ge(sec_T, at(lay, 12, 2 * si - 2))
                        dst = stage[si % 2]
                    elif c in V_CHUNKS:
                        dst = vnat[V_CHUNKS[c]]
                    else:
                        dst = gate1[(c - 9) // 2][:, :, halves((c - 9) % 2)]
                    for tt in range(TT):
                        a = nc.scalar.activation(dst[:, tt, :], acc[c % 2][tt][:], ACT.Copy, scale=rstd[:, tt:tt + 1])
                    a.then_inc(chunk_out, 1)
                if u == 4:
                    act.wait_ge(lam_sum, at(lay, 1, 1))
                    nc.scalar.activation(lame[:], lams[:], ACT.Exp).then_inc(lam_exp, 1)
                for si, steps in enumerate(((4, 4), (6, 6), (11, 11), (12, 12), (16, 17), (18, 19))):
                    for half, step in enumerate(steps):
                        if u == step:
                            act.wait_ge(sec_T, at(lay, 12, 2 * si + half + 1))
                            nc.scalar.activation(secT[SECTIONS[si]][:, 2 * half:2 * half + 2, :],
                                                 wk[half if si < 4 else 2][:].rearrange("p (k n) -> p k n", k=2), ACT.Copy,
                                                 scale=HD ** -0.5 if si % 2 == 0 else 1.0).then_inc(sec_out, 1)
                for first, n, i0, pv0 in ((DIFF0 + 2, NDI, 0, 0), (MOBA0 + 2, NMO, NDI, NDI + NSB)):
                    j = u - first
                    if 0 <= j < n:
                        act.wait_ge(wT_done, at(lay, NDI + NMO, i0 + j + 1))
                        if pv0 + j >= 2:
                            act.wait_ge(pv_done, at(lay, NPV, pv0 + j - 1))
                        nc.scalar.activation(wT[j % 2][:], wk[2][:, 0:384], ACT.Copy).then_inc(wT_out, 1)
                for step, n, g in ((DIFF0 + 4, 2, 0), (DIFF0 + 6, 4, 1)):
                    if u == step:
                        act.wait_ge(pv_done, at(lay, NPV, n))
                        nc.scalar.activation(onat[0][:].rearrange("p t (h d) -> p h t d", d=P)[:, 2 * g:2 * g + 2],
                                             wk[3][:].rearrange("p (h t d) -> p h t d", h=2, t=TT), ACT.Copy).then_inc(o_out, 1)
                for step, n, g in ((SB0 + 6, 4, 0), (SB0 + 10, 8, 1)):
                    if u == step:
                        act.wait_ge(pv_done, at(lay, NPV, NDI + n))
                        nc.scalar.activation(onat[1][:].rearrange("p t (h d) -> p h t d", d=HD)[:, 4 * g:4 * g + 4],
                                             wk[3][:].rearrange("p (h t d) -> p h t d", h=4, t=TT), ACT.Copy).then_inc(o_out, 1)
                j = u - SB0 - 2
                if 0 <= j < NSB:
                    act.wait_ge(arg_done, at(lay, NSB, j + 1))
                    act.wait_ge(pv_done, at(lay, NPV, NDI + j - 1))
                    nc.scalar.activation(wT[j % 2][:], sag[:], ACT.Exp).then_inc(sbw_done, 1)
                j = u - SB0 - 1
                if 0 <= j < NSB:
                    act.wait_ge(abs_done, at(lay, NSB, j + 1))
                    if j > 0:
                        act.wait_ge(keep_done, at(lay, NSB, j))
                    nc.scalar.activation(sex[:], saz[:], ACT.Exp).then_inc(sbe_done, 1)
                    act.wait_ge(sbe_done, at(lay, NSB, j + 1))
                    nc.scalar.activation(sex[:], sex[:], ACT.Ln, bias=1.0).then_inc(ln_done, 1)
                h = u - DIFF0 - 1
                if 0 <= h < NDI:
                    act.wait_ge(max_done, at(lay, NDI + NMO, h + 1))
                    if h > 0:
                        act.wait_ge(wdf_done, at(lay, NDI, h))
                    for m in range(2):
                        for tt, seg in enumerate((slice(0, P), slice(P, 384))):
                            a = nc.scalar.activation(ex[m][:, seg], smk[m][:, seg], ACT.Exp, bias=nmx[:, 2 * m + tt:2 * m + tt + 1],
                                                     accum_out=lsum[:, 2 * m + tt:2 * m + tt + 1])
                    a.then_inc(exp_done, 1)
                j = u - MOBA0 - 1
                if 0 <= j < NMO:
                    act.wait_ge(max_done, at(lay, NDI + NMO, NDI + j + 1))
                    if j < 2:
                        act.wait_ge(wdf_done, at(lay, NDI, NDI))
                    else:
                        act.wait_ge(wT_done, at(lay, NDI + NMO, NDI + j - 1))
                    for tt, seg in enumerate((slice(0, P), slice(P, 384))):
                        a = nc.scalar.activation(ex[j % 2][:, seg], smk[j % 2][:, seg], ACT.Exp, bias=nmx[:, 2 * (j % 2) + tt:2 * (j % 2) + tt + 1],
                                                 accum_out=lmo[:, tt, j:j + 1])
                    a.then_inc(exp_done, 1)
                for step, b, i, bank in ((14, 0, 0, 2), (15, 0, 1, 2), (29, 1, 0, 0), (29, 1, 1, 1), (31, 2, 0, 0), (31, 2, 1, 1)):
                    if u == step:
                        act.wait_ge(oT_done, at(lay, 6, 2 * b + i + 1))
                        nc.scalar.activation(oTh[b][:, 2 * i:2 * i + 2, :], wk[bank][:].rearrange("p (k n) -> p k n", k=2), ACT.Copy,
                                             scale=gdiff[:] if b == 0 else 1.0).then_inc(oTh_done, 1)
                k = u - PROJ1
                if 0 <= k < 6:
                    _, b, half = BRANCH[k]
                    if k == 0:
                        act.wait_ge(chunk_out, at(lay, CH1, CH1))
                    g = gate1[b][:, :, halves(half)]
                    nc.scalar.activation(g, g, ACT.Sigmoid).then_inc(sig_done, 1)
                if u in (35, 37):
                    half = (u - 35) // 2
                    for i in range(2):
                        act.wait_ge(mT_done, at(lay, 4, 2 * half + i + 1))
                        nc.scalar.activation(xh[:, 4 * half + 2 * i:4 * half + 2 * i + 2, :],
                                             wk[2 * half + i][:].rearrange("p (k n) -> p k n", k=2), ACT.Copy).then_inc(mTh_done, 1)

        def mix1_dve(dve, lay):
            causal = kblk[:, K1_CAUSAL:K1_CAUSAL + 384]
            keep = kblk[:, K1_KEEP:K1_KEEP + 384]
            drop = kblk[:, K1_DROP:K1_DROP + 384]

            def table(col):
                return kblk[:, col:col + TT * 8].rearrange("p (t e) -> p t e", t=TT).unsqueeze(2).broadcast_to((P, TT, 8, 8))

            for tt in range(TT):
                norm_dve(dve, lay, 1, tt)
            dve.wait_ge(kblk_in, at(lay, 16, 16))
            for u in range(MIX1 + 1):
                if u < MIX1 and slot_of(u + 2) != POOLS:
                    split_low(dve, nc.vector, 1, slot_of(u + 2), lay, mix_use(u + 2))
                if u == 0:
                    qk = cols[:, C1_LQK:C1_LQK + 4 * HD].rearrange("p (a b d) -> p a b d", a=2, b=2)
                    link(dve, nc.vector.tensor_tensor(lamp[:], qk[:, :, 0, :], qk[:, :, 1, :], ALU.mult))
                    nc.vector.tensor_reduce(lams[:], lamp[:], AX.X, ALU.add).then_inc(lam_sum, 1)
                if u == 4:
                    dve.wait_ge(lam_exp, at(lay, 1, 1))
                    link(dve, nc.vector.tensor_tensor(lam[:], lame[:, 0:1], lame[:, 1:2], ALU.subtract))
                    nc.vector.tensor_tensor(lam[:], lam[:], cols[:, C1_LAM0:C1_LAM0 + 1], ALU.add)
                    link(dve, nc.vector.tensor_tensor(gdiff[:], cols[:, C1_DIFF:C1_DIFF + 1], cols[:, C1_LAM1:C1_LAM1 + 1], ALU.mult))
                for n, (si, step) in enumerate(((0, 2), (1, 4), (4, 14), (5, 16))):
                    if u == step:
                        dve.wait_ge(chunk_out, at(lay, CH1, SECTIONS[si] + 1))
                        v = stage[si % 2][:].rearrange("p t (h d) -> p t h d", d=HD)
                        x1, x2 = v[:, :, :, 0:8], v[:, :, :, 8:16]
                        for i, (x, col) in enumerate(((x1, K1_COS), (x2, K1_SIN), (x2, K1_COS), (x1, K1_SIN))):
                            a = nc.vector.tensor_tensor(rt[i][:], x, table(col), ALU.mult)
                        link(dve, a)
                        nc.vector.tensor_tensor(x1, rt[0][:], rt[1][:], ALU.subtract)
                        nc.vector.tensor_tensor(x2, rt[2][:], rt[3][:], ALU.add).then_inc(rope_done, 1)
                j = u - SB0 - 2
                if 0 <= j < NSB:
                    dve.wait_ge(cum_done, at(lay, NSB, j + 1))
                    if j > 0:
                        dve.wait_ge(sbw_done, at(lay, NSB, j))
                    nc.vector.tensor_tensor(sag[:], wk[j % 2][:, 0:384], drop, ALU.add).then_inc(arg_done, 1)
                j = u - SB0 - 1
                if 0 <= j < NSB:
                    bank = wk[j % 2]
                    dve.wait_ge(z_done, at(lay, NSB, j + 1))
                    link(dve, nc.vector.tensor_scalar(smx[:], bank[:, 0:384], 0.0, None, ALU.max))
                    nc.vector.scalar_tensor_tensor(saz[:], smx[:], -2.0, bank[:, 0:384], ALU.mult, ALU.add).then_inc(abs_done, 1)
                    dve.wait_ge(ln_done, at(lay, NSB, j + 1))
                    link(dve, nc.vector.tensor_tensor(saz[:], smx[:], sex[:], ALU.add))
                    if j > 0:
                        dve.wait_ge(cum_done, at(lay, NSB, j))
                    nc.vector.scalar_tensor_tensor(slk[:], saz[:], -1.0, keep, ALU.mult, ALU.mult).then_inc(keep_done, 1)
                h = u - DIFF0 - 1
                if 0 <= h < NDI:
                    if h > 0:
                        dve.wait_ge(exp_done, at(lay, NDI + NMO, h))
                    for m in range(2):
                        dve.wait_ge(score_done, at(lay, 2 * NDI + NMO, 2 * h + m + 1))
                        nc.vector.tensor_tensor(smk[m][:], wk[m][:, 0:384], causal, ALU.add).then_inc(mask_done, 1)
                    dve.wait_ge(mask_done, at(lay, 2 * NDI + NMO, 2 * h + 2))
                    for m in range(2):
                        nc.vector.tensor_reduce(nmx[:, 2 * m:2 * m + 1], smk[m][:, 0:P], AX.X, ALU.max, negate=True)
                        a = nc.vector.tensor_reduce(nmx[:, 2 * m + 1:2 * m + 2], smk[m][:, P:384], AX.X, ALU.max, negate=True)
                    a.then_inc(max_done, 1)
                    dve.wait_ge(exp_done, at(lay, NDI + NMO, h + 1))
                    link(dve, nc.vector.reciprocal(rsum[:], lsum[:]))
                    link(dve, nc.vector.tensor_scalar(rsl[:], rsum[:, 2:4], lam[:], None, ALU.mult))
                    if h > 0:
                        dve.wait_ge(wT_done, at(lay, NDI + NMO, h))
                    for tt, seg in enumerate((slice(0, P), slice(P, 384))):
                        a = nc.vector.tensor_scalar(wdf[:, seg], ex[1][:, seg], rsl[:, tt:tt + 1], None, ALU.mult)
                    link(dve, a)
                    for tt, seg in enumerate((slice(0, P), slice(P, 384))):
                        a = nc.vector.scalar_tensor_tensor(wdf[:, seg], ex[0][:, seg], rsum[:, tt:tt + 1], wdf[:, seg], ALU.mult, ALU.subtract)
                    a.then_inc(wdf_done, 1)
                j = u - MOBA0 - 1
                if 0 <= j < NMO:
                    m = j % 2
                    dve.wait_ge(score_done, at(lay, 2 * NDI + NMO, 2 * NDI + j + 1))
                    if j >= 2:
                        dve.wait_ge(exp_done, at(lay, NDI + NMO, NDI + j - 1))
                    nc.vector.tensor_tensor(smk[m][:], wk[m][:, 0:384], causal, ALU.add).then_inc(mask_done, 1)
                    dve.wait_ge(mask_done, at(lay, 2 * NDI + NMO, 2 * NDI + j + 1))
                    nc.vector.tensor_reduce(nmx[:, 2 * m:2 * m + 1], smk[m][:, 0:P], AX.X, ALU.max, negate=True)
                    nc.vector.tensor_reduce(nmx[:, 2 * m + 1:2 * m + 2], smk[m][:, P:384], AX.X, ALU.max, negate=True).then_inc(max_done, 1)
                for step, g in ((MOBA0 + 6, 0), (MOBA0 + 10, 1)):
                    if u == step:
                        hs = slice(4 * g, 4 * g + 4)
                        dve.wait_ge(pv_done, at(lay, NPV, NDI + NSB + 4 * g + 4))
                        link(dve, nc.vector.reciprocal(rmo[:, :, hs], lmo[:, :, hs]))
                        for tt in range(TT):
                            a = nc.vector.tensor_tensor(onat[2][:, tt, :].rearrange("p (h d) -> p h d", d=HD)[:, hs],
                                                        wk[3][:].rearrange("p (h t d) -> p h t d", h=4, t=TT)[:, :, tt, :],
                                                        rmo[:, tt, hs].unsqueeze(2).broadcast_to((P, 4, HD)), ALU.mult)
                        a.then_inc(o_out, 1)
                if u == 12:
                    dve.wait_ge(osq_done, at(lay, 1, 1))
                    link(dve, nc.vector.tensor_reduce(ssd[:], osq[:].rearrange("p t (h d) -> p (t h) d", d=P), AX.X, ALU.add))
                    nc.vector.tensor_scalar(msd[:], ssd[:], 1.0 / P, EPS, ALU.mult, ALU.add).then_inc(od_ms, 1)
                if u == 13:
                    dve.wait_ge(od_pow, at(lay, 1, 1))
                    o = onat[0][:].rearrange("p t (h d) -> p (t h) d", d=P)
                    nc.vector.tensor_tensor(o, o, rsd[:].unsqueeze(2).broadcast_to((P, 8, P)), ALU.mult).then_inc(od_done, 1)
                for step, b, i, bank in ((14, 0, 0, 2), (15, 0, 1, 2), (29, 1, 0, 0), (29, 1, 1, 1), (31, 2, 0, 0), (31, 2, 1, 1)):
                    if u == step:
                        dve.wait_ge(oTh_done, at(lay, 6, 2 * b + i + 1))
                        nc.vector.scalar_tensor_tensor(oTl[b][:, 2 * i:2 * i + 2, :], wk[bank][:].rearrange("p (k n) -> p k n", k=2),
                                                       gdiff[:] if b == 0 else 1.0, oTh[b][:, 2 * i:2 * i + 2, :].bitcast(F32),
                                                       ALU.mult, ALU.subtract).then_inc(oTl_done, 1)
                k = u - PROJ1 - 1
                if 0 <= k < 6:
                    _, b, half = BRANCH[k]
                    c = CH1 + k
                    unit1_done(dve, lay, PROJ1 + k)
                    dve.wait_ge(sig_done, at(lay, 6, k + 1))
                    dst = mrg[:, :, halves(half)] if b == 0 else mtm[:]
                    if k == 4:
                        dve.wait_ge(merged, at(lay, 2, 1))
                    for tt in range(TT):
                        a = nc.vector.tensor_tensor(dst[:, tt, :], acc[c % 2][tt][:], gate1[b][:, tt, halves(half)], ALU.mult)
                    a.then_inc(proj_out, 1)
                    if b > 0:
                        dve.wait_ge(proj_out, at(lay, 6, k + 1))
                        a = nc.vector.tensor_tensor(mrg[:, :, halves(half)], mrg[:, :, halves(half)], mtm[:], ALU.add)
                        if b == 2:
                            a.then_inc(merged, 1)
                        else:
                            link(dve, a)
                if u in (35, 37):
                    half = (u - 35) // 2
                    for i in range(2):
                        kt = 4 * half + 2 * i
                        dve.wait_ge(mTh_done, at(lay, 4, 2 * half + i + 1))
                        nc.vector.tensor_tensor(xl[:, kt:kt + 2, :], wk[2 * half + i][:].rearrange("p (k n) -> p k n", k=2),
                                                xh[:, kt:kt + 2, :].bitcast(F32), ALU.subtract).then_inc(mTl_done, 1)

        def mix1_pool(pool, lay):
            norm_pool(pool, lay, 1)
            for u in range(MIX1):
                if slot_of(u + 2) == POOLS:
                    split_low(pool, nc.gpsimd, 1, POOLS, lay, mix_use(u + 2))
                if u == 12:
                    pool.wait_ge(o_out, at(lay, 6, 2))
                    nc.gpsimd.tensor_tensor(osq[:], onat[0][:], onat[0][:], ALU.mult).then_inc(osq_done, 1)
                    pool.wait_ge(od_ms, at(lay, 1, 1))
                    nc.gpsimd.tensor_tensor(rsd[:], msd[:], neghalf[:, 0:8], ALU.pow).then_inc(od_pow, 1)

        NHG = 2 * LEVELS
        HG0, AQ0, ATT0 = 9, 24, 36
        EARLY = ((2, 0), (4, 1), (6, 2), (8, 3))
        NSEC = 4 + 6

        def at2(lay, per_layer, k):
            return lay * per_layer + (k - LAYERS * per_layer)

        def unit2_done(eng, lay, u):
            eng.wait_ge(slot_used[slot_of(u)], use(2, slot_of(u), lay, mix_use(u) + 1))

        def mix2_sp(sp, lay):
            for u in range(MIX2):
                s = slot_of(u)
                if u < PROJ2:
                    weights, row, col = t["w_in2"], lay * D + ((u % 2) * 512 - LAYERS * D), slice(CHUNKS2[u // 2], CHUNKS2[u // 2] + 512)
                elif u < PROJ2 + 4:
                    half, kh = divmod(u - PROJ2, 2)
                    weights, row, col = t["w_a"], lay * D + (kh * 512 - LAYERS * D), halves(half)
                elif u < PROJ2 + 6:
                    weights, row, col = t["w_b"], lay * 512 - LAYERS * 512, halves(u - PROJ2 - 4)
                else:
                    kh, half = divmod(u - PROJ2 - 6, 2)
                    weights, row, col = t["w_out2"], lay * D + (kh * 512 - LAYERS * D), halves(half)
                sp.wait_ge(low_done[s], use(2, s, lay, mix_use(u)))
                load_unit(sp, s, weights, row, col)

        def mix2_pe(pe, lay):
            lead_in(pe, 2, lay, 1, (0, 1), lambda s: FSTEPS)
            for u in range(2, MIX2 - 2):
                s = slot_of(u)
                if u < PROJ2:
                    c, half = divmod(u, 2)
                    if half == 0 and c >= 2:
                        pe.wait_ge(chunk_out2, at2(lay, CH2, c - 1))
                    lhs = [(xh[:, 4 * half + k, :], xl[:, 4 * half + k, :]) for k in range(4)]
                    out, first, last = acc[c % 2], half == 0, half == 1
                elif u < PROJ2 + 4:
                    half, kh = divmod(u - PROJ2, 2)
                    if kh == 0:
                        pe.wait_ge(chunk_out2, at2(lay, CH2, CH2 - 1 + half))
                    pe.wait_ge(oaTl_done, at2(lay, 8, 4 * kh + 4))
                    lhs = [(oaTh[:, 4 * kh + k, :], oaTl[:, 4 * kh + k, :]) for k in range(4)]
                    out, first, last = acc[(CH2 + half) % 2], kh == 0, kh == 1
                elif u < PROJ2 + 6:
                    half = u - PROJ2 - 4
                    pe.wait_ge(proj_out2, at2(lay, 4, half + 1))
                    pe.wait_ge(obTl_done, at2(lay, 2, 2))
                    lhs = [(obTh[:, k, :], obTl[:, k, :]) for k in range(4)]
                    out, first, last = acc[(CH2 + half) % 2], True, True
                else:
                    half = u - PROJ2 - 6
                    pe.wait_ge(proj_out2, at2(lay, 4, 3 + half))
                    pe.wait_ge(mTl_done2, at2(lay, 4, 2))
                    lhs = [(xh[:, k, :], xl[:, k, :]) for k in range(4)]
                    out, first, last = [YMIX[tt][half] for tt in range(TT)], True, False
                pe.wait_ge(low_done[s], use(2, s, lay, mix_use(u) + 1))
                for k in range(4):
                    mm = product(pe, [[o] for o in out], lhs[k][0], lhs[k][1], s, k * 512, 512, first and k == 0, last and k == 3)
                mm.then_inc(slot_used[s], 1)
                mix2_tail(pe, lay, u)
            pe.wait_ge(mTl_done2, at2(lay, 4, 4))
            mixer_end(pe, 2, lay, MIX2)

        def mix2_tail(pe, lay, u):
            for hf, step, b0 in ((0, HG0 + LEVELS, 2), (1, HG0 + NHG, 0)):
                if u == step:
                    pe.wait_ge(lev_out, at2(lay, NHG, LEVELS * (hf + 1)))
                    pe.wait_ge(chunk_out2, at2(lay, CH2, 5 + hf))
                    if hf == 0:
                        pe.wait_ge(f_done, at2(lay, 2, 2))
                    for h in range(4):
                        o = wk[b0 + h // 2][:, (h % 2) * SEQ:(h % 2 + 1) * SEQ]
                        v = hv[:, :, (4 * hf + h) * P:(4 * hf + h + 1) * P]
                        pe.matmul(o[:, 0:P], att[:, h, 0, :], v[:, 0, :], start=True, stop=True)
                        pe.matmul(o[:, P:SEQ], att[:, h, 2, :], v[:, 0, :], start=True, stop=False)
                        mm = pe.matmul(o[:, P:SEQ], att[:, h, 1, :], v[:, 1, :], start=False, stop=True)
                    mm.then_inc(pvh_done, 1)
            n = u - HG0
            if 0 <= n < NHG:
                hf, lev = divmod(n, LEVELS)
                if n == 0:
                    pe.wait_ge(hq_out, at2(lay, 2, 2))
                else:
                    pe.wait_ge(lev_out, at2(lay, NHG, n))
                if lev == 0:
                    pe.wait_ge(k_done, at2(lay, 2, hf + 1))
                else:
                    pe.wait_ge(A_done, at2(lay, 2 * (LEVELS - 1), (LEVELS - 1) * hf + lev))
                for h in range(4):
                    hd = 4 * hf + h
                    if lev == LEVELS - 1:
                        mm = pe.matmul(wk[0][:, h * P:(h + 1) * P], Av[:, h, 0:P], Av[:, h, P:SEQ], start=True, stop=True)
                        continue
                    for tl in range(TT):
                        cs = slice(tl * P, (tl + 1) * P)
                        k, q = (kT[:, hd, cs], qT[:, hd, cs]) if lev == 0 else (Av[:, h, cs], Av[:, h, cs])
                        mm = pe.matmul(wk[h // 2][:, (h % 2) * SEQ + tl * P:(h % 2) * SEQ + (tl + 1) * P], k, q, start=True, stop=True)
                mm.then_inc(lev_done, 1)
            if u in (29, 30):
                i0 = u - 29
                pe.wait_ge(oa_done, at2(lay, 2, i0 + 1))
                if i0 == 0:
                    pe.wait_ge(oh_out, at2(lay, 2, 2))
                else:
                    pe.wait_ge(oaTl_done, at2(lay, 8, 4))
                for i in range(2):
                    turn_tokens(pe, wk[i], hgt, 4 * i0 + 2 * i).then_inc(oaT_done, 1)
            hd, odd = divmod(u - ATT0 - 2, 2)
            if odd == 0 and 0 <= hd < ATT_HEADS:
                pe.wait_ge(wTa_out, at2(lay, ATT_HEADS, hd + 1))
                if hd == 0:
                    pe.wait_ge(sec_out2, at2(lay, 6, 6))
                if hd == 2:
                    pe.wait_ge(ob_out, at2(lay, 2, 1))
                o = wk[3][:, (hd % 2) * SEQ:(hd % 2 + 1) * SEQ]
                for g in range(ATT_GROUPS):
                    pe.matmul(o[:, 0:P], wTa[:, g, 0:P], av[:, g, 0, hd * P:(hd + 1) * P], start=g == 0, stop=g == ATT_GROUPS - 1)
                for g in range(ATT_GROUPS):
                    pe.matmul(o[:, P:SEQ], wTa[:, g, P:2 * P], av[:, g, 0, hd * P:(hd + 1) * P], start=g == 0, stop=False)
                    mm = pe.matmul(o[:, P:SEQ], wTa[:, g, 2 * P:384], av[:, g, 1, hd * P:(hd + 1) * P], start=False, stop=g == ATT_GROUPS - 1)
                mm.then_inc(dpv_done, 1)
            hd, odd = divmod(u - ATT0 - 1, 2)
            if odd == 0 and 0 <= hd < ATT_HEADS:
                pe.wait_ge(dexp_done, at2(lay, ATT_HEADS, hd + 1))
                for g in range(ATT_GROUPS):
                    for b in range(3):
                        tr = pe.transpose(wk[g][:, b * P:(b + 1) * P], exa[:, g, b * P:(b + 1) * P], ident)
                tr.then_inc(dT_done, 1)
            for step, s in EARLY:
                if u == step:
                    pe.wait_ge(chunk_out2, at2(lay, CH2, s + 1))
                    if s == 2:
                        pe.wait_ge(hq_out, at2(lay, 2, 1))
                    if s == 3:
                        pe.wait_ge(f_done, at2(lay, 2, 1))
                    for i in range(2):
                        tr = turn_tokens(pe, wk[2 * (s % 2) + i], stg[s % 2], 2 * i)
                    tr.then_inc(sec_T2, 1)
            a, odd = divmod(u - AQ0 - 1, 2)
            if odd == 0 and 0 <= a < 6:
                pe.wait_ge(rope_done2, at2(lay, 6, a + 1))
                if a == 0:
                    pe.wait_ge(oh_out, at2(lay, 2, 1))
                else:
                    pe.wait_ge(sec_out2, at2(lay, 6, a))
                for i in range(2):
                    tr = turn_tokens(pe, wk[2 + i], stg[a % 2], 2 * i)
                tr.then_inc(sec_T2, 1)
            if u == 45:
                pe.wait_ge(ob_out, at2(lay, 2, 2))
                pe.wait_ge(wTa_out, at2(lay, ATT_HEADS, ATT_HEADS))
                for i in range(2):
                    turn_tokens(pe, wk[i], ob, 2 * i).then_inc(obT_done, 1)
            if u in (47, 48):
                half = u - 47
                pe.wait_ge(merged2, at2(lay, 2, half + 1))
                if half == 0:
                    pe.wait_ge(obTl_done, at2(lay, 2, 2))
                for i in range(2):
                    turn_tokens(pe, wk[2 * half + i], mrg2, 4 * half + 2 * i).then_inc(mT_done2, 1)
            hd, odd = divmod(u - ATT0, 2)
            if odd == 0 and 0 <= hd < ATT_HEADS:
                if hd == 0:
                    pe.wait_ge(sec_out2, at2(lay, 6, 6))
                    pe.wait_ge(oaTl_done, at2(lay, 8, 8))
                else:
                    pe.wait_ge(wTa_out, at2(lay, ATT_HEADS, hd))
                for g in range(ATT_GROUPS):
                    q, k = aqT[:, 4 * g + hd, :], akT[:, 4 * g + hd, :]
                    pe.matmul(wk[g][:, 0:P], q[:, 0:P], k[:, 0:P], start=True, stop=True)
                    pe.matmul(wk[g][:, P:384], q[:, P:SEQ], k[:, 0:SEQ], start=True, stop=True).then_inc(dsc_done, 1)

        def mix2_act(act, lay):
            norm_act(act, lay, 1)
            act.wait_ge(lbw, at2(lay, 1, 1))
            nc.scalar.activation(lbe[:], lbe[:], ACT.Exp).then_inc(lbx, 1)
            act.wait_ge(rstd_done, at(lay, 3, 2))
            for u in range(MIX2 + 1):
                if u < MIX2:
                    split_high(act, 2, slot_of(u + 2), lay, mix_use(u + 2))
                c = u // 2 - 1
                if u % 2 == 0 and 0 <= c < CH2:
                    unit2_done(act, lay, u - 1)
                    func = ACT.Copy
                    if c < 4:
                        func, dst = (ACT.Silu, ACT.Sigmoid)[c % 2], stg[c % 2]
                        if c >= 2:
                            act.wait_ge(sec_T2, at2(lay, NSEC, c - 1))
                    elif c < 8:
                        dst = (hv, hgt)[(c - 4) // 2][:, :, halves(c % 2)]
                    elif c < 11:
                        dst = av[:, c - 8]
                    elif c < 17:
                        act.wait_ge(sec_T2, at2(lay, NSEC, 4 + c - 11 - 1))
                        dst = stg[(c - 11) % 2]
                    else:
                        dst = gate2[(c - 17) // 2][:, :, halves((c - 17) % 2)]
                    for tt in range(TT):
                        a = nc.scalar.activation(dst[:, tt, :], acc[c % 2][tt][:], func, scale=rstd[:, tt:tt + 1])
                    a.then_inc(chunk_out2, 1)
                for hf, step in ((0, 3), (1, 7)):
                    if u == step:
                        act.wait_ge(sec_T2, at2(lay, NSEC, 2 * hf + 1))
                        for i in range(2):
                            a = nc.scalar.activation(qT[:, 4 * hf + 2 * i:4 * hf + 2 * i + 2, :], wk[i][:].rearrange("p (k n) -> p k n", k=2), ACT.Copy)
                        a.then_inc(hq_out, 1)
                for hf, step in ((0, 5), (1, 9)):
                    if u == step:
                        act.preload_act_table_set(EXP_LN)
                        act.wait_ge(k_done, at2(lay, 2, hf + 1))
                        g = gc[:, 4 * hf:4 * hf + 4, :]
                        nc.scalar.activation(g, g, ACT.Ln).then_inc(lnf_done, 1)
                n = u - HG0
                if 0 <= n < NHG and n % LEVELS:
                    hf, lev = divmod(n, LEVELS)
                    i = (LEVELS - 1) * hf + lev
                    if lev < LEVELS - 1:
                        L = 1 << (lev - 1)
                        d = dl[:].rearrange("p h (b l) -> p (h b) l", l=2 * L)
                        act.wait_ge(diff_ready, at2(lay, 2 * (LEVELS - 2), (LEVELS - 2) * hf + lev))
                        nc.scalar.activation(d[:, :, L:2 * L], d[:, :, L:2 * L], ACT.Exp)
                        nc.scalar.activation(d[:, :, 0:L], d[:, :, 0:L], ACT.Exp, scale=-1.0).then_inc(dec_done, 1)
                    else:
                        act.wait_ge(A_done, at2(lay, 2 * (LEVELS - 1), i - 1))
                        for h in range(4):
                            hd = 4 * hf + h
                            nc.scalar.activation(dl[:, h, 0:P], gc[:, hd, 0:P], ACT.Exp, bias=gc[:, hd, P - 1:P], scale=-1.0)
                        nc.scalar.activation(dl[:, :, P:SEQ], gc[:, 4 * hf:4 * hf + 4, P:SEQ], ACT.Exp).then_inc(dec_done, 1)
                if u == 28:
                    act.wait_ge(chunk_out2, at2(lay, CH2, 8))
                    nc.scalar.activation(hgt[:], hgt[:], ACT.Silu).then_inc(hgs_done, 1)
                a, odd = divmod(u - AQ0, 2)
                if odd == 0 and 0 <= a < 6:
                    act.wait_ge(chunk_out2, at2(lay, CH2, 12 + a))
                    if a > 0:
                        act.wait_ge(rope_done2, at2(lay, 6, a))
                    nc.scalar.activation(rsq[:], stg[a % 2][:], ACT.Square).then_inc(asq_done, 1)
                a, odd = divmod(u - AQ0 - 2, 2)
                if odd == 0 and 0 <= a < 6:
                    act.wait_ge(sec_T2, at2(lay, NSEC, 4 + a + 1))
                    for i in range(2):
                        r = nc.scalar.activation((aqT, akT)[a // 3][:, 4 * (a % 3) + 2 * i:4 * (a % 3) + 2 * i + 2, :],
                                                 wk[2 + i][:].rearrange("p (k n) -> p k n", k=2), ACT.Copy)
                    r.then_inc(sec_out2, 1)
                if u in (30, 31):
                    for kt in range(4 * (u - 30), 4 * (u - 30) + 4):
                        if kt % 2 == 0:
                            act.wait_ge(oaT_done, at2(lay, 4, kt // 2 + 1))
                        nc.scalar.activation(oaTh[:, kt, :], wk[kt // 2 % 2][:, (kt % 2) * SEQ:(kt % 2 + 1) * SEQ], ACT.Copy,
                                             scale=cols[:, C2_OUT + kt:C2_OUT + kt + 1]).then_inc(oaTh_done, 1)
                hd, odd = divmod(u - ATT0 - 2, 2)
                if odd == 0 and 0 <= hd < ATT_HEADS:
                    act.wait_ge(dT_done, at2(lay, ATT_HEADS, hd + 1))
                    if hd > 0:
                        act.wait_ge(dpv_done, at2(lay, ATT_HEADS, hd))
                    for g in range(ATT_GROUPS):
                        a = nc.scalar.activation(wTa[:, g, :], wk[g][:, 0:384], ACT.Copy)
                    a.then_inc(wTa_out, 1)
                hd, odd = divmod(u - ATT0 - 1, 2)
                if odd == 0 and 0 <= hd < ATT_HEADS:
                    act.wait_ge(dmax_done, at2(lay, ATT_HEADS, hd + 1))
                    if hd > 0:
                        act.wait_ge(dT_done, at2(lay, ATT_HEADS, hd))
                    for tt, seg in enumerate((slice(0, P), slice(P, 384))):
                        a = nc.scalar.activation(exa[:, :, seg], sma[:, :, seg], ACT.Exp, bias=nma[:, tt:tt + 1], accum_out=lat[:, hd, tt:tt + 1])
                    a.then_inc(dexp_done, 1)
                k = u - 44
                if 0 <= k < 4:
                    if k == 0:
                        act.wait_ge(chunk_out2, at2(lay, CH2, CH2))
                    g = gate2[k // 2][:, :, halves(k % 2)]
                    nc.scalar.activation(g, g, ACT.Sigmoid).then_inc(sig_done2, 1)
                if u == 46:
                    for i in range(2):
                        act.wait_ge(obT_done, at2(lay, 2, i + 1))
                        nc.scalar.activation(obTh[:, 2 * i:2 * i + 2, :], wk[i][:].rearrange("p (k n) -> p k n", k=2), ACT.Copy).then_inc(obTh_done, 1)
                if u in (48, 49):
                    half = u - 48
                    for i in range(2):
                        act.wait_ge(mT_done2, at2(lay, 4, 2 * half + i + 1))
                        nc.scalar.activation(xh[:, 4 * half + 2 * i:4 * half + 2 * i + 2, :],
                                             wk[2 * half + i][:].rearrange("p (k n) -> p k n", k=2), ACT.Copy).then_inc(mTh_done2, 1)

        def mix2_dve(dve, lay):
            def per_head(x, n):
                return x.unsqueeze(2).broadcast_to((P, n, P))

            for tt in range(TT):
                norm_dve(dve, lay, 1, tt)
            dve.wait_ge(kblk_in, at(lay, 16, 16))
            l2 = cols[:, C2_LB:C2_LB + 2 * HG_HEADS].rearrange("p (l h) -> p l h", l=2)
            link(dve, nc.vector.tensor_tensor(lbm[:], l2[:, 0, :], l2[:, 1, :], ALU.max))
            nc.vector.tensor_tensor(lbe[:], l2, lbm[:].unsqueeze(1).broadcast_to((P, 2, HG_HEADS)), ALU.subtract).then_inc(lbw, 1)
            for u in range(MIX2 + 1):
                if u < MIX2 and slot_of(u + 2) != POOLS:
                    split_low(dve, nc.vector, 2, slot_of(u + 2), lay, mix_use(u + 2))
                if u == 1:
                    dve.wait_ge(lbx, at2(lay, 1, 1))
                    link(dve, nc.vector.tensor_tensor(lbs[:], lbe[:, 0, :], lbe[:, 1, :], ALU.add))
                    link(dve, nc.vector.reciprocal(lbm[:], lbs[:]))
                    link(dve, nc.vector.tensor_tensor(lbe[:], lbe[:], lbm[:].unsqueeze(1).broadcast_to((P, 2, HG_HEADS)), ALU.mult))
                    link(dve, nc.vector.tensor_tensor(lbs[:], lbe[:, 0, :], lbe[:, 1, :], ALU.add))
                    link(dve, nc.vector.tensor_tensor(lbs[:], lbs[:], lbe[:, 0, :], ALU.subtract))
                    link(dve, nc.vector.tensor_scalar(lb[:], lbs[:], cols[:, C2_LAYER:C2_LAYER + 1], None, ALU.mult))
                    link(dve, nc.vector.tensor_scalar(omlb[:], lb[:], -1.0, 1.0, ALU.mult, ALU.add))
                for hf, step in ((0, 5), (1, 9)):
                    if u == step:
                        dve.wait_ge(sec_T2, at2(lay, NSEC, 2 * hf + 2))
                        for h in range(4):
                            hd = 4 * hf + h
                            a = nc.vector.tensor_scalar(gc[:, hd, :], wk[2 + h // 2][:, (h % 2) * SEQ:(h % 2 + 1) * SEQ],
                                                        omlb[:, hd:hd + 1], lb[:, hd:hd + 1], ALU.mult, ALU.add)
                        a.then_inc(f_done, 1)
                        dve.wait_ge(f_done, at2(lay, 2, hf + 1))
                        hs = slice(4 * hf, 4 * hf + 4)
                        nc.vector.tensor_scalar(kT[:, hs, :], gc[:, hs, :], -1.0, 1.0, ALU.mult, ALU.add).then_inc(k_done, 1)
                        dve.wait_ge(lnf_done, at2(lay, 2, hf + 1))
                        for h in range(4):
                            for tl in range(TT):
                                g = gc[:, 4 * hf + h, tl * P:(tl + 1) * P]
                                a = nc.vector.tensor_tensor_scan(g, ones, g, 0.0, ALU.mult, ALU.add)
                        a.then_inc(g_done, 1)
                n = u - HG0
                if 0 <= n < NHG and n % LEVELS:
                    hf, lev = divmod(n, LEVELS)
                    L = 1 << (lev - 1)
                    dve.wait_ge(dec_done, at2(lay, 2 * (LEVELS - 1), (LEVELS - 1) * hf + lev))
                    if lev == 1:
                        dve.wait_ge(hq_out, at2(lay, 2, hf + 1))
                    dve.wait_ge(lev_done, at2(lay, NHG, n))
                    view = [x.rearrange("p h (b l) -> p (h b) l", l=2 * L)
                            for x in (Av[:], dl[:], qT[:, 4 * hf:4 * hf + 4, :], kT[:, 4 * hf:4 * hf + 4, :])]
                    nc.vector.tensor_tensor(view[0][:, :, L:2 * L], view[1][:, :, L:2 * L], view[2][:, :, L:2 * L], ALU.mult)
                    nc.vector.tensor_tensor(view[0][:, :, 0:L], view[1][:, :, 0:L], view[3][:, :, 0:L], ALU.mult).then_inc(A_done, 1)
                n = u - HG0 - 1
                if 0 <= n < NHG:
                    hf, lev = divmod(n, LEVELS)
                    if lev == LEVELS - 1:
                        dve.wait_ge(lev_done, at2(lay, NHG, n + 1))
                    if lev == LEVELS - 1:
                        a = nc.vector.tensor_copy(att[:, :, 2, :], wk[0][:].rearrange("p (h s) -> p h s", h=4))
                    else:
                        mask = kblk[:, K2_LEV + lev * P:K2_LEV + (lev + 1) * P].unsqueeze(1).broadcast_to((P, 2, P))
                        if n == LEVELS:
                            dve.wait_ge(pvh_done, at2(lay, 2, 1))
                        for h in range(4):
                            src = wk[h // 2][:, (h % 2) * SEQ:(h % 2 + 1) * SEQ].rearrange("p (t s) -> p t s", t=TT)
                            if lev == 0:
                                a = nc.vector.tensor_tensor(att[:, h, 0:2, :], src, mask, ALU.mult)
                            else:
                                a = nc.vector.copy_predicated(att[:, h, 0:2, :], mask.bitcast(U32), src)
                    a.then_inc(lev_out, 1)
                for hf, step, b0 in ((0, HG0 + LEVELS + 1, 2), (1, HG0 + NHG + 1, 0)):
                    if u == step:
                        o = osb[hf][:].rearrange("p h t d -> p (h t d)")
                        dve.wait_ge(pvh_done, at2(lay, 2, hf + 1))
                        for i in range(2):
                            a = nc.vector.tensor_copy(o[:, i * 512:(i + 1) * 512], wk[b0 + i][:])
                        a.then_inc(oh_out, 1)
                        dve.wait_ge(oh_sq, at2(lay, 2, hf + 1))
                        link(dve, nc.vector.tensor_reduce(sso[:], oq[hf][:].rearrange("p h t d -> p (h t) d"), AX.X, ALU.add))
                        nc.vector.tensor_scalar(mso[:], sso[:], 1.0 / P, EPS, ALU.mult, ALU.add).then_inc(oh_ms, 1)
                        dve.wait_ge(oh_pow, at2(lay, 2, hf + 1))
                        for tt in range(TT):
                            a = nc.vector.tensor_tensor(hv[:, tt, halves(hf)].rearrange("p (h d) -> p h d", d=P), osb[hf][:, :, tt, :],
                                                        per_head(rso[:].rearrange("p (h t) -> p h t", t=TT)[:, :, tt], 4), ALU.mult)
                        link(dve, a)
                if u == HG0 + NHG + 1:
                    dve.wait_ge(hgs_done, at2(lay, 1, 1))
                    for hf in range(2):
                        g = hgt[:, :, halves(hf)]
                        nc.vector.tensor_tensor(g, g, hv[:, :, halves(hf)], ALU.mult).then_inc(oa_done, 1)
                if u in (30, 31):
                    for kt in range(4 * (u - 30), 4 * (u - 30) + 4):
                        dve.wait_ge(oaTh_done, at2(lay, 8, kt + 2 - kt % 2))
                        nc.vector.scalar_tensor_tensor(oaTl[:, kt, :], wk[kt // 2 % 2][:, (kt % 2) * SEQ:(kt % 2 + 1) * SEQ],
                                                       cols[:, C2_OUT + kt:C2_OUT + kt + 1], oaTh[:, kt, :].bitcast(F32),
                                                       ALU.mult, ALU.subtract).then_inc(oaTl_done, 1)
                a, odd = divmod(u - AQ0, 2)
                if odd == 0 and 0 <= a < 6:
                    x = stg[a % 2][:].rearrange("p t (h d) -> p t h d", d=DH)
                    x8 = stg[a % 2][:].rearrange("p t (h d) -> p (t h) d", d=DH)
                    r8 = rtm[:].rearrange("p t (h d) -> p t h d", d=DH)
                    dve.wait_ge(asq_done, at2(lay, 6, a + 1))
                    link(dve, nc.vector.tensor_reduce(ssa[:], rsq[:].rearrange("p t (h d) -> p (t h) d", d=DH), AX.X, ALU.add))
                    nc.vector.tensor_scalar(msa[:], ssa[:], 1.0 / DH, EPS, ALU.mult, ALU.add).then_inc(ams_done, 1)
                    dve.wait_ge(apow_done, at2(lay, 6, a + 1))
                    link(dve, nc.vector.tensor_tensor(x8, x8, per_head(rsa[:], 8), ALU.mult))
                    gain = cols[:, C2_QK + a * DH:C2_QK + (a + 1) * DH]
                    link(dve, nc.vector.tensor_tensor(x8, x8, gain.unsqueeze(1).broadcast_to((P, 8, DH)), ALU.mult))
                    H = DH // 2
                    for tt in range(TT):
                        sin = kblk[:, K2_SIN + tt * DH:K2_SIN + (tt + 1) * DH].unsqueeze(1).broadcast_to((P, ATT_HEADS, DH))
                        nc.vector.tensor_tensor(r8[:, tt, :, 0:H], x[:, tt, :, H:DH], sin[:, :, 0:H], ALU.mult)
                        nc.vector.tensor_tensor(r8[:, tt, :, H:DH], x[:, tt, :, 0:H], sin[:, :, H:DH], ALU.mult)
                    for tt in range(TT):
                        cos = kblk[:, K2_COS + tt * DH:K2_COS + (tt + 1) * DH].unsqueeze(1).broadcast_to((P, ATT_HEADS, DH))
                        r = nc.vector.tensor_tensor(rsq[:, tt, :].rearrange("p (h d) -> p h d", d=DH), x[:, tt, :, :], cos, ALU.mult)
                    link(dve, r)
                    nc.vector.tensor_tensor(stg[a % 2][:], rsq[:], rtm[:], ALU.add).then_inc(rope_done2, 1)
                for step, p in ((ATT0 + 5, 0), (ATT0 + 9, 1)):
                    if u == step:
                        hs = slice(2 * p, 2 * p + 2)
                        dve.wait_ge(dpv_done, at2(lay, ATT_HEADS, 2 * p + 2))
                        link(dve, nc.vector.reciprocal(rat[:, hs, :], lat[:, hs, :]))
                        for tt in range(TT):
                            r = nc.vector.tensor_tensor(ob[:, tt, :].rearrange("p (h d) -> p h d", d=DH)[:, hs],
                                                        wk[3][:].rearrange("p (h t d) -> p h t d", h=2, t=TT)[:, :, tt, :],
                                                        per_head(rat[:, hs, tt], 2), ALU.mult)
                        r.then_inc(ob_out, 1)
                hd, odd = divmod(u - ATT0 - 1, 2)
                if odd == 0 and 0 <= hd < ATT_HEADS:
                    if hd > 0:
                        dve.wait_ge(dexp_done, at2(lay, ATT_HEADS, hd))
                    for g in range(ATT_GROUPS):
                        dve.wait_ge(dsc_done, at2(lay, 3 * ATT_HEADS, 3 * hd + g + 1))
                        a = nc.vector.scalar_tensor_tensor(sma[:, g, :], wk[g][:, 0:384], DH ** -0.5,
                                                           kblk[:, K2_MASK + 384 * g:K2_MASK + 384 * (g + 1)], ALU.mult, ALU.add)
                    link(dve, a)
                    nc.vector.tensor_reduce(nma[:, 0:1], sma[:, :, 0:P], AX.XY, ALU.max, negate=True)
                    nc.vector.tensor_reduce(nma[:, 1:2], sma[:, :, P:384], AX.XY, ALU.max, negate=True).then_inc(dmax_done, 1)
                for k, (step, b, half, unit) in enumerate(((44, 0, 0, 43), (46, 0, 1, 45), (47, 1, 0, 46), (48, 1, 1, 47))):
                    if u == step:
                        unit2_done(dve, lay, unit)
                        dve.wait_ge(sig_done2, at2(lay, 4, k + 1))
                        dst = mrg2[:, :, halves(half)] if b == 0 else mtm2[:]
                        if k == 3:
                            dve.wait_ge(merged2, at2(lay, 2, 1))
                        for tt in range(TT):
                            a = nc.vector.tensor_tensor(dst[:, tt, :], acc[(CH2 + half) % 2][tt][:], gate2[b][:, tt, halves(half)], ALU.mult)
                        a.then_inc(proj_out2, 1)
                        if b == 1:
                            dve.wait_ge(proj_out2, at2(lay, 4, k + 1))
                            m = mrg2[:, :, halves(half)]
                            nc.vector.tensor_tensor(m, m, mtm2[:], ALU.add).then_inc(merged2, 1)
                if u == 46:
                    for i in range(2):
                        dve.wait_ge(obTh_done, at2(lay, 2, i + 1))
                        nc.vector.tensor_tensor(obTl[:, 2 * i:2 * i + 2, :], wk[i][:].rearrange("p (k n) -> p k n", k=2),
                                                obTh[:, 2 * i:2 * i + 2, :].bitcast(F32), ALU.subtract).then_inc(obTl_done, 1)
                if u in (48, 49):
                    half = u - 48
                    for i in range(2):
                        kt = 4 * half + 2 * i
                        dve.wait_ge(mTh_done2, at2(lay, 4, 2 * half + i + 1))
                        nc.vector.tensor_tensor(xl[:, kt:kt + 2, :], wk[2 * half + i][:].rearrange("p (k n) -> p k n", k=2),
                                                xh[:, kt:kt + 2, :].bitcast(F32), ALU.subtract).then_inc(mTl_done2, 1)

        def mix2_pool(pool, lay):
            norm_pool(pool, lay, 1)
            for u in range(MIX2):
                if slot_of(u + 2) == POOLS:
                    split_low(pool, nc.gpsimd, 2, POOLS, lay, mix_use(u + 2))
                n = u - HG0
                if 0 <= n < NHG and 0 < n % LEVELS < LEVELS - 1:
                    hf, lev = divmod(n, LEVELS)
                    L = 1 << (lev - 1)
                    g = gc[:, 4 * hf:4 * hf + 4, :].rearrange("p h (b l) -> p (h b) l", l=2 * L)
                    if lev == 1:
                        pool.wait_ge(g_done, at2(lay, 2, hf + 1))
                    if (LEVELS - 1) * hf + lev > 1:
                        pool.wait_ge(A_done, at2(lay, 2 * (LEVELS - 1), (LEVELS - 1) * hf + lev - 1))
                    nc.gpsimd.tensor_tensor(dl[:].rearrange("p h (b l) -> p (h b) l", l=2 * L), g,
                                            g[:, :, L - 1:L].broadcast_to((P, 4 * SEQ // (2 * L), 2 * L)), ALU.subtract).then_inc(diff_ready, 1)
                for hf, step in ((0, HG0 + LEVELS + 1), (1, HG0 + NHG + 1)):
                    if u == step:
                        pool.wait_ge(oh_out, at2(lay, 2, hf + 1))
                        nc.gpsimd.tensor_tensor(oq[hf][:], osb[hf][:], osb[hf][:], ALU.mult).then_inc(oh_sq, 1)
                        pool.wait_ge(oh_ms, at2(lay, 2, hf + 1))
                        nc.gpsimd.tensor_tensor(rso[:], mso[:], neghalf[:, 0:8], ALU.pow).then_inc(oh_pow, 1)
                a, odd = divmod(u - AQ0, 2)
                if odd == 0 and 0 <= a < 6:
                    pool.wait_ge(ams_done, at2(lay, 6, a + 1))
                    nc.gpsimd.tensor_tensor(rsa[:], msa[:], neghalf[:, 0:8], ALU.pow).then_inc(apow_done, 1)

        t_mix = {1: dict(sp=mix1_sp, pe=mix1_pe, act=mix1_act, dve=mix1_dve, pool=mix1_pool),
                 2: dict(sp=mix2_sp, pe=mix2_pe, act=mix2_act, dve=mix2_dve, pool=mix2_pool)}


        block = ctx.enter_context(nc.Block())

        @block.sync
        def _(sp):
            sp.dma_start(X[:], t["x"].rearrange("(t p) d -> p t d", p=P)).then_inc(x_in, 16)
            sp.dma_start(konst[:], t["konst"]).then_inc(konst_in, 16)
            sp.dma_start(gain0[:], t["gain0"][0:P, :]).then_inc(gain0_in, 16)
            for blk in (1, 2):
                with sp.Fori((blk - 1) * LAYERS, blk * LAYERS) as lay:
                    l = lay if blk == 1 else lay - LAYERS
                    ffn_sp(sp, blk, lay, 0)
                    sp.wait_ge(x_ready, at(lay, 6, LOADED))
                    sp.dma_start(cols[:, 0:(NC1, NC2)[blk - 1]], t["cols"][blk][bass.ds(l * P, P), :]).then_inc(cols_in, 16)
                    sp.dma_start(kblk[:, 0:(NK1, NK2)[blk - 1]], t["kblk"][blk]).then_inc(kblk_in, 16)
                    post_sp(sp, blk, lay, 0)
                    t_mix[blk]["sp"](sp, lay)
                    sp.wait_ge(x_ready, at(lay, 6, LOADED + 2))
                    sp.dma_start(gain0[:], t["gain0"][bass.ds(lay * P + P, P), :]).then_inc(gain0_in, 16)
                    post_sp(sp, blk, lay, 1)
                    ffn_sp(sp, blk, lay, 1)
                    if blk == 1:
                        sp.wait_ge(x_ready, at(lay, 6, LOADED + 4))
                    post_sp(sp, blk, lay, 2)
            for s in AHEAD:
                sp.wait_ge(low_done[s], use(2, s, 2 * LAYERS, 0))
                sp.sem_inc(raw_in[s], 32)
            sp.wait_ge(x_ready, LOADED + 6 * 2 * LAYERS)
            sp.dma_start(t["out"].rearrange("(t p) d -> p t d", p=P), X[:]).then_inc(out_sent, 16)
            sp.wait_ge(out_sent, 16)

        @block.tensor
        def _(pe):
            for s in range(SLOTS):
                pe.sem_inc(slot_used[s], FREE)
            for blk in (1, 2):
                with pe.Fori((blk - 1) * LAYERS, blk * LAYERS) as lay:
                    ffn_pe(pe, blk, lay, 0)
                    t_mix[blk]["pe"](pe, lay)
                    ffn_pe(pe, blk, lay, 1)

        @block.scalar
        def _(act):
            for s in AHEAD:
                split_high(act, 1, s, 0, 0)
            for blk in (1, 2):
                with act.Fori((blk - 1) * LAYERS, blk * LAYERS) as lay:
                    ffn_act(act, blk, lay, 0)
                    post_act(act, blk, lay, 0)
                    t_mix[blk]["act"](act, lay)
                    post_act(act, blk, lay, 1)
                    ffn_act(act, blk, lay, 1)
                    post_act(act, blk, lay, 2)

        @block.vector
        def _(dve):
            for s in (0, 1):
                dve.sem_inc(low_done[s], FREE)
            dve.sem_inc(x_ready, LOADED)
            split_low(dve, nc.vector, 1, 0, 0, 0)
            for blk in (1, 2):
                with dve.Fori((blk - 1) * LAYERS, blk * LAYERS) as lay:
                    per = LINKS[blk]
                    chain.update(n=0, lay=lay, per=per, off=0 if blk == 1 else LAYERS * (LINKS[1] - LINKS[2]))
                    ffn_dve(dve, blk, lay, 0)
                    post_dve(dve, blk, lay, 0)
                    t_mix[blk]["dve"](dve, lay)
                    post_dve(dve, blk, lay, 1)
                    ffn_dve(dve, blk, lay, 1)
                    post_dve(dve, blk, lay, 2)
                links[blk] = chain["n"]

        @block.gpsimd
        def _(pool):
            nc.gpsimd.memset(neghalf[:], -0.5).then_inc(const_set, 1)
            pool.sem_inc(low_done[POOLS], FREE)
            pool.wait_ge(const_set, 1)
            split_low(pool, nc.gpsimd, 1, POOLS, 0, 0)
            for blk in (1, 2):
                with pool.Fori((blk - 1) * LAYERS, blk * LAYERS) as lay:
                    ffn_pool(pool, blk, lay, 0)
                    post_pool(pool, blk, lay, 0)
                    t_mix[blk]["pool"](pool, lay)
                    post_pool(pool, blk, lay, 1)
                    ffn_pool(pool, blk, lay, 1)
                    post_pool(pool, blk, lay, 2)
        assert links == LINKS, links


def constants():
    i = np.arange(P)
    konst = np.concatenate([np.eye(P), np.ones((P, P)), i[:, None] >= i[None, :]], 1).astype(np.float32)

    def logit_blocks(ok):
        return np.concatenate([ok[0:P, 0:P], ok[P:SEQ, 0:SEQ]], 1)

    tok = np.arange(SEQ)
    gap = tok[:, None] - tok[None, :]
    causal = np.where(logit_blocks(gap >= 0), 0.0, NEG)
    before = (gap > 0).T
    keep = np.concatenate([before[0:P, :], before[P:SEQ, P:SEQ]], 1)

    def angles(theta, width):
        inv = (np.float32(theta) ** (-np.arange(0, width, 2, dtype=np.float32) / np.float32(width))).astype(np.float32)
        a = (tok.astype(np.float32)[:, None] * inv[None, :]).astype(np.float32)
        return np.cos(a), np.sin(a)

    def by_tile(a):
        return a.reshape(TT, P, -1).transpose(1, 0, 2).reshape(P, -1)

    c1, s1 = angles(500000.0, ROT)
    kb1 = np.concatenate([causal, keep, np.where(keep, 0.0, NEG), by_tile(c1), by_tile(s1)], 1).astype(np.float32)
    c2, s2 = angles(10000.0, DH)
    masks = [np.where(logit_blocks((gap >= 0) & (gap <= w) & (gap % d == 0)), 0.0, NEG) for w, d in PATTERNS]
    levels = [np.eye(P)]
    for n in range(7):
        L = 1 << n
        same = i[:, None] // (2 * L) == i[None, :] // (2 * L)
        levels.append(same & (i[:, None] % (2 * L) < L) & (i[None, :] % (2 * L) >= L))
    kb2 = np.concatenate([by_tile(np.concatenate([c2, c2], 1)), by_tile(np.concatenate([-s2, s2], 1))] + masks + levels, 1).astype(np.float32)
    assert konst.shape[1] == NK0 and kb1.shape[1] == NK1 and kb2.shape[1] == NK2
    return konst, kb1, kb2


WEIGHTS = ["w_in", "w_diff_o", "w_sb_o", "w_moba_o", "w_out", "ffn1_wg", "ffn1_wu", "ffn1_wd", "ffn2_wg", "ffn2_wu", "ffn2_wd",
           "ffn1_w_in_2", "ffn1_w_out_2", "w_in_2", "w_branch_a_2", "w_branch_b_2", "w_out_2", "ffn2_w_in_2", "ffn2_w_out_2"]


def laid_out(inputs):
    arrays = {n: np.ascontiguousarray(inputs[n]) for n in WEIGHTS}
    arrays["x"] = np.ascontiguousarray(inputs["x"]).reshape(SEQ, D)

    def column(a):
        return np.asarray(a).reshape(-1, P).T

    def repeated(a):
        return np.tile(np.asarray(a).reshape(1, -1), (P, 1))

    def const(v):
        return np.full((P, 1), v, np.float32)

    one, two = [], []
    for l in range(LAYERS):
        start = 0.8 - 0.6 * math.exp(-0.3 * l)
        one.append(np.concatenate([column(inputs[n][l]) for n in ("g_ffn1_pre", "g_mix_pre", "g_ffn2_pre", "diff_norm_g")]
                                  + [const(start), const(1.0 - start)]
                                  + [repeated(inputs[n][l]) for n in ("lam_q1", "lam_k1", "lam_q2", "lam_k2")], 1))
        two.append(np.concatenate([column(inputs[n][l]) for n in ("ffn1_norm_2", "mix_norm_2", "ffn2_norm_2", "hgrn_out_norm_2")]
                                  + [column(inputs["hgrn_lb_logits_2"][m]) for m in range(LAYERS)]
                                  + [const(float(l))]
                                  + [repeated(inputs[n][l]) for n in ("attn_q_norm_2", "attn_k_norm_2")], 1))
    first = [inputs["g_ffn1_pre"][l] for l in range(LAYERS)] + [inputs["ffn1_norm_2"][l] for l in range(LAYERS)]
    arrays["gain0"] = np.ascontiguousarray(np.concatenate([column(g) for g in first + first[-1:]], 0))
    arrays["post"] = np.ascontiguousarray(np.concatenate([inputs[n][l:l + 1] for l in range(LAYERS) for n in ("g_ffn1_post", "g_mix_post", "g_ffn2_post")], 0))
    arrays["cols1"] = np.ascontiguousarray(np.concatenate(one, 0))
    arrays["cols2"] = np.ascontiguousarray(np.concatenate(two, 0))
    arrays["konst"], arrays["kblk1"], arrays["kblk2"] = constants()
    return arrays


def program(nc, shapes):
    dram = {n: nc.dram_tensor(f"in_{n}", s, F32, kind="ExternalInput").ap() for n, s in shapes.items()}
    out = nc.dram_tensor("out_x", (SEQ, D), F32, kind="ExternalOutput").ap()
    rows = {n: dram[n].rearrange("l k n -> (l k) n") for n in WEIGHTS }
    build(nc, {
        "x": dram["x"], "out": out, "konst": dram["konst"], "gain0": dram["gain0"], "kblk": {1: dram["kblk1"], 2: dram["kblk2"]},
        "cols": {1: dram["cols1"], 2: dram["cols2"]},
        "post": dram["post"],
        "ffn": {1: [(rows["ffn1_wg"], rows["ffn1_wu"], rows["ffn1_wd"], 0), (rows["ffn2_wg"], rows["ffn2_wu"], rows["ffn2_wd"], 0)],
                2: [(rows["ffn1_w_in_2"], rows["ffn1_w_in_2"], rows["ffn1_w_out_2"], FFN),
                    (rows["ffn2_w_in_2"], rows["ffn2_w_in_2"], rows["ffn2_w_out_2"], FFN)]},
        "w_in": rows["w_in"], "w_o": [rows["w_diff_o"], rows["w_sb_o"], rows["w_moba_o"]], "w_out": rows["w_out"],
        "w_in2": rows["w_in_2"], "w_a": rows["w_branch_a_2"], "w_b": rows["w_branch_b_2"], "w_out2": rows["w_out_2"],
    })


def kernel(**inputs):
    import concourse.bacc as _bacc
    from concourse.bass_utils import run_bass_kernel_spmd as _run

    arrays = laid_out(inputs)
    nc = _bacc.Bacc("TRN2", target_bir_lowering=False, num_devices=1)
    program(nc, {n: a.shape for n, a in arrays.items()})
    r = _run(nc, [{f"in_{n}": a for n, a in arrays.items()}], core_ids=[0])
    return r.results[0]["out_x"].reshape(1, SEQ, D)
```

```python
import math
from contextlib import ExitStack

import numpy as np
import concourse.bass as bass
from concourse import mybir

F32 = mybir.dt.float32
F32R = mybir.dt.float32r
U32 = mybir.dt.uint32
ALU = mybir.AluOpType
ACT = mybir.ActivationFunctionType
AX = mybir.AxisListType

P = 128
SEQ = 256
TT = SEQ // P
D = 1024
KT = D // P
LAYERS = 2
EPS = 1e-6
NEG = -1e30
FFN = 2816
FC = 256
FSTEPS = FFN // FC
UNIT = 2048
SLOTS = 3
FREE = 1
LOADED = 2 * TT
EXP_LN = "natural_log_exp_and_others"

HD = 64
ROT = HD // 4
DIFF_HEADS, SB_HEADS, MOBA_HEADS = 4, 8, 8
IN1 = 9 * 512 + 3 * D
CH1 = IN1 // 512
Q_DIFF, K_DIFF, V_DIFF, Q_SB, K_SB, V_SB, Q_MOBA, K_MOBA, V_MOBA = range(9)
PROJ1 = 2 * CH1
MIX1 = PROJ1 + 6 + 4

HG_HEADS = 8
ATT_GROUPS, ATT_HEADS, DH = 3, 4, 128
PATTERNS = ((128, 1), (512, 4), (2048, 16))
IN2 = 4 * D + 3 * 1536 + 2 * D
HQ, HF, HI, HG, AQ, AK, AV, GA, GB = 0, D, 2 * D, 3 * D, 4 * D, 4 * D + 1536, 4 * D + 3072, 4 * D + 4608, 5 * D + 4608
CHUNKS2 = [HQ, HF, HQ + 512, HF + 512, HI, HI + 512, HG, HG + 512, AV, AV + 512,
           AQ, AQ + 512, AQ + 1024, AK, AK + 512, AK + 1024, AV + 1024, GA, GA + 512, GB, GB + 512]
AV_CHUNKS = {8: 0, 9: 1, 16: 2}
AQ_CHUNK = 10
CH2 = len(CHUNKS2)
PROJ2 = 2 * CH2
MIX2 = PROJ2 + 4 + 2 + 4
LEVELS = 9

C_G = {0: 0, 1: KT, 2: 2 * KT}
C1_DIFF, C1_LAM0, C1_LAM1, C1_LQK = 24, 25, 26, 27
NC1 = C1_LQK + 4 * HD
C2_OUT, C2_LB, C2_LAYER, C2_QK = 24, 32, 48, 49
NC2 = C2_QK + 2 * ATT_GROUPS * DH
NCOL = max(NC1, NC2)
K_ID, K_ONES, K_TRI = 0, P, 2 * P
NK0 = 3 * P
K1_CAUSAL, K1_KEEP, K1_DROP, K1_COS, K1_SIN = 0, 384, 768, 1152, 1152 + TT * 8
NK1 = K1_SIN + TT * 8
K2_COS, K2_SIN, K2_MASK, K2_LEV = 0, TT * DH, 2 * TT * DH, 2 * TT * DH + 3 * 384
NK2 = K2_LEV + 8 * P
NKB = max(NK1 + D, NK2)


LEAD = (0, 1)
UP = (2, 0)
DN = 1
TURN = 2
POOLS = 2


def slot_of(u):
    return u % SLOTS if u <= TURN else (u + 1) % SLOTS if u == TURN + 1 else (u - 1) % SLOTS


def slot_uses(units, slot):
    return sum(slot_of(u) == slot for u in range(units))


U1 = [2 * FSTEPS + slot_uses(MIX1, s) for s in range(SLOTS)]
U2 = [2 * FSTEPS + slot_uses(MIX2, s) for s in range(SLOTS)]


def at(lay, per_layer, k):
    return lay * per_layer + k


def use(blk, slot, lay, k):
    if blk == 1:
        return lay * U1[slot] + (FREE + k)
    return lay * U2[slot] + (FREE + LAYERS * (U1[slot] - U2[slot]) + k)


def ffn_use(blk, f, slot):
    return 0 if f == 0 else FSTEPS + slot_uses(MIX1 if blk == 1 else MIX2, slot)


def mix_use(u):
    return FSTEPS + slot_uses(u, slot_of(u))


LINKS = {1: 46, 2: 32}


def build(nc, t):
    ctx = ExitStack()
    with ctx:
        def sb(name, shape, dt=F32):
            return ctx.enter_context(nc.sbuf_tensor(name, shape, dt))

        def sem(name):
            return ctx.enter_context(nc.semaphore(name))

        raw = [sb(f"raw{s}", [P, UNIT]) for s in range(SLOTS)]
        wh = [sb(f"w_high{s}", [P, UNIT], F32R) for s in range(SLOTS)]
        wl = [sb(f"w_low{s}", [P, UNIT], F32R) for s in range(SLOTS)]
        X = sb("x_res", [P, TT, D])
        xh = sb("xT_high", [P, KT, SEQ], F32R)
        xl = sb("xT_low", [P, KT, SEQ], F32R)
        konst = sb("konst", [P, NK0])
        kblk = sb("kblk", [P, NKB])
        cols = sb("cols", [P, NCOL])
        gain0 = sb("gain0", [P, KT])
        grow = kblk[:, NK1:NK1 + D]
        neghalf = sb("neghalf", [P, 16])
        ss = sb("ss", [P, TT]); ms = sb("ms", [P, TT]); rstd = sb("rstd", [P, TT])
        ssy = sb("ssy", [P, TT, 2]); msy = sb("msy", [P, TT]); rsy = sb("rsy", [P, TT])
        lamp = sb("lam_prod", [P, 2, HD]); lams = sb("lam_sum", [P, 2]); lame = sb("lam_exp", [P, 2])
        lam = sb("lam", [P, 1]); gdiff = sb("gain_diff", [P, 1])
        nmx = sb("neg_max", [P, 4]); lsum = sb("exp_sum", [P, 4]); rsum = sb("inv_sum", [P, 4])
        rsl = sb("inv_sum_lam", [P, 2])
        rmo = sb("inv_moba", [P, TT, MOBA_HEADS]); lmo = sb("sum_moba", [P, TT, MOBA_HEADS])
        ssd = sb("ss_diff", [P, 8]); msd = sb("ms_diff", [P, 8]); rsd = sb("rstd_diff", [P, 8])
        lbe = sb("lb_exp", [P, 2, HG_HEADS]); lbm = sb("lb_max", [P, HG_HEADS]); lbs = sb("lb_sum", [P, HG_HEADS])
        lb = sb("lb", [P, HG_HEADS]); omlb = sb("one_minus_lb", [P, HG_HEADS])
        sso = sb("ss_o", [P, 8]); mso = sb("ms_o", [P, 8]); rso = sb("rstd_o", [P, 8])
        ssa = sb("ss_a", [P, 8]); msa = sb("ms_a", [P, 8]); rsa = sb("rstd_a", [P, 8])
        rat = sb("inv_att", [P, ATT_HEADS, TT]); lat = sb("sum_att", [P, ATT_HEADS, TT]); nma = sb("neg_max_att", [P, TT])

        ARENA = 94 * 1024
        arena = sb("arena", [P, ARENA // 4])
        base = nc.sbuf_base - ARENA

        def over(name, shape, kib, dt=F32):
            size = 4 * int(np.prod(shape[1:]))
            assert kib * 1024 + size <= ARENA, name
            return nc.alloc_sbuf_tensor_at(name, shape, dt, offset=int(base + kib * 1024))

        hTh = over("hT_high", [P, 2, SEQ], 0, F32R)
        hTl = over("hT_low", [P, 2, SEQ], 2, F32R)
        sil = over("silu", [P, TT, FC], 4)
        hid = over("hidden", [P, TT, FC], 6)
        tpost = over("post", [P, TT, D], 8)
        junk = over("squares", [P, TT, D], 16)
        hTh_last = over("hT_high_last", [P, 2, SEQ], 24, F32R)
        hTl_last = over("hT_low_last", [P, 2, SEQ], 26, F32R)

        vnat = [over(f"v{b}", [P, TT, 512], 4 * b) for b in range(3)]
        gate1 = [over(f"gate{b}", [P, TT, D], 12 + 8 * b) for b in range(3)]
        stage = [over(f"stage{i}", [P, TT, 512], 36 + 4 * i) for i in range(2)]
        secT = {Q_DIFF: over("dqT", [P, 4, SEQ], 44), K_DIFF: over("dkT", [P, 4, SEQ], 48),
                Q_SB: over("sqT", [P, 4, SEQ], 52), K_SB: over("skT", [P, 4, SEQ], 56),
                Q_MOBA: over("mqT", [P, 4, SEQ], 44), K_MOBA: over("mkT", [P, 4, SEQ], 48)}
        oTh = [over(f"oT_high{b}", [P, 4, SEQ], k, F32R) for b, k in enumerate((60, 52, 0))]
        oTl = [over(f"oT_low{b}", [P, 4, SEQ], k, F32R) for b, k in enumerate((64, 56, 4))]
        onat = [over("o_diff", [P, TT, 512], 68), over("o_sb", [P, TT, 512], 72), over("o_moba", [P, TT, 512], 68)]
        smk = [over(f"masked{m}", [P, 384], 76 + 1.5 * m) for m in range(2)]
        ex = [over(f"expd{m}", [P, 384], 79 + 1.5 * m) for m in range(2)]
        osq = over("o_sq", [P, TT, 512], 76)
        wdf = over("w_diff", [P, 384], 82)
        wT = [over(f"wT{i}", [P, 384], 83.5 + 1.5 * i) for i in range(2)]
        saz = over("sb_abs", [P, 384], 86.5)
        sex = over("sb_exp", [P, 384], 88)
        slk = over("sb_keep", [P, 384], 89.5)
        sag = over("sb_arg", [P, 384], 91)
        smx = over("sb_max", [P, 384], 92.5)
        rt = [over(f"rope_t{i}", [P, TT, 8, 8], 76 + 0.5 * i) for i in range(4)]
        mrg = over("merged1", [P, TT, D], 36)
        mtm = over("merge_term", [P, TT, 512], 76)

        qT = over("hqT", [P, HG_HEADS, SEQ], 0)
        kT = over("hkT", [P, HG_HEADS, SEQ], 8)
        gc = over("log_decay", [P, HG_HEADS, SEQ], 16)
        dl = over("decay", [P, 4, SEQ], 24)
        Av = over("decayed", [P, 4, SEQ], 28)
        att = over("hg_att", [P, 4, 3, P], 32)
        hv = over("hg_v", [P, TT, D], 38)
        hgt = over("hg_gate", [P, TT, D], 46)
        stg = [over(f"stage2_{i}", [P, TT, 512], 54 + 4 * i) for i in range(2)]
        aqT = over("aqT", [P, 12, SEQ], 62)
        rsq = over("rope_sq", [P, TT, 512], 74)
        rtm = over("rope_tm", [P, TT, 512], 78)
        av = over("a_v", [P, 3, TT, 512], 82)
        akT = over("akT", [P, 12, SEQ], 0)
        ob = over("o_b", [P, TT, 512], 12)
        oaTh = over("oaT_high", [P, KT, SEQ], 16, F32R)
        oaTl = over("oaT_low", [P, KT, SEQ], 24, F32R)
        gate2 = [over(f"gate2_{b}", [P, TT, D], 32 + 8 * b) for b in range(2)]
        sma = over("masked_att", [P, 3, 384], 48)
        wTa = over("wT_att", [P, 3, 384], 54)
        exa = over("exp_att", [P, 3, 384], 74)
        obTh = over("obT_high", [P, 4, SEQ], 62, F32R)
        obTl = over("obT_low", [P, 4, SEQ], 66, F32R)
        mrg2 = over("merged2", [P, TT, D], 0)
        mtm2 = over("merge_term2", [P, TT, 512], 74)
        oq = [over("o_sq0", [P, 8, P], 90), over("o_sq1", [P, 8, P], 24)]

        ps = [ctx.enter_context(nc.psum_tensor(f"bank{b}", [P, 512], F32)) for b in range(8)]
        acc = [[ps[0], ps[1]], [ps[2], ps[3]]]
        wk = ps[4:8]
        DOWN = [[ps[4], ps[5]], [ps[6], ps[7]]]
        YMIX = [[ps[2], ps[0]], [ps[3], ps[1]]]

        ident = konst[:, K_ID:K_ID + P]
        ones = konst[:, K_ONES:K_ONES + P]
        tri = konst[:, K_TRI:K_TRI + P]

        konst_in = sem("konst_in"); kblk_in = sem("kblk_in"); cols_in = sem("cols_in"); grow_in = sem("grow_in")
        out_sent = sem("out_sent"); const_set = sem("const_set")
        raw_in = [sem(f"raw_in{s}") for s in range(SLOTS)]
        high_done = [sem(f"high_done{s}") for s in range(SLOTS)]
        low_done = [sem(f"low_done{s}") for s in range(SLOTS)]
        slot_used = [sem(f"slot_used{s}") for s in range(SLOTS)]
        x_in = [sem(f"x_in{tt}") for tt in range(TT)]; post_done = sem("post_done"); x_ready = sem("x_ready"); y_half = sem("y_half"); gain0_in = sem("gain0_in"); xT_done = sem("xT_done"); xh_done = sem("xh_done"); xl_done = sem("xl_done")
        ss_done = sem("ss_done"); ms_done = sem("ms_done"); rstd_done = sem("rstd_done")
        silu_done = sem("silu_done"); hid_done = sem("hid_done")
        hT_done = sem("hT_done"); hTh_done = sem("hTh_done"); hTl_done = sem("hTl_done")
        ssy_done = sem("ssy_done"); msy_done = sem("msy_done"); rsy_done = sem("rsy_done")
        dve_link = sem("dve_link"); lam_sum = sem("lam_sum_done"); lam_exp = sem("lam_exp_done")
        chunk_out = sem("chunk_out")
        rope_done = sem("rope_done"); sec_T = sem("sec_T"); sec_out = sem("sec_out")
        score_done = sem("score_done"); mask_done = sem("mask_done"); max_done = sem("max_done"); exp_done = sem("exp_done")
        wdf_done = sem("wdf_done"); wT_done = sem("wT_done"); wT_out = sem("wT_out")
        z_done = sem("z_done"); abs_done = sem("abs_done"); sbe_done = sem("sbe_done"); ln_done = sem("ln_done")
        keep_done = sem("keep_done"); cum_done = sem("cum_done"); arg_done = sem("arg_done"); sbw_done = sem("sbw_done")
        pv_done = sem("pv_done"); o_out = sem("o_out")
        osq_done = sem("osq_done"); od_ms = sem("od_ms"); od_pow = sem("od_pow"); od_done = sem("od_done")
        oT_done = sem("oT_done"); oTh_done = sem("oTh_done"); oTl_done = sem("oTl_done")
        proj_out = sem("proj_out"); sig_done = sem("sig_done"); merged = sem("merged")
        mT_done = sem("mT_done"); mTh_done = sem("mTh_done"); mTl_done = sem("mTl_done")
        lbx = sem("lb_exp_done"); lbw = sem("lb_max_done")
        f_done = sem("f_done"); lnf_done = sem("lnf_done"); g_done = sem("g_done"); k_done = sem("k_done")
        diff_ready = sem("diff_ready"); dec_done = sem("dec_done"); A_done = sem("A_done")
        lev_done = sem("lev_done"); lev_out = sem("lev_out")
        pvh_done = sem("pvh_done"); oh_out = sem("oh_out"); oh_sq = sem("oh_sq"); oh_ms = sem("oh_ms"); oh_pow = sem("oh_pow")
        hgs_done = sem("hgs_done"); oa_done = sem("oa_done")
        asq_done = sem("asq_done"); ams_done = sem("ams_done"); apow_done = sem("apow_done")
        chunk_out2 = sem("chunk_out2"); dT_done = sem("dT_done"); dexp_done = sem("dexp_done"); dmax_done = sem("dmax_done"); dpv_done = sem("dpv_done")
        dsc_done = sem("dsc_done"); hq_out = sem("hq_out"); mT_done2 = sem("mT_done2"); mTh_done2 = sem("mTh_done2"); mTl_done2 = sem("mTl_done2")
        merged2 = sem("merged2"); oaT_done = sem("oaT_done"); oaTh_done = sem("oaTh_done"); oaTl_done = sem("oaTl_done"); obT_done = sem("obT_done")
        obTh_done = sem("obTh_done"); obTl_done = sem("obTl_done"); ob_out = sem("ob_out"); proj_out2 = sem("proj_out2"); rope_done2 = sem("rope_done2")
        sec_T2 = sem("sec_T2"); sec_out2 = sem("sec_out2"); sig_done2 = sem("sig_done2"); wTa_out = sem("wTa_out")
        links = {}

        def split_high(act, blk, slot, lay, k):
            act.wait_ge(raw_in[slot], use(blk, slot, lay, k + 1 - FREE) * 32)
            act.wait_ge(slot_used[slot], use(blk, slot, lay, k))
            nc.scalar.activation(wh[slot][:], raw[slot][:], ACT.Copy).then_inc(high_done[slot], 1)

        def split_low(eng, ops, blk, slot, lay, k):
            eng.wait_ge(high_done[slot], use(blk, slot, lay, k + 1 - FREE))
            ops.tensor_tensor(wl[slot][:], raw[slot][:], wh[slot][:].bitcast(F32), ALU.subtract).then_inc(low_done[slot], 1)

        def product(pe, outs, xhi, xlo, slot, col, n, start, stop, tiles=range(TT)):
            for tt in tiles:
                rows = slice(tt * P, (tt + 1) * P)
                for x, w, first, last in ((xhi, wh, True, False), (xhi, wl, False, False), (xlo, wh, False, True)):
                    for j, o in enumerate(outs[tt]):
                        mm = pe.matmul(o[:, 0:n], x[:, rows], w[slot][:, col + j * n:col + (j + 1) * n],
                                       start=start and first, stop=stop and last)
            return mm

        def gain(n, kt):
            return gain0[:, kt:kt + 1] if n in (0, 3) else cols[:, C_G[n] + kt:C_G[n] + kt + 1]

        def norm_pe(pe, lay, n, tt):
            pe.wait_ge(konst_in, 16)
            pe.wait_ge(x_in[tt], 16)
            for kt in range(KT):
                if kt % 4 == 0:
                    pe.wait_ge(x_ready, at(lay, 12, LOADED + 4 * (n - 1) + 2 * tt + kt // 4 + 1))
                tr = pe.transpose(wk[2 * tt + kt // 4][:, (kt % 4) * P:(kt % 4 + 1) * P], X[:, tt, kt * P:(kt + 1) * P], ident)
                if kt % 4 == 3:
                    tr.then_inc(xT_done, 1)

        def norm_act(act, lay, n, between):
            for tt in range(TT):
                if tt == 1:
                    between()
                for kt in range(KT):
                    if kt % 4 == 0:
                        act.wait_ge(xT_done, at(lay, 12, 4 * n + 2 * tt + kt // 4 + 1))
                    if tt == 0 and kt == 0 and n in (0, 3):
                        act.wait_ge(gain0_in, at(lay, 16, 16 if n == 0 else 32))
                    if tt == 0 and kt == 0 and n == 1:
                        act.wait_ge(cols_in, at(lay, 16, 16))
                    nc.scalar.activation(xh[:, kt, tt * P:(tt + 1) * P], wk[2 * tt + kt // 4][:, (kt % 4) * P:(kt % 4 + 1) * P],
                                         ACT.Copy, scale=gain(n, kt)).then_inc(xh_done, 1)
            for tt in range(TT):
                nc.scalar.activation(junk[:, tt, :], X[:, tt, :], ACT.Square, accum_out=ss[:, tt:tt + 1]).then_inc(ss_done, 1)

        def norm_dve(dve, lay, n, tt):
            for kt in range(KT):
                if kt % 4 == 0:
                    dve.wait_ge(xh_done, at(lay, 48, 16 * n + 8 * tt + kt + 4))
                nc.vector.scalar_tensor_tensor(xl[:, kt, tt * P:(tt + 1) * P], wk[2 * tt + kt // 4][:, (kt % 4) * P:(kt % 4 + 1) * P],
                                               gain(n, kt), xh[:, kt, tt * P:(tt + 1) * P].bitcast(F32),
                                               ALU.mult, ALU.subtract).then_inc(xl_done, 1)
            if tt == TT - 1:
                dve.wait_ge(ss_done, at(lay, 6, 2 * n + 2))
                nc.vector.tensor_scalar(ms[:], ss[:], 1.0 / D, EPS, ALU.mult, ALU.add).then_inc(ms_done, 1)

        def lead_in(pe, blk, lay, n, used, out):
            for tt in range(TT):
                for half, s in enumerate(LEAD):
                    if tt == 0:
                        pe.wait_ge(low_done[s], use(blk, s, lay, used(s) + 1))
                    for k in range(4):
                        kt = 4 * half + k
                        pe.wait_ge(xl_done, at(lay, 48, 16 * n + 8 * tt + kt + 1))
                        mm = product(pe, [[o] for o in out], xh[:, kt, :], xl[:, kt, :], s, k * 512, 512,
                                     kt == 0, kt == KT - 1, tiles=(tt,))
                        if tt == 0 and half == 1 and k == 1:
                            norm_pe(pe, lay, n, 1)
                    if tt == TT - 1:
                        mm.then_inc(slot_used[s], 1)

        def norm_pool(pool, lay, n):
            pool.wait_ge(ms_done, at(lay, 3, n + 1))
            nc.gpsimd.tensor_tensor(rstd[:], ms[:], neghalf[:, 0:TT], ALU.pow).then_inc(rstd_done, 1)

        def ffn_pe(pe, blk, lay, f):
            (sa, sb), sd = UP, DN
            b = [ffn_use(blk, f, s) for s in range(SLOTS)]

            def up(i, turn_between=None):
                for half, s, before in ((0, sa, b[sa] - 1), (1, sb, b[sb])):
                    pe.wait_ge(low_done[s], use(blk, s, lay, before + 1) + i)
                    for k in range(4):
                        kt = 4 * half + k
                        mm = product(pe, [[acc[0][tt]] for tt in range(TT)], xh[:, kt, :], xl[:, kt, :],
                                     s, k * 512, 512, kt == 0, kt == KT - 1)
                    mm.then_inc(slot_used[s], 1)
                    if half == 0 and turn_between is not None:
                        turn(turn_between)

            def down(i, k, slot, start, stop, tiles=range(TT)):
                pe.wait_ge(hTl_done, at(lay, 44, 2 * FSTEPS * f + k + 1) + i * 2)
                if k == 0:
                    before = b[sd] + 1 if slot == sd else b[sa]
                    pe.wait_ge(low_done[slot], use(blk, slot, lay, before + 1) + i)
                high, low = (hTh_last, hTl_last) if slot == sa else (hTh, hTl)
                return product(pe, DOWN, high[:, k, :], low[:, k, :], slot, k * D, 512, start and k == 0, stop and k == 1, tiles)

            def turn(i):
                pe.wait_ge(hid_done, at(lay, 22, FSTEPS * f + 1) + i)
                for k in range(2):
                    for tt in range(TT):
                        tr = pe.transpose(ps[2 + k][:, tt * P:(tt + 1) * P],
                                          hid[:, tt, k * P:(k + 1) * P], ident)
                tr.then_inc(hT_done, 1)

            lead_in(pe, blk, lay, 2 * f, lambda s: b[s], acc[1])
            up(1, turn_between=0)
            down(0, 0, sd, True, False)
            turn(1)
            down(0, 1, sd, True, False).then_inc(slot_used[sd], 1)
            with pe.Fori(2, FSTEPS - 1) as i:
                up(i)
                down(i - 1, 0, sd, False, False)
                turn(i)
                down(i - 1, 1, sd, False, False).then_inc(slot_used[sd], 1)
            last = FSTEPS - 1
            up(last)
            for k in range(2):
                down(last - 1, k, sd, False, False, tiles=(0,))
            turn(last)
            down(last - 1, 0, sd, False, False, tiles=(1,))
            for k in range(2):
                mm = down(last, k, sa, False, True, tiles=(0,))
            mm.then_inc(y_half, 1)
            down(last - 1, 1, sd, False, False, tiles=(1,)).then_inc(slot_used[sd], 1)
            down(last, 0, sa, False, True, tiles=(1,))
            norm_pe(pe, lay, 2 * f + 1, 0)
            down(last, 1, sa, False, True, tiles=(1,)).then_inc(slot_used[sa], 1)

        def ffn_act(act, blk, lay, f):
            (sa, sb), sd = UP, DN
            b = [ffn_use(blk, f, s) for s in range(SLOTS)]

            def silu(i):
                first = isinstance(i, int) and i == 0
                sums = acc[first]
                if first:
                    s = LEAD[1]
                    act.wait_ge(slot_used[s], use(blk, s, lay, b[s] + 1))
                else:
                    act.wait_ge(slot_used[sb], use(blk, sb, lay, b[sb] + 1) + i)
                for tt in range(TT):
                    a = nc.scalar.activation(sil[:, tt, :], sums[tt][:, 0:FC], ACT.Silu, scale=rstd[:, tt:tt + 1])
                a.then_inc(silu_done, 1)

            def turn_high(i, dst=hTh):
                act.wait_ge(hT_done, at(lay, 22, FSTEPS * f + 1) + i)
                for k in range(2):
                    if k == 1 and dst is hTh:
                        act.wait_ge(slot_used[sd], use(blk, sd, lay, b[sd] + 1) + i)
                    nc.scalar.activation(dst[:, k, :], ps[2 + k][:, 0:SEQ], ACT.Copy).then_inc(hTh_done, 1)

            act.preload_act_table(ACT.Silu)
            act.wait_ge(rstd_done, at(lay, 3, 2 * f + 1))
            silu(0)
            split_high(act, blk, sb, lay, b[sb] + 1)
            split_high(act, blk, sd, lay, b[sd] + 1)
            turn_high(0)
            with act.Fori(1, FSTEPS - 1) as i:
                split_high(act, blk, sa, lay, b[sa] + i)
                silu(i)
                split_high(act, blk, sb, lay, b[sb] + 1 + i)
                turn_high(i)
                split_high(act, blk, sd, lay, b[sd] + 1 + i)
            split_high(act, blk, sa, lay, b[sa] + FSTEPS - 1)
            silu(FSTEPS - 1)
            split_high(act, blk, sb, lay, b[sb] + FSTEPS)
            turn_high(FSTEPS - 1, hTh_last)

        def ffn_dve(dve, blk, lay, f):
            (sa, sb), sd = UP, DN
            b = [ffn_use(blk, f, s) for s in range(SLOTS)]

            def low(slot, k):
                if slot != POOLS:
                    split_low(dve, nc.vector, blk, slot, lay, b[slot] + k)

            def hidden(i):
                sums = acc[isinstance(i, int) and i == 0]
                dve.wait_ge(silu_done, at(lay, 22, FSTEPS * f + 1) + i)
                for tt in range(TT):
                    h = nc.vector.scalar_tensor_tensor(hid[:, tt, :], sums[tt][:, FC:2 * FC], rstd[:, tt:tt + 1],
                                                       sil[:, tt, :], ALU.mult, ALU.mult)
                h.then_inc(hid_done, 1)

            def turn_low(i, high=hTh, dst=hTl):
                for k in range(2):
                    dve.wait_ge(hTh_done, at(lay, 44, 2 * FSTEPS * f + k + 1) + i * 2)
                    nc.vector.tensor_tensor(dst[:, k, :], ps[2 + k][:, 0:SEQ], high[:, k, :].bitcast(F32),
                                            ALU.subtract).then_inc(hTl_done, 1)

            low(sa, 0)
            hidden(0)
            low(sb, 1)
            low(sd, 1)
            turn_low(0)
            with dve.Fori(1, FSTEPS - 1) as i:
                low(sa, i)
                hidden(i)
                low(sb, i + 1)
                turn_low(i)
                low(sd, i + 1)
            low(sa, FSTEPS - 1)
            hidden(FSTEPS - 1)
            turn_low(FSTEPS - 1, hTh_last, hTl_last)
            low(sb, FSTEPS)

        def ffn_pool(pool, blk, lay, f):
            split_low(pool, nc.gpsimd, blk, POOLS, lay, ffn_use(blk, f, POOLS))
            norm_pool(pool, lay, 2 * f)
            with pool.Fori(0, FSTEPS - 1) as i:
                split_low(pool, nc.gpsimd, blk, POOLS, lay, ffn_use(blk, f, POOLS) + 1 + i)

        def ffn_sp(sp, blk, lay, f):
            gate_w, up_w, down_w, up_col = t["ffn"][blk][f]
            (sa, sb), sd = UP, DN
            row = lay * D if blk == 1 else lay * D - LAYERS * D
            drow = lay * FFN if blk == 1 else lay * FFN - LAYERS * FFN

            def free(slot, k):
                sp.wait_ge(low_done[slot], use(blk, slot, lay, ffn_use(blk, f, slot)) + k)

            def up(col, slots, uses):
                for half, (s, k) in enumerate(zip(slots, uses)):
                    free(s, k)
                    dst = raw[s][:].rearrange("p (k g n) -> p k g n", k=4, g=2)
                    for g, (w, c0) in enumerate(((gate_w, 0), (up_w, up_col))):
                        sp.dma_start(dst[:, :, g, :], w[bass.ds(row + 4 * half * P, 4 * P), bass.ds(col + c0, FC)]
                                     .rearrange("(k p) n -> p k n", p=P)).then_inc(raw_in[s], 16)

            def down(i, s, k):
                free(s, k)
                for h in range(2):
                    sp.dma_start(raw[s][:, h * D:(h + 1) * D], down_w[bass.ds(drow + i * FC + h * P, P), :]).then_inc(raw_in[s], 16)

            up(0, LEAD, (0, 0))
            with sp.Fori(0, FSTEPS - 1) as i:
                up(i * FC + FC, UP, (i, i + 1))
                down(i, sd, i + 1)
            down(FSTEPS - 1, sa, FSTEPS - 1)

        def halves(k):
            return slice(k * 512, (k + 1) * 512)

        def y_wait(eng, blk, lay, f, tt):
            if tt == 0:
                eng.wait_ge(y_half, at(lay, 3, f + 1))
            elif f == 1:
                u = (MIX1 if blk == 1 else MIX2) - 1
                eng.wait_ge(slot_used[slot_of(u)], use(blk, slot_of(u), lay, mix_use(u) + 1))
            else:
                s = UP[0]
                eng.wait_ge(slot_used[s], use(blk, s, lay, ffn_use(blk, f // 2, s) + FSTEPS))

        def post_act(act, blk, lay, f, tt):
            Y = YMIX if f == 1 else DOWN
            if blk == 1:
                y_wait(act, blk, lay, f, tt)
                for j in range(2):
                    nc.scalar.activation(junk[:, tt, halves(j)], Y[tt][j][:], ACT.Square, accum_out=ssy[:, tt, j:j + 1]).then_inc(ssy_done, 1)

        def post_dve(dve, blk, lay, f, tt):
            Y = YMIX if f == 1 else DOWN
            weight = 1.0 if f == 1 else 0.5
            if blk == 2:
                y_wait(dve, blk, lay, f, tt)
                for j in range(2):
                    xs = X[:, tt, halves(j)]
                    nc.vector.scalar_tensor_tensor(xs, Y[tt][j][:], weight, xs, ALU.mult, ALU.add).then_inc(x_ready, 1)
                return
            if tt == 0:
                dve.wait_ge(grow_in, at(lay, 48, 16 * (f + 1)))
            for j in range(2):
                dve.wait_ge(ssy_done, at(lay, 12, 4 * f + 2 * tt + j + 1))
                if j == 1:
                    link(dve, nc.vector.tensor_tensor(msy[:, tt:tt + 1], ssy[:, tt, 0:1], ssy[:, tt, 1:2], ALU.add))
                    nc.vector.tensor_scalar(msy[:, tt:tt + 1], msy[:, tt:tt + 1], 1.0 / (D * weight ** 2), EPS / weight ** 2,
                                            ALU.mult, ALU.add).then_inc(msy_done, 1)
                nc.vector.tensor_tensor(tpost[:, tt, halves(j)], Y[tt][j][:], grow[:, halves(j)], ALU.mult).then_inc(post_done, 1)
            dve.wait_ge(rsy_done, at(lay, 6, 2 * f + tt + 1))
            for j in range(2):
                dve.wait_ge(post_done, at(lay, 12, 4 * f + 2 * tt + j + 1))
                xs = X[:, tt, halves(j)]
                nc.vector.scalar_tensor_tensor(xs, tpost[:, tt, halves(j)], rsy[:, tt:tt + 1], xs, ALU.mult, ALU.add).then_inc(x_ready, 1)

        def post_pool(pool, blk, lay, f, tt):
            if blk == 1:
                pool.wait_ge(msy_done, at(lay, 6, 2 * f + tt + 1))
                nc.gpsimd.tensor_tensor(rsy[:, tt:tt + 1], msy[:, tt:tt + 1], neghalf[:, 0:1], ALU.pow).then_inc(rsy_done, 1)

        def post_sp(sp, blk, lay, f):
            if blk == 1:
                sp.dma_start(grow, t["post"][bass.ds(lay * 3 + f, 1), :].broadcast_to((P, D))).then_inc(grow_in, 16)

        chain = {"n": 0, "lay": 0, "per": 0, "off": 0}

        def link(dve, ins):
            chain["n"] += 1
            ins.then_inc(dve_link, 1)
            dve.wait_ge(dve_link, chain["lay"] * chain["per"] + (chain["off"] + chain["n"]))

        SECTIONS = (Q_DIFF, K_DIFF, Q_SB, K_SB, Q_MOBA, K_MOBA)
        DIFF0, SB0, MOBA0 = 6, 12, 20
        V_CHUNKS = {V_DIFF: 0, V_SB: 1, V_MOBA: 2}
        BRANCH = [(u, (u - PROJ1) % 3, (u - PROJ1) // 3) for u in range(PROJ1, PROJ1 + 6)]
        NDI, NSB, NMO = DIFF_HEADS, SB_HEADS, MOBA_HEADS
        NPV = NDI + NSB + NMO

        def unit1_done(eng, lay, u):
            eng.wait_ge(slot_used[slot_of(u)], use(1, slot_of(u), lay, mix_use(u) + 1))

        def load_unit(sp, s, weights, row, col):
            for k in range(2):
                sp.dma_start(raw[s][:, k * D:(k + 1) * D].rearrange("p (k n) -> p k n", k=2),
                             weights[bass.ds(row + k * SEQ, SEQ), col].rearrange("(k p) n -> p k n", p=P)).then_inc(raw_in[s], 16)

        def mix1_sp(sp, lay):
            for u in range(MIX1):
                s = slot_of(u)
                if u < PROJ1:
                    weights, row, col = t["w_in"], lay * D + (u % 2) * 512, halves(u // 2)
                elif u < PROJ1 + 6:
                    _, b, half = BRANCH[u - PROJ1]
                    weights, row, col = t["w_o"][b], lay * 512, halves(half)
                else:
                    kh, half = divmod(u - PROJ1 - 6, 2)
                    weights, row, col = t["w_out"], lay * D + kh * 512, halves(half)
                sp.wait_ge(low_done[s], use(1, s, lay, mix_use(u)))
                load_unit(sp, s, weights, row, col)

        def scores1(pe, bank, q, k, lo, blk):
            rows = slice(lo, lo + HD)
            pe.matmul(bank[:, 0:P], q[rows, blk, 0:P], k[rows, blk, 0:P], start=True, stop=True)
            return pe.matmul(bank[:, P:384], q[rows, blk, P:SEQ], k[rows, blk, 0:SEQ], start=True, stop=True)

        def values(pe, out0, out1, w, v0, v1):
            pe.matmul(out0, w[:, 0:P], v0, start=True, stop=True)
            pe.matmul(out1, w[:, P:2 * P], v0, start=True, stop=False)
            return pe.matmul(out1, w[:, 2 * P:384], v1, start=False, stop=True)

        def turn_tokens(pe, bank, src, kt):
            for k in range(2):
                for tt in range(TT):
                    tr = pe.transpose(bank[:, k * SEQ + tt * P:k * SEQ + (tt + 1) * P], src[:, tt, (kt + k) * P:(kt + k + 1) * P], ident)
            return tr

        def mix1_pe(pe, lay):
            lead_in(pe, 1, lay, 1, lambda s: FSTEPS, acc[0])
            for u in range(2, MIX1 - 2):
                s = slot_of(u)
                if u < PROJ1:
                    c, half = divmod(u, 2)
                    if half == 0 and c >= 2:
                        pe.wait_ge(chunk_out, at(lay, CH1, c - 1))
                    lhs = [(xh[:, 4 * half + k, :], xl[:, 4 * half + k, :]) for k in range(4)]
                    out, first, last = acc[c % 2], half == 0, half == 1
                elif u < PROJ1 + 6:
                    _, b, half = BRANCH[u - PROJ1]
                    c = CH1 + u - PROJ1
                    if u < PROJ1 + 2:
                        pe.wait_ge(chunk_out, at(lay, CH1, c - 1))
                    else:
                        pe.wait_ge(proj_out, at(lay, 6, u - PROJ1 - 1))
                    pe.wait_ge(oTl_done, at(lay, 6, 2 * b + 2))
                    lhs = [(oTh[b][:, k, :], oTl[b][:, k, :]) for k in range(4)]
                    out, first, last = acc[c % 2], True, True
                else:
                    half = u - PROJ1 - 6
                    pe.wait_ge(proj_out, at(lay, 6, 5 + half))
                    pe.wait_ge(mTl_done, at(lay, 4, 2))
                    lhs = [(xh[:, k, :], xl[:, k, :]) for k in range(4)]
                    out, first, last = [YMIX[tt][half] for tt in range(TT)], True, False
                pe.wait_ge(low_done[s], use(1, s, lay, mix_use(u) + 1))
                for k in range(4):
                    mm = product(pe, [[o] for o in out], lhs[k][0], lhs[k][1], s, k * 512, 512, first and k == 0, last and k == 3)
                    if k == 1:
                        mix1_mid(pe, lay, u)
                mm.then_inc(slot_used[s], 1)
                mix1_tail(pe, lay, u)
            pe.wait_ge(mTl_done, at(lay, 4, 4))
            mixer_end(pe, 1, lay, MIX1)

        def mixer_end(pe, blk, lay, units):
            for tt in range(TT):
                for half in range(2):
                    u = units - 2 + half
                    s = slot_of(u)
                    if tt == 0:
                        pe.wait_ge(low_done[s], use(blk, s, lay, mix_use(u) + 1))
                    for k in range(4):
                        mm = product(pe, [[YMIX[t][half]] for t in range(TT)], xh[:, 4 + k, :], xl[:, 4 + k, :], s, k * 512, 512,
                                     False, k == 3, tiles=(tt,))
                        if tt == 1 and half == 1 and k == 1:
                            norm_pe(pe, lay, 2, 0)
                    if tt == TT - 1:
                        mm.then_inc(slot_used[s], 1)
                if tt == 0:
                    mm.then_inc(y_half, 1)

        def mix1_mid(pe, lay, u):
            if u in (34, 36):
                half = (u - 34) // 2
                pe.wait_ge(merged, at(lay, 2, half + 1))
                if half == 0:
                    pe.wait_ge(oTl_done, at(lay, 6, 6))
                else:
                    pe.wait_ge(wT_out, at(lay, NDI + NMO, NDI + NMO))
                    pe.wait_ge(o_out, at(lay, 6, 6))
                for i in range(2):
                    turn_tokens(pe, wk[2 * half + i], mrg, 4 * half + 2 * i).then_inc(mT_done, 1)

        def mix1_tail(pe, lay, u):
            h = u - DIFF0 - 2
            if 0 <= h < NDI:
                pe.wait_ge(wT_out, at(lay, NDI + NMO, h + 1))
                if h == 0:
                    pe.wait_ge(chunk_out, at(lay, CH1, V_DIFF + 1))
                if h == 2:
                    pe.wait_ge(o_out, at(lay, 6, 1))
                o = wk[3][:, (h % 2) * 256:(h % 2 + 1) * 256]
                v = vnat[0][:, :, h * P:(h + 1) * P]
                values(pe, o[:, 0:P], o[:, P:256], wT[h % 2], v[:, 0, :], v[:, 1, :]).then_inc(pv_done, 1)
            j = u - SB0 - 2
            if 0 <= j < NSB:
                pe.wait_ge(sbw_done, at(lay, NSB, j + 1))
                if j % 4 == 0:
                    pe.wait_ge(o_out, at(lay, 6, 2 + j // 4))
                if j == 0:
                    pe.wait_ge(chunk_out, at(lay, CH1, V_SB + 1))
                o = wk[3][:, (j % 4) * P:(j % 4 + 1) * P]
                v = vnat[1][:, :, j * HD:(j + 1) * HD]
                values(pe, o[:, 0:HD], o[:, HD:P], wT[j % 2], v[:, 0, :], v[:, 1, :]).then_inc(pv_done, 1)
            j = u - MOBA0 - 2
            if 0 <= j < NMO:
                pe.wait_ge(wT_out, at(lay, NDI + NMO, NDI + j + 1))
                if j % 4 == 0:
                    pe.wait_ge(o_out, at(lay, 6, 4 + j // 4))
                if j == 0:
                    pe.wait_ge(chunk_out, at(lay, CH1, V_MOBA + 1))
                o = wk[3][:, (j % 4) * P:(j % 4 + 1) * P]
                v = vnat[2][:, :, j * HD:(j + 1) * HD]
                values(pe, o[:, 0:HD], o[:, HD:P], wT[j % 2], v[:, 0, :], v[:, 1, :]).then_inc(pv_done, 1)
            h = u - DIFF0 - 1
            if 0 <= h < NDI:
                pe.wait_ge(wdf_done, at(lay, NDI, h + 1))
                if h > 0:
                    pe.wait_ge(wT_out, at(lay, NDI + NMO, h))
                for b in range(3):
                    tr = pe.transpose(wk[2][:, b * P:(b + 1) * P], wdf[:, b * P:(b + 1) * P], ident)
                tr.then_inc(wT_done, 1)
            j = u - MOBA0 - 1
            if 0 <= j < NMO:
                pe.wait_ge(exp_done, at(lay, NDI + NMO, NDI + j + 1))
                if j == 0:
                    pe.wait_ge(sec_out, at(lay, 12, 12))
                else:
                    pe.wait_ge(wT_out, at(lay, NDI + NMO, NDI + j))
                for b in range(3):
                    tr = pe.transpose(wk[2][:, b * P:(b + 1) * P], ex[j % 2][:, b * P:(b + 1) * P], ident)
                tr.then_inc(wT_done, 1)
            j = u - SB0 - 1
            if 0 <= j < NSB:
                pe.wait_ge(keep_done, at(lay, NSB, j + 1))
                bank = wk[j % 2]
                pe.matmul(bank[:, 0:384], tri, slk[:], start=False, stop=False, skip_group_check=True)
                pe.matmul(bank[:, P:2 * P], ones, slk[:, 2 * P:384], start=False, stop=True, skip_group_check=True).then_inc(cum_done, 1)
            if u in (13, 14):
                pe.wait_ge(od_done, at(lay, 1, 1))
                if u == 13:
                    pe.wait_ge(wT_out, at(lay, NDI + NMO, NDI))
                else:
                    pe.wait_ge(oTl_done, at(lay, 6, 1))
                turn_tokens(pe, wk[2], onat[0], 2 * (u - 13)).then_inc(oT_done, 1)
            if u == 28:
                pe.wait_ge(mask_done, at(lay, 2 * NDI + NMO, 2 * NDI + NMO))
                pe.wait_ge(o_out, at(lay, 6, 4))
                for i in range(2):
                    turn_tokens(pe, wk[i], onat[1], 2 * i).then_inc(oT_done, 1)
            if u == 30:
                pe.wait_ge(oTl_done, at(lay, 6, 4))
                pe.wait_ge(o_out, at(lay, 6, 6))
                for i in range(2):
                    turn_tokens(pe, wk[i], onat[2], 2 * i).then_inc(oT_done, 1)
            for si, (first, second, b0, b1) in enumerate(((3, 3, 0, 1), (5, 5, 0, 1), (10, 10, 0, 1), (11, 11, 0, 1), (15, 16, 2, 2), (17, 18, 2, 2))):
                for half, (step, b) in enumerate(((first, b0), (second, b1))):
                    if u != step:
                        continue
                    src = stage[si % 2]
                    if half == 0:
                        if si in (2, 3):
                            pe.wait_ge(chunk_out, at(lay, CH1, SECTIONS[si] + 1))
                        else:
                            pe.wait_ge(rope_done, at(lay, 4, si + 1 if si < 2 else si - 1))
                        if si == 2:
                            pe.wait_ge(mask_done, at(lay, 2 * NDI + NMO, 2 * NDI))
                        elif si == 4:
                            pe.wait_ge(oTl_done, at(lay, 6, 2))
                        elif si > 0:
                            pe.wait_ge(sec_out, at(lay, 12, 2 * si))
                    elif si >= 4:
                        pe.wait_ge(sec_out, at(lay, 12, 2 * si + 1))
                    turn_tokens(pe, wk[b], src, 2 * half).then_inc(sec_T, 1)
            h = u - DIFF0
            if 0 <= h < NDI:
                if h == 0:
                    pe.wait_ge(sec_out, at(lay, 12, 4))
                else:
                    pe.wait_ge(mask_done, at(lay, 2 * NDI + NMO, 2 * h))
                for m in range(2):
                    scores1(pe, wk[m], secT[Q_DIFF], secT[K_DIFF], HD * m, h).then_inc(score_done, 1)
            j = u - SB0
            if 0 <= j < NSB:
                if j == 0:
                    pe.wait_ge(sec_out, at(lay, 12, 8))
                if j >= 2:
                    pe.wait_ge(arg_done, at(lay, NSB, j - 1))
                q, k, rows, blk, bank = secT[Q_SB], secT[K_SB], slice(HD * (j % 2), HD * (j % 2) + HD), j // 2, wk[j % 2]
                pe.matmul(bank[:, 0:SEQ], k[rows, blk, 0:P], q[rows, blk, :], start=True, stop=False, skip_group_check=True)
                pe.matmul(bank[:, SEQ:384], k[rows, blk, P:SEQ], q[rows, blk, P:SEQ], start=False, stop=True, skip_group_check=True).then_inc(z_done, 1)
            j = u - MOBA0
            if 0 <= j < NMO:
                if j < 2:
                    pe.wait_ge(sec_out, at(lay, 12, 12))
                    pe.wait_ge(arg_done, at(lay, NSB, NSB - 1 + j))
                else:
                    pe.wait_ge(mask_done, at(lay, 2 * NDI + NMO, 2 * NDI + j - 1))
                scores1(pe, wk[j % 2], secT[Q_MOBA], secT[K_MOBA], HD * (j % 2), j // 2).then_inc(score_done, 1)

        def mix1_act(act, lay):
            act.preload_act_table_set(EXP_LN)
            act.wait_ge(rstd_done, at(lay, 3, 2))
            for u in range(MIX1 + 1):
                j = u - SB0 - 2
                if 0 <= j < NSB:
                    act.wait_ge(arg_done, at(lay, NSB, j + 1))
                    act.wait_ge(pv_done, at(lay, NPV, NDI + j - 1))
                    nc.scalar.activation(wT[j % 2][:], sag[:], ACT.Exp).then_inc(sbw_done, 1)
                j = u - SB0 - 1
                if 0 <= j < NSB:
                    act.wait_ge(abs_done, at(lay, NSB, j + 1))
                    if j > 0:
                        act.wait_ge(keep_done, at(lay, NSB, j))
                    nc.scalar.activation(sex[:], saz[:], ACT.Exp).then_inc(sbe_done, 1)
                    act.wait_ge(sbe_done, at(lay, NSB, j + 1))
                    nc.scalar.activation(sex[:], sex[:], ACT.Ln, bias=1.0).then_inc(ln_done, 1)
                if u in (14, 15):
                    i = u - 14
                    act.wait_ge(oT_done, at(lay, 6, i + 1))
                    nc.scalar.activation(oTh[0][:, 2 * i:2 * i + 2, :], wk[2][:].rearrange("p (k n) -> p k n", k=2), ACT.Copy,
                                         scale=gdiff[:]).then_inc(oTh_done, 1)
                for step, n, g in ((SB0 + 6, 4, 0), (SB0 + 10, 8, 1)):
                    if u == step:
                        act.wait_ge(pv_done, at(lay, NPV, NDI + n))
                        nc.scalar.activation(onat[1][:].rearrange("p t (h d) -> p h t d", d=HD)[:, 4 * g:4 * g + 4],
                                             wk[3][:].rearrange("p (h t d) -> p h t d", h=4, t=TT), ACT.Copy).then_inc(o_out, 1)
                if 0 < u < MIX1 - 1:
                    split_high(act, 1, slot_of(u + 2), lay, mix_use(u + 2))
                c = u // 2 - 1
                if u % 2 == 0 and 0 <= c < CH1:
                    unit1_done(act, lay, u - 1)
                    if c in SECTIONS:
                        si = SECTIONS.index(c)
                        if si >= 2:
                            act.wait_ge(sec_T, at(lay, 12, 2 * si - 2))
                        dst = stage[si % 2]
                    elif c in V_CHUNKS:
                        dst = vnat[V_CHUNKS[c]]
                    else:
                        dst = gate1[(c - 9) // 2][:, :, halves((c - 9) % 2)]
                    for tt in range(TT):
                        a = nc.scalar.activation(dst[:, tt, :], acc[c % 2][tt][:], ACT.Copy, scale=rstd[:, tt:tt + 1])
                    a.then_inc(chunk_out, 1)
                h = u - DIFF0 - 1
                if 0 <= h < NDI:
                    act.wait_ge(max_done, at(lay, NDI + NMO, h + 1))
                    if h > 0:
                        act.wait_ge(wdf_done, at(lay, NDI, h))
                    for m in range(2):
                        for tt, seg in enumerate((slice(0, P), slice(P, 384))):
                            a = nc.scalar.activation(ex[m][:, seg], smk[m][:, seg], ACT.Exp, bias=nmx[:, 2 * m + tt:2 * m + tt + 1],
                                                     accum_out=lsum[:, 2 * m + tt:2 * m + tt + 1])
                    a.then_inc(exp_done, 1)
                j = u - MOBA0 - 1
                if 0 <= j < NMO:
                    act.wait_ge(max_done, at(lay, NDI + NMO, NDI + j + 1))
                    if j < 2:
                        act.wait_ge(wdf_done, at(lay, NDI, NDI))
                    else:
                        act.wait_ge(wT_done, at(lay, NDI + NMO, NDI + j - 1))
                    for tt, seg in enumerate((slice(0, P), slice(P, 384))):
                        a = nc.scalar.activation(ex[j % 2][:, seg], smk[j % 2][:, seg], ACT.Exp, bias=nmx[:, 2 * (j % 2) + tt:2 * (j % 2) + tt + 1],
                                                 accum_out=lmo[:, tt, j:j + 1])
                    a.then_inc(exp_done, 1)
                if u == 4:
                    act.wait_ge(lam_sum, at(lay, 1, 1))
                    nc.scalar.activation(lame[:], lams[:], ACT.Exp).then_inc(lam_exp, 1)
                for si, steps in enumerate(((4, 4), (6, 6), (11, 11), (12, 12), (16, 17), (18, 19))):
                    for half, step in enumerate(steps):
                        if u == step:
                            act.wait_ge(sec_T, at(lay, 12, 2 * si + half + 1))
                            nc.scalar.activation(secT[SECTIONS[si]][:, 2 * half:2 * half + 2, :],
                                                 wk[half if si < 4 else 2][:].rearrange("p (k n) -> p k n", k=2), ACT.Copy,
                                                 scale=HD ** -0.5 if si % 2 == 0 else 1.0).then_inc(sec_out, 1)
                for first, n, i0, pv0 in ((DIFF0 + 2, NDI, 0, 0), (MOBA0 + 2, NMO, NDI, NDI + NSB)):
                    j = u - first
                    if 0 <= j < n:
                        act.wait_ge(wT_done, at(lay, NDI + NMO, i0 + j + 1))
                        if pv0 + j >= 2:
                            act.wait_ge(pv_done, at(lay, NPV, pv0 + j - 1))
                        nc.scalar.activation(wT[j % 2][:], wk[2][:, 0:384], ACT.Copy).then_inc(wT_out, 1)
                for step, n, g in ((DIFF0 + 4, 2, 0), (DIFF0 + 6, 4, 1)):
                    if u == step:
                        act.wait_ge(pv_done, at(lay, NPV, n))
                        nc.scalar.activation(onat[0][:].rearrange("p t (h d) -> p h t d", d=P)[:, 2 * g:2 * g + 2],
                                             wk[3][:].rearrange("p (h t d) -> p h t d", h=2, t=TT), ACT.Copy).then_inc(o_out, 1)
                for step, b in ((29, 1), (31, 2)):
                    if u == step:
                        for i in range(2):
                            act.wait_ge(oT_done, at(lay, 6, 2 * b + i + 1))
                            nc.scalar.activation(oTh[b][:, 2 * i:2 * i + 2, :], wk[i][:].rearrange("p (k n) -> p k n", k=2), ACT.Copy).then_inc(oTh_done, 1)
                k = u - PROJ1
                if 0 <= k < 6:
                    _, b, half = BRANCH[k]
                    if k == 0:
                        act.wait_ge(chunk_out, at(lay, CH1, CH1))
                    g = gate1[b][:, :, halves(half)]
                    nc.scalar.activation(g, g, ACT.Sigmoid).then_inc(sig_done, 1)
                if u in (34, 36):
                    half = (u - 34) // 2
                    for i in range(2):
                        act.wait_ge(mT_done, at(lay, 4, 2 * half + i + 1))
                        nc.scalar.activation(xh[:, 4 * half + 2 * i:4 * half + 2 * i + 2, :],
                                             wk[2 * half + i][:].rearrange("p (k n) -> p k n", k=2), ACT.Copy).then_inc(mTh_done, 1)

        def mix1_dve(dve, lay):
            causal = kblk[:, K1_CAUSAL:K1_CAUSAL + 384]
            keep = kblk[:, K1_KEEP:K1_KEEP + 384]
            drop = kblk[:, K1_DROP:K1_DROP + 384]

            def table(col):
                return kblk[:, col:col + TT * 8].rearrange("p (t e) -> p t e", t=TT).unsqueeze(2).broadcast_to((P, TT, 8, 8))

            dve.wait_ge(kblk_in, at(lay, 16, 16))
            for u in range(MIX1 + 1):
                k = u - PROJ1 - 1
                if 0 <= k < 6:
                    _, b, half = BRANCH[k]
                    c = CH1 + k
                    unit1_done(dve, lay, PROJ1 + k)
                    dve.wait_ge(sig_done, at(lay, 6, k + 1))
                    dst = mrg[:, :, halves(half)] if b == 0 else mtm[:]
                    if k == 4:
                        dve.wait_ge(merged, at(lay, 2, 1))
                    for tt in range(TT):
                        a = nc.vector.tensor_tensor(dst[:, tt, :], acc[c % 2][tt][:], gate1[b][:, tt, halves(half)], ALU.mult)
                    a.then_inc(proj_out, 1)
                    if b > 0:
                        dve.wait_ge(proj_out, at(lay, 6, k + 1))
                        a = nc.vector.tensor_tensor(mrg[:, :, halves(half)], mrg[:, :, halves(half)], mtm[:], ALU.add)
                        if b == 2:
                            a.then_inc(merged, 1)
                        else:
                            link(dve, a)
                j = u - SB0 - 2
                if 0 <= j < NSB:
                    dve.wait_ge(cum_done, at(lay, NSB, j + 1))
                    if j > 0:
                        dve.wait_ge(sbw_done, at(lay, NSB, j))
                    nc.vector.tensor_tensor(sag[:], wk[j % 2][:, 0:384], drop, ALU.add).then_inc(arg_done, 1)
                j = u - SB0 - 1
                if 0 <= j < NSB:
                    bank = wk[j % 2]
                    dve.wait_ge(z_done, at(lay, NSB, j + 1))
                    link(dve, nc.vector.tensor_scalar(smx[:], bank[:, 0:384], 0.0, None, ALU.max))
                    nc.vector.scalar_tensor_tensor(saz[:], smx[:], -2.0, bank[:, 0:384], ALU.mult, ALU.add).then_inc(abs_done, 1)
                h = u - DIFF0 - 1
                if 0 <= h < NDI:
                    if h > 0:
                        dve.wait_ge(exp_done, at(lay, NDI + NMO, h))
                    for m in range(2):
                        dve.wait_ge(score_done, at(lay, 2 * NDI + NMO, 2 * h + m + 1))
                        nc.vector.tensor_tensor(smk[m][:], wk[m][:, 0:384], causal, ALU.add).then_inc(mask_done, 1)
                    dve.wait_ge(mask_done, at(lay, 2 * NDI + NMO, 2 * h + 2))
                    for m in range(2):
                        nc.vector.tensor_reduce(nmx[:, 2 * m:2 * m + 1], smk[m][:, 0:P], AX.X, ALU.max, negate=True)
                        a = nc.vector.tensor_reduce(nmx[:, 2 * m + 1:2 * m + 2], smk[m][:, P:384], AX.X, ALU.max, negate=True)
                    a.then_inc(max_done, 1)
                j = u - MOBA0 - 1
                if 0 <= j < NMO:
                    m = j % 2
                    dve.wait_ge(score_done, at(lay, 2 * NDI + NMO, 2 * NDI + j + 1))
                    if j >= 2:
                        dve.wait_ge(exp_done, at(lay, NDI + NMO, NDI + j - 1))
                    nc.vector.tensor_tensor(smk[m][:], wk[m][:, 0:384], causal, ALU.add).then_inc(mask_done, 1)
                    dve.wait_ge(mask_done, at(lay, 2 * NDI + NMO, 2 * NDI + j + 1))
                    nc.vector.tensor_reduce(nmx[:, 2 * m:2 * m + 1], smk[m][:, 0:P], AX.X, ALU.max, negate=True)
                    nc.vector.tensor_reduce(nmx[:, 2 * m + 1:2 * m + 2], smk[m][:, P:384], AX.X, ALU.max, negate=True).then_inc(max_done, 1)
                j = u - SB0 - 1
                if 0 <= j < NSB:
                    dve.wait_ge(ln_done, at(lay, NSB, j + 1))
                    link(dve, nc.vector.tensor_tensor(saz[:], smx[:], sex[:], ALU.add))
                    if j > 0:
                        dve.wait_ge(cum_done, at(lay, NSB, j))
                    nc.vector.scalar_tensor_tensor(slk[:], saz[:], -1.0, keep, ALU.mult, ALU.mult).then_inc(keep_done, 1)
                if u in (14, 15):
                    i = u - 14
                    dve.wait_ge(oTh_done, at(lay, 6, i + 1))
                    nc.vector.scalar_tensor_tensor(oTl[0][:, 2 * i:2 * i + 2, :], wk[2][:].rearrange("p (k n) -> p k n", k=2), gdiff[:],
                                                   oTh[0][:, 2 * i:2 * i + 2, :].bitcast(F32), ALU.mult, ALU.subtract).then_inc(oTl_done, 1)
                if u < MIX1 - 1 and slot_of(u + 2) != POOLS:
                    split_low(dve, nc.vector, 1, slot_of(u + 2), lay, mix_use(u + 2))
                h = u - DIFF0 - 1
                if 0 <= h < NDI:
                    dve.wait_ge(exp_done, at(lay, NDI + NMO, h + 1))
                    link(dve, nc.vector.reciprocal(rsum[:], lsum[:]))
                    link(dve, nc.vector.tensor_scalar(rsl[:], rsum[:, 2:4], lam[:], None, ALU.mult))
                    if h > 0:
                        dve.wait_ge(wT_done, at(lay, NDI + NMO, h))
                    for tt, seg in enumerate((slice(0, P), slice(P, 384))):
                        a = nc.vector.tensor_scalar(wdf[:, seg], ex[1][:, seg], rsl[:, tt:tt + 1], None, ALU.mult)
                    link(dve, a)
                    for tt, seg in enumerate((slice(0, P), slice(P, 384))):
                        a = nc.vector.scalar_tensor_tensor(wdf[:, seg], ex[0][:, seg], rsum[:, tt:tt + 1], wdf[:, seg], ALU.mult, ALU.subtract)
                    a.then_inc(wdf_done, 1)
                if u == 0:
                    qk = cols[:, C1_LQK:C1_LQK + 4 * HD].rearrange("p (a b d) -> p a b d", a=2, b=2)
                    link(dve, nc.vector.tensor_tensor(lamp[:], qk[:, :, 0, :], qk[:, :, 1, :], ALU.mult))
                    nc.vector.tensor_reduce(lams[:], lamp[:], AX.X, ALU.add).then_inc(lam_sum, 1)
                if u == 4:
                    dve.wait_ge(lam_exp, at(lay, 1, 1))
                    link(dve, nc.vector.tensor_tensor(lam[:], lame[:, 0:1], lame[:, 1:2], ALU.subtract))
                    nc.vector.tensor_tensor(lam[:], lam[:], cols[:, C1_LAM0:C1_LAM0 + 1], ALU.add)
                    link(dve, nc.vector.tensor_tensor(gdiff[:], cols[:, C1_DIFF:C1_DIFF + 1], cols[:, C1_LAM1:C1_LAM1 + 1], ALU.mult))
                for n, (si, step) in enumerate(((0, 2), (1, 4), (4, 14), (5, 16))):
                    if u == step:
                        dve.wait_ge(chunk_out, at(lay, CH1, SECTIONS[si] + 1))
                        v = stage[si % 2][:].rearrange("p t (h d) -> p t h d", d=HD)
                        x1, x2 = v[:, :, :, 0:8], v[:, :, :, 8:16]
                        for i, (x, col) in enumerate(((x1, K1_COS), (x2, K1_SIN), (x2, K1_COS), (x1, K1_SIN))):
                            a = nc.vector.tensor_tensor(rt[i][:], x, table(col), ALU.mult)
                        link(dve, a)
                        nc.vector.tensor_tensor(x1, rt[0][:], rt[1][:], ALU.subtract)
                        nc.vector.tensor_tensor(x2, rt[2][:], rt[3][:], ALU.add).then_inc(rope_done, 1)
                for step, g in ((MOBA0 + 6, 0), (MOBA0 + 10, 1)):
                    if u == step:
                        hs = slice(4 * g, 4 * g + 4)
                        dve.wait_ge(pv_done, at(lay, NPV, NDI + NSB + 4 * g + 4))
                        link(dve, nc.vector.reciprocal(rmo[:, :, hs], lmo[:, :, hs]))
                        for tt in range(TT):
                            a = nc.vector.tensor_tensor(onat[2][:, tt, :].rearrange("p (h d) -> p h d", d=HD)[:, hs],
                                                        wk[3][:].rearrange("p (h t d) -> p h t d", h=4, t=TT)[:, :, tt, :],
                                                        rmo[:, tt, hs].unsqueeze(2).broadcast_to((P, 4, HD)), ALU.mult)
                        a.then_inc(o_out, 1)
                if u == 12:
                    dve.wait_ge(osq_done, at(lay, 1, 1))
                    link(dve, nc.vector.tensor_reduce(ssd[:], osq[:].rearrange("p t (h d) -> p (t h) d", d=P), AX.X, ALU.add))
                    nc.vector.tensor_scalar(msd[:], ssd[:], 1.0 / P, EPS, ALU.mult, ALU.add).then_inc(od_ms, 1)
                if u == 13:
                    dve.wait_ge(od_pow, at(lay, 1, 1))
                    o = onat[0][:].rearrange("p t (h d) -> p (t h) d", d=P)
                    nc.vector.tensor_tensor(o, o, rsd[:].unsqueeze(2).broadcast_to((P, 8, P)), ALU.mult).then_inc(od_done, 1)
                for step, b in ((29, 1), (31, 2)):
                    if u == step:
                        for i in range(2):
                            dve.wait_ge(oTh_done, at(lay, 6, 2 * b + i + 1))
                            nc.vector.tensor_tensor(oTl[b][:, 2 * i:2 * i + 2, :], wk[i][:].rearrange("p (k n) -> p k n", k=2),
                                                    oTh[b][:, 2 * i:2 * i + 2, :].bitcast(F32), ALU.subtract).then_inc(oTl_done, 1)
                if u in (34, 36):
                    half = (u - 34) // 2
                    for i in range(2):
                        kt = 4 * half + 2 * i
                        dve.wait_ge(mTh_done, at(lay, 4, 2 * half + i + 1))
                        nc.vector.tensor_tensor(xl[:, kt:kt + 2, :], wk[2 * half + i][:].rearrange("p (k n) -> p k n", k=2),
                                                xh[:, kt:kt + 2, :].bitcast(F32), ALU.subtract).then_inc(mTl_done, 1)

        def mix1_pool(pool, lay):
            split_low(pool, nc.gpsimd, 1, POOLS, lay, mix_use(2))
            norm_pool(pool, lay, 1)
            for u in range(MIX1):
                if u == 12:
                    pool.wait_ge(o_out, at(lay, 6, 2))
                    nc.gpsimd.tensor_tensor(osq[:], onat[0][:], onat[0][:], ALU.mult).then_inc(osq_done, 1)
                if 0 < u < MIX1 - 1 and slot_of(u + 2) == POOLS:
                    split_low(pool, nc.gpsimd, 1, POOLS, lay, mix_use(u + 2))
                if u == 12:
                    pool.wait_ge(od_ms, at(lay, 1, 1))
                    nc.gpsimd.tensor_tensor(rsd[:], msd[:], neghalf[:, 0:8], ALU.pow).then_inc(od_pow, 1)

        NHG = 2 * LEVELS
        HG0, AQ0, ATT0 = 9, 2 * AQ_CHUNK + 2, 36
        EARLY = ((3, 0), (5, 1), (7, 2), (8, 3))
        NSEC = 4 + 6

        def at2(lay, per_layer, k):
            return lay * per_layer + (k - LAYERS * per_layer)

        def unit2_done(eng, lay, u):
            eng.wait_ge(slot_used[slot_of(u)], use(2, slot_of(u), lay, mix_use(u) + 1))

        def mix2_sp(sp, lay):
            for u in range(MIX2):
                s = slot_of(u)
                if u < PROJ2:
                    weights, row, col = t["w_in2"], lay * D + ((u % 2) * 512 - LAYERS * D), slice(CHUNKS2[u // 2], CHUNKS2[u // 2] + 512)
                elif u < PROJ2 + 4:
                    half, kh = divmod(u - PROJ2, 2)
                    weights, row, col = t["w_a"], lay * D + (kh * 512 - LAYERS * D), halves(half)
                elif u < PROJ2 + 6:
                    weights, row, col = t["w_b"], lay * 512 - LAYERS * 512, halves(u - PROJ2 - 4)
                else:
                    kh, half = divmod(u - PROJ2 - 6, 2)
                    weights, row, col = t["w_out2"], lay * D + (kh * 512 - LAYERS * D), halves(half)
                sp.wait_ge(low_done[s], use(2, s, lay, mix_use(u)))
                load_unit(sp, s, weights, row, col)

        def mix2_pe(pe, lay):
            lead_in(pe, 2, lay, 1, lambda s: FSTEPS, acc[0])
            for u in range(2, MIX2 - 2):
                s = slot_of(u)
                if u < PROJ2:
                    c, half = divmod(u, 2)
                    if half == 0 and c >= 2:
                        pe.wait_ge(chunk_out2, at2(lay, CH2, c - 1))
                    lhs = [(xh[:, 4 * half + k, :], xl[:, 4 * half + k, :]) for k in range(4)]
                    out, first, last = acc[c % 2], half == 0, half == 1
                elif u < PROJ2 + 4:
                    half, kh = divmod(u - PROJ2, 2)
                    if kh == 0:
                        pe.wait_ge(chunk_out2, at2(lay, CH2, CH2 - 1 + half))
                    pe.wait_ge(oaTl_done, at2(lay, 8, 4 * kh + 4))
                    lhs = [(oaTh[:, 4 * kh + k, :], oaTl[:, 4 * kh + k, :]) for k in range(4)]
                    out, first, last = acc[(CH2 + half) % 2], kh == 0, kh == 1
                elif u < PROJ2 + 6:
                    half = u - PROJ2 - 4
                    pe.wait_ge(proj_out2, at2(lay, 4, half + 1))
                    pe.wait_ge(obTl_done, at2(lay, 2, 2))
                    lhs = [(obTh[:, k, :], obTl[:, k, :]) for k in range(4)]
                    out, first, last = acc[(CH2 + half) % 2], True, True
                else:
                    half = u - PROJ2 - 6
                    pe.wait_ge(proj_out2, at2(lay, 4, 3 + half))
                    pe.wait_ge(mTl_done2, at2(lay, 4, 2))
                    lhs = [(xh[:, k, :], xl[:, k, :]) for k in range(4)]
                    out, first, last = [YMIX[tt][half] for tt in range(TT)], True, False
                pe.wait_ge(low_done[s], use(2, s, lay, mix_use(u) + 1))
                for k in range(4):
                    mm = product(pe, [[o] for o in out], lhs[k][0], lhs[k][1], s, k * 512, 512, first and k == 0, last and k == 3)
                    if k == 1:
                        mix2_mid(pe, lay, u)
                mm.then_inc(slot_used[s], 1)
                mix2_tail(pe, lay, u)
            pe.wait_ge(mTl_done2, at2(lay, 4, 4))
            mixer_end(pe, 2, lay, MIX2)

        def mix2_mid(pe, lay, u):
            if u == 45:
                pe.wait_ge(ob_out, at2(lay, 2, 2))
                pe.wait_ge(wTa_out, at2(lay, ATT_HEADS, ATT_HEADS))
                for i in range(2):
                    turn_tokens(pe, wk[i], ob, 2 * i).then_inc(obT_done, 1)
            if u in (47, 48):
                half = u - 47
                pe.wait_ge(merged2, at2(lay, 2, half + 1))
                if half == 0:
                    pe.wait_ge(obTl_done, at2(lay, 2, 2))
                for i in range(2):
                    turn_tokens(pe, wk[2 * half + i], mrg2, 4 * half + 2 * i).then_inc(mT_done2, 1)

        def mix2_tail(pe, lay, u):
            for hf, step, b0 in ((0, HG0 + LEVELS, 2), (1, HG0 + NHG, 0)):
                if u == step:
                    pe.wait_ge(lev_out, at2(lay, NHG, LEVELS * (hf + 1)))
                    pe.wait_ge(chunk_out2, at2(lay, CH2, 5 + hf))
                    if hf == 0:
                        pe.wait_ge(f_done, at2(lay, 2, 2))
                    for h in range(4):
                        o = wk[b0 + h // 2][:, (h % 2) * SEQ:(h % 2 + 1) * SEQ]
                        v = hv[:, :, (4 * hf + h) * P:(4 * hf + h + 1) * P]
                        pe.matmul(o[:, 0:P], att[:, h, 0, :], v[:, 0, :], start=True, stop=True)
                        pe.matmul(o[:, P:SEQ], att[:, h, 2, :], v[:, 0, :], start=True, stop=False)
                        mm = pe.matmul(o[:, P:SEQ], att[:, h, 1, :], v[:, 1, :], start=False, stop=True)
                    mm.then_inc(pvh_done, 1)
            n = u - HG0
            if 0 <= n < NHG:
                hf, lev = divmod(n, LEVELS)
                if n == 0:
                    pe.wait_ge(hq_out, at2(lay, 2, 2))
                else:
                    pe.wait_ge(lev_out, at2(lay, NHG, n))
                if lev == 0:
                    pe.wait_ge(k_done, at2(lay, 2, hf + 1))
                else:
                    pe.wait_ge(A_done, at2(lay, 2 * (LEVELS - 1), (LEVELS - 1) * hf + lev))
                for h in range(4):
                    hd = 4 * hf + h
                    if lev == LEVELS - 1:
                        mm = pe.matmul(wk[0][:, h * P:(h + 1) * P], Av[:, h, 0:P], Av[:, h, P:SEQ], start=True, stop=True)
                        continue
                    for tl in range(TT):
                        cs = slice(tl * P, (tl + 1) * P)
                        out = wk[h // 2][:, (h % 2) * SEQ + tl * P:(h % 2) * SEQ + (tl + 1) * P]
                        if lev == 0:
                            mm = pe.matmul(out, kT[:, hd, cs], qT[:, hd, cs], start=True, stop=True)
                            continue
                        L = 1 << (lev - 1)
                        late = [x.rearrange("p (b l) -> p b l", l=2 * L)[:, :, L:2 * L] for x in (out, Av[:, h, cs])]
                        mm = pe.matmul(late[0], Av[:, h, cs], late[1], start=True, stop=True)
                mm.then_inc(lev_done, 1)
            if u in (32, 34):
                i0 = (u - 32) // 2
                pe.wait_ge(oa_done, at2(lay, 2, i0 + 1))
                if i0 == 0:
                    pe.wait_ge(oh_out, at2(lay, 2, 2))
                else:
                    pe.wait_ge(oaTl_done, at2(lay, 8, 4))
                for i in range(2):
                    turn_tokens(pe, wk[i], hgt, 4 * i0 + 2 * i).then_inc(oaT_done, 1)
            hd, odd = divmod(u - ATT0 - 2, 2)
            if odd == 0 and 0 <= hd < ATT_HEADS:
                pe.wait_ge(wTa_out, at2(lay, ATT_HEADS, hd + 1))
                if hd == 0:
                    pe.wait_ge(sec_out2, at2(lay, 6, 6))
                if hd == 2:
                    pe.wait_ge(ob_out, at2(lay, 2, 1))
                o = wk[3][:, (hd % 2) * SEQ:(hd % 2 + 1) * SEQ]
                for g in range(ATT_GROUPS):
                    pe.matmul(o[:, 0:P], wTa[:, g, 0:P], av[:, g, 0, hd * P:(hd + 1) * P], start=g == 0, stop=g == ATT_GROUPS - 1)
                for g in range(ATT_GROUPS):
                    pe.matmul(o[:, P:SEQ], wTa[:, g, P:2 * P], av[:, g, 0, hd * P:(hd + 1) * P], start=g == 0, stop=False)
                    mm = pe.matmul(o[:, P:SEQ], wTa[:, g, 2 * P:384], av[:, g, 1, hd * P:(hd + 1) * P], start=False, stop=g == ATT_GROUPS - 1)
                mm.then_inc(dpv_done, 1)
            hd, odd = divmod(u - ATT0 - 1, 2)
            if odd == 0 and 0 <= hd < ATT_HEADS:
                pe.wait_ge(dexp_done, at2(lay, ATT_HEADS, hd + 1))
                for g in range(ATT_GROUPS):
                    for b in range(3):
                        tr = pe.transpose(wk[g][:, b * P:(b + 1) * P], exa[:, g, b * P:(b + 1) * P], ident)
                tr.then_inc(dT_done, 1)
            for step, s in EARLY:
                if u == step:
                    pe.wait_ge(chunk_out2, at2(lay, CH2, s + 1))
                    if s == 2:
                        pe.wait_ge(hq_out, at2(lay, 2, 1))
                    if s == 3:
                        pe.wait_ge(f_done, at2(lay, 2, 1))
                    for i in range(2):
                        tr = turn_tokens(pe, wk[2 * (s % 2) + i], stg[s % 2], 2 * i)
                    tr.then_inc(sec_T2, 1)
            a, odd = divmod(u - AQ0 - 3, 2)
            if odd == 0 and 0 <= a < 6:
                pe.wait_ge(rope_done2, at2(lay, 6, a + 1))
                if a == 0:
                    pe.wait_ge(oh_out, at2(lay, 2, 1))
                else:
                    pe.wait_ge(sec_out2, at2(lay, 6, a))
                for i in range(2):
                    tr = turn_tokens(pe, wk[2 + i], stg[a % 2], 2 * i)
                tr.then_inc(sec_T2, 1)
            hd, odd = divmod(u - ATT0, 2)
            if odd == 0 and 0 <= hd < ATT_HEADS:
                if hd == 0:
                    pe.wait_ge(sec_out2, at2(lay, 6, 6))
                    pe.wait_ge(oaTl_done, at2(lay, 8, 8))
                else:
                    pe.wait_ge(wTa_out, at2(lay, ATT_HEADS, hd))
                for g in range(ATT_GROUPS):
                    q, k = aqT[:, 4 * g + hd, :], akT[:, 4 * g + hd, :]
                    pe.matmul(wk[g][:, 0:P], q[:, 0:P], k[:, 0:P], start=True, stop=True)
                    pe.matmul(wk[g][:, P:384], q[:, P:SEQ], k[:, 0:SEQ], start=True, stop=True).then_inc(dsc_done, 1)

        def mix2_act(act, lay):
            act.wait_ge(lbw, at2(lay, 1, 1))
            nc.scalar.activation(lbe[:], lbe[:], ACT.Exp).then_inc(lbx, 1)
            act.wait_ge(rstd_done, at(lay, 3, 2))
            for u in range(MIX2 + 1):
                n = u - HG0
                if 0 <= n < NHG and n % LEVELS:
                    hf, lev = divmod(n, LEVELS)
                    i = (LEVELS - 1) * hf + lev
                    if lev < LEVELS - 1:
                        L = 1 << (lev - 1)
                        d = dl[:].rearrange("p h (b l) -> p (h b) l", l=2 * L)
                        act.wait_ge(diff_ready, at2(lay, 2 * (LEVELS - 2), (LEVELS - 2) * hf + lev))
                        nc.scalar.activation(d[:, :, L:2 * L], d[:, :, L:2 * L], ACT.Exp)
                        nc.scalar.activation(d[:, :, 0:L], d[:, :, 0:L], ACT.Exp, scale=-1.0).then_inc(dec_done, 1)
                    else:
                        act.wait_ge(A_done, at2(lay, 2 * (LEVELS - 1), i - 1))
                        for h in range(4):
                            hd = 4 * hf + h
                            nc.scalar.activation(dl[:, h, 0:P], gc[:, hd, 0:P], ACT.Exp, bias=gc[:, hd, P - 1:P], scale=-1.0)
                        nc.scalar.activation(dl[:, :, P:SEQ], gc[:, 4 * hf:4 * hf + 4, P:SEQ], ACT.Exp).then_inc(dec_done, 1)
                if 0 < u < MIX2 - 1:
                    split_high(act, 2, slot_of(u + 2), lay, mix_use(u + 2))
                c = u // 2 - 1
                if u % 2 == 0 and 0 <= c < CH2:
                    unit2_done(act, lay, u - 1)
                    func = ACT.Copy
                    if c < 4:
                        func, dst = (ACT.Silu, ACT.Sigmoid)[c % 2], stg[c % 2]
                        if c >= 2:
                            act.wait_ge(sec_T2, at2(lay, NSEC, c - 1))
                    elif c < 8:
                        dst = (hv, hgt)[(c - 4) // 2][:, :, halves(c % 2)]
                    elif c in AV_CHUNKS:
                        if c > AQ_CHUNK:
                            act.wait_ge(asq_done, at2(lay, 6, 6))
                        dst = av[:, AV_CHUNKS[c]]
                    elif c < AQ_CHUNK + 6:
                        act.wait_ge(sec_T2, at2(lay, NSEC, 4 + c - AQ_CHUNK - 1))
                        dst = stg[(c - AQ_CHUNK) % 2]
                    else:
                        dst = gate2[(c - 17) // 2][:, :, halves((c - 17) % 2)]
                    for tt in range(TT):
                        a = nc.scalar.activation(dst[:, tt, :], acc[c % 2][tt][:], func, scale=rstd[:, tt:tt + 1])
                    a.then_inc(chunk_out2, 1)
                for hf, step in ((0, 4), (1, 8)):
                    if u == step:
                        act.wait_ge(sec_T2, at2(lay, NSEC, 2 * hf + 1))
                        for i in range(2):
                            a = nc.scalar.activation(qT[:, 4 * hf + 2 * i:4 * hf + 2 * i + 2, :], wk[i][:].rearrange("p (k n) -> p k n", k=2), ACT.Copy)
                        a.then_inc(hq_out, 1)
                for hf, step in ((0, 6), (1, 9)):
                    if u == step:
                        act.preload_act_table_set(EXP_LN)
                        act.wait_ge(k_done, at2(lay, 2, hf + 1))
                        g = gc[:, 4 * hf:4 * hf + 4, :]
                        nc.scalar.activation(g, g, ACT.Ln).then_inc(lnf_done, 1)
                for hf, step, b0 in ((0, HG0 + LEVELS + 1, 2), (1, HG0 + NHG + 1, 0)):
                    if u == step:
                        act.wait_ge(pvh_done, at2(lay, 2, hf + 1))
                        for i in range(8):
                            a = nc.scalar.activation(oq[hf][:, i], wk[b0 + i // 4][:, (i % 4) * P:(i % 4 + 1) * P], ACT.Square, accum_out=sso[:, i:i + 1])
                        a.then_inc(oh_sq, 1)
                if u == 28:
                    act.wait_ge(chunk_out2, at2(lay, CH2, 8))
                    nc.scalar.activation(hgt[:], hgt[:], ACT.Silu).then_inc(hgs_done, 1)
                a, odd = divmod(u - AQ0, 2)
                if odd == 0 and 0 <= a < 6:
                    act.wait_ge(chunk_out2, at2(lay, CH2, AQ_CHUNK + a + 1))
                    if a > 0:
                        act.wait_ge(apow_done, at2(lay, 6, a))
                    for i in range(8):
                        tt, h = divmod(i, ATT_HEADS)
                        cs = slice(h * DH, (h + 1) * DH)
                        r = nc.scalar.activation(oq[0][:, i], stg[a % 2][:, tt, cs], ACT.Square, accum_out=ssa[:, i:i + 1])
                    r.then_inc(asq_done, 1)
                a, odd = divmod(u - AQ0 - 4, 2)
                if odd == 0 and 0 <= a < 6:
                    act.wait_ge(sec_T2, at2(lay, NSEC, 4 + a + 1))
                    for i in range(2):
                        r = nc.scalar.activation((aqT, akT)[a // 3][:, 4 * (a % 3) + 2 * i:4 * (a % 3) + 2 * i + 2, :],
                                                 wk[2 + i][:].rearrange("p (k n) -> p k n", k=2), ACT.Copy)
                    r.then_inc(sec_out2, 1)
                if u in (33, 35):
                    for kt in range(2 * (u - 33), 2 * (u - 33) + 4):
                        if kt % 2 == 0:
                            act.wait_ge(oaT_done, at2(lay, 4, kt // 2 + 1))
                        nc.scalar.activation(oaTh[:, kt, :], wk[kt // 2 % 2][:, (kt % 2) * SEQ:(kt % 2 + 1) * SEQ], ACT.Copy,
                                             scale=cols[:, C2_OUT + kt:C2_OUT + kt + 1]).then_inc(oaTh_done, 1)
                hd, odd = divmod(u - ATT0 - 2, 2)
                if odd == 0 and 0 <= hd < ATT_HEADS:
                    act.wait_ge(dT_done, at2(lay, ATT_HEADS, hd + 1))
                    if hd > 0:
                        act.wait_ge(dpv_done, at2(lay, ATT_HEADS, hd))
                    for g in range(ATT_GROUPS):
                        a = nc.scalar.activation(wTa[:, g, :], wk[g][:, 0:384], ACT.Copy)
                    a.then_inc(wTa_out, 1)
                hd, odd = divmod(u - ATT0 - 1, 2)
                if odd == 0 and 0 <= hd < ATT_HEADS:
                    act.wait_ge(dmax_done, at2(lay, ATT_HEADS, hd + 1))
                    if hd > 0:
                        act.wait_ge(dT_done, at2(lay, ATT_HEADS, hd))
                    for tt, seg in enumerate((slice(0, P), slice(P, 384))):
                        a = nc.scalar.activation(exa[:, :, seg], sma[:, :, seg], ACT.Exp, bias=nma[:, tt:tt + 1], accum_out=lat[:, hd, tt:tt + 1])
                    a.then_inc(dexp_done, 1)
                k = u - 44
                if 0 <= k < 4:
                    if k == 0:
                        act.wait_ge(chunk_out2, at2(lay, CH2, CH2))
                    g = gate2[k // 2][:, :, halves(k % 2)]
                    nc.scalar.activation(g, g, ACT.Sigmoid).then_inc(sig_done2, 1)
                if u == 45:
                    for i in range(2):
                        act.wait_ge(obT_done, at2(lay, 2, i + 1))
                        nc.scalar.activation(obTh[:, 2 * i:2 * i + 2, :], wk[i][:].rearrange("p (k n) -> p k n", k=2), ACT.Copy).then_inc(obTh_done, 1)
                if u in (47, 48):
                    half = u - 47
                    for i in range(2):
                        act.wait_ge(mT_done2, at2(lay, 4, 2 * half + i + 1))
                        nc.scalar.activation(xh[:, 4 * half + 2 * i:4 * half + 2 * i + 2, :],
                                             wk[2 * half + i][:].rearrange("p (k n) -> p k n", k=2), ACT.Copy).then_inc(mTh_done2, 1)

        def mix2_dve(dve, lay):
            def per_head(x, n):
                return x.unsqueeze(2).broadcast_to((P, n, P))

            dve.wait_ge(kblk_in, at(lay, 16, 16))
            l2 = cols[:, C2_LB:C2_LB + 2 * HG_HEADS].rearrange("p (l h) -> p l h", l=2)
            link(dve, nc.vector.tensor_tensor(lbm[:], l2[:, 0, :], l2[:, 1, :], ALU.max))
            nc.vector.tensor_tensor(lbe[:], l2, lbm[:].unsqueeze(1).broadcast_to((P, 2, HG_HEADS)), ALU.subtract).then_inc(lbw, 1)
            for u in range(MIX2 + 1):
                n = u - HG0
                if 0 <= n < NHG and n % LEVELS:
                    hf, lev = divmod(n, LEVELS)
                    L = 1 << (lev - 1)
                    dve.wait_ge(dec_done, at2(lay, 2 * (LEVELS - 1), (LEVELS - 1) * hf + lev))
                    if lev == 1:
                        dve.wait_ge(hq_out, at2(lay, 2, hf + 1))
                    dve.wait_ge(lev_done, at2(lay, NHG, n))
                    view = [x.rearrange("p h (b l) -> p (h b) l", l=2 * L)
                            for x in (Av[:], dl[:], qT[:, 4 * hf:4 * hf + 4, :], kT[:, 4 * hf:4 * hf + 4, :])]
                    nc.vector.tensor_tensor(view[0][:, :, L:2 * L], view[1][:, :, L:2 * L], view[2][:, :, L:2 * L], ALU.mult)
                    nc.vector.tensor_tensor(view[0][:, :, 0:L], view[1][:, :, 0:L], view[3][:, :, 0:L], ALU.mult).then_inc(A_done, 1)
                n = u - HG0 - 1
                if 0 <= n < NHG:
                    hf, lev = divmod(n, LEVELS)
                    if lev == LEVELS - 1:
                        dve.wait_ge(lev_done, at2(lay, NHG, n + 1))
                    if lev == LEVELS - 1:
                        a = nc.vector.tensor_copy(att[:, :, 2, :], wk[0][:].rearrange("p (h s) -> p h s", h=4))
                    else:
                        mask = kblk[:, K2_LEV + lev * P:K2_LEV + (lev + 1) * P].unsqueeze(1).broadcast_to((P, 2, P))
                        if n == LEVELS:
                            dve.wait_ge(pvh_done, at2(lay, 2, 1))
                        for h in range(4):
                            src = wk[h // 2][:, (h % 2) * SEQ:(h % 2 + 1) * SEQ].rearrange("p (t s) -> p t s", t=TT)
                            if lev == 0:
                                a = nc.vector.tensor_tensor(att[:, h, 0:2, :], src, mask, ALU.mult)
                            else:
                                a = nc.vector.copy_predicated(att[:, h, 0:2, :], mask.bitcast(U32), src)
                    a.then_inc(lev_out, 1)
                for step, p in ((ATT0 + 5, 0), (ATT0 + 9, 1)):
                    if u == step:
                        hs = slice(2 * p, 2 * p + 2)
                        dve.wait_ge(dpv_done, at2(lay, ATT_HEADS, 2 * p + 2))
                        link(dve, nc.vector.reciprocal(rat[:, hs, :], lat[:, hs, :]))
                        for tt in range(TT):
                            r = nc.vector.tensor_tensor(ob[:, tt, :].rearrange("p (h d) -> p h d", d=DH)[:, hs],
                                                        wk[3][:].rearrange("p (h t d) -> p h t d", h=2, t=TT)[:, :, tt, :],
                                                        per_head(rat[:, hs, tt], 2), ALU.mult)
                        r.then_inc(ob_out, 1)
                for k, (step, b, half, unit) in enumerate(((44, 0, 0, 43), (46, 0, 1, 45), (47, 1, 0, 46), (48, 1, 1, 47))):
                    if u == step:
                        unit2_done(dve, lay, unit)
                        dve.wait_ge(sig_done2, at2(lay, 4, k + 1))
                        dst = mrg2[:, :, halves(half)] if b == 0 else mtm2[:]
                        if k == 3:
                            dve.wait_ge(merged2, at2(lay, 2, 1))
                        for tt in range(TT):
                            a = nc.vector.tensor_tensor(dst[:, tt, :], acc[(CH2 + half) % 2][tt][:], gate2[b][:, tt, halves(half)], ALU.mult)
                        a.then_inc(proj_out2, 1)
                        if b == 1:
                            dve.wait_ge(proj_out2, at2(lay, 4, k + 1))
                            m = mrg2[:, :, halves(half)]
                            nc.vector.tensor_tensor(m, m, mtm2[:], ALU.add).then_inc(merged2, 1)
                a, odd = divmod(u - AQ0 - 2, 2)
                if odd == 0 and 0 <= a < 6:
                    x = stg[a % 2][:].rearrange("p t (h d) -> p t h d", d=DH)
                    r8 = rtm[:].rearrange("p t (h d) -> p t h d", d=DH)
                    H = DH // 2
                    for tt in range(TT):
                        sin = kblk[:, K2_SIN + tt * DH:K2_SIN + (tt + 1) * DH].unsqueeze(1).broadcast_to((P, ATT_HEADS, DH))
                        nc.vector.tensor_tensor(r8[:, tt, :, 0:H], x[:, tt, :, H:DH], sin[:, :, 0:H], ALU.mult)
                        nc.vector.tensor_tensor(r8[:, tt, :, H:DH], x[:, tt, :, 0:H], sin[:, :, H:DH], ALU.mult)
                    for tt in range(TT):
                        cos = kblk[:, K2_COS + tt * DH:K2_COS + (tt + 1) * DH].unsqueeze(1).broadcast_to((P, ATT_HEADS, DH))
                        r = nc.vector.tensor_tensor(rsq[:, tt, :].rearrange("p (h d) -> p h d", d=DH), x[:, tt, :, :], cos, ALU.mult)
                    link(dve, r)
                    nc.vector.tensor_tensor(stg[a % 2][:], rsq[:], rtm[:], ALU.add).then_inc(rope_done2, 1)
                if u < MIX2 - 1 and slot_of(u + 2) != POOLS:
                    split_low(dve, nc.vector, 2, slot_of(u + 2), lay, mix_use(u + 2))
                if u == 1:
                    dve.wait_ge(lbx, at2(lay, 1, 1))
                    link(dve, nc.vector.tensor_tensor(lbs[:], lbe[:, 0, :], lbe[:, 1, :], ALU.add))
                    link(dve, nc.vector.reciprocal(lbm[:], lbs[:]))
                    link(dve, nc.vector.tensor_tensor(lbe[:], lbe[:], lbm[:].unsqueeze(1).broadcast_to((P, 2, HG_HEADS)), ALU.mult))
                    link(dve, nc.vector.tensor_tensor(lbs[:], lbe[:, 0, :], lbe[:, 1, :], ALU.add))
                    link(dve, nc.vector.tensor_tensor(lbs[:], lbs[:], lbe[:, 0, :], ALU.subtract))
                    link(dve, nc.vector.tensor_scalar(lb[:], lbs[:], cols[:, C2_LAYER:C2_LAYER + 1], None, ALU.mult))
                    link(dve, nc.vector.tensor_scalar(omlb[:], lb[:], -1.0, 1.0, ALU.mult, ALU.add))
                for hf, step in ((0, 6), (1, 9)):
                    if u == step:
                        dve.wait_ge(sec_T2, at2(lay, NSEC, 2 * hf + 2))
                        for h in range(4):
                            hd = 4 * hf + h
                            a = nc.vector.tensor_scalar(gc[:, hd, :], wk[2 + h // 2][:, (h % 2) * SEQ:(h % 2 + 1) * SEQ],
                                                        omlb[:, hd:hd + 1], lb[:, hd:hd + 1], ALU.mult, ALU.add)
                        a.then_inc(f_done, 1)
                        dve.wait_ge(f_done, at2(lay, 2, hf + 1))
                        hs = slice(4 * hf, 4 * hf + 4)
                        nc.vector.tensor_scalar(kT[:, hs, :], gc[:, hs, :], -1.0, 1.0, ALU.mult, ALU.add).then_inc(k_done, 1)
                        dve.wait_ge(lnf_done, at2(lay, 2, hf + 1))
                        for h in range(4):
                            for tl in range(TT):
                                g = gc[:, 4 * hf + h, tl * P:(tl + 1) * P]
                                a = nc.vector.tensor_tensor_scan(g, ones, g, 0.0, ALU.mult, ALU.add)
                        a.then_inc(g_done, 1)
                if u in (33, 35):
                    for kt in range(2 * (u - 33), 2 * (u - 33) + 4):
                        dve.wait_ge(oaTh_done, at2(lay, 8, kt + 2 - kt % 2))
                        nc.vector.scalar_tensor_tensor(oaTl[:, kt, :], wk[kt // 2 % 2][:, (kt % 2) * SEQ:(kt % 2 + 1) * SEQ],
                                                       cols[:, C2_OUT + kt:C2_OUT + kt + 1], oaTh[:, kt, :].bitcast(F32),
                                                       ALU.mult, ALU.subtract).then_inc(oaTl_done, 1)
                a, odd = divmod(u - AQ0, 2)
                if odd == 0 and 0 <= a < 6:
                    dve.wait_ge(asq_done, at2(lay, 6, a + 1))
                    nc.vector.tensor_scalar(msa[:], ssa[:], 1.0 / DH, EPS, ALU.mult, ALU.add).then_inc(ams_done, 1)
                a, odd = divmod(u - AQ0, 2)
                if odd == 1 and 0 <= a < 6:
                    x = stg[a % 2][:].rearrange("p t (h d) -> p t h d", d=DH)
                    x8 = stg[a % 2][:].rearrange("p t (h d) -> p (t h) d", d=DH)
                    r8 = rtm[:].rearrange("p t (h d) -> p t h d", d=DH)
                    dve.wait_ge(apow_done, at2(lay, 6, a + 1))
                    link(dve, nc.vector.tensor_tensor(x8, x8, per_head(rsa[:], 8), ALU.mult))
                    gain = cols[:, C2_QK + a * DH:C2_QK + (a + 1) * DH]
                    link(dve, nc.vector.tensor_tensor(x8, x8, gain.unsqueeze(1).broadcast_to((P, 8, DH)), ALU.mult))
                for hf, step, b0 in ((0, HG0 + LEVELS + 1, 2), (1, HG0 + NHG + 1, 0)):
                    if u == step:
                        dve.wait_ge(oh_sq, at2(lay, 2, hf + 1))
                        nc.vector.tensor_scalar(mso[:], sso[:], 1.0 / P, EPS, ALU.mult, ALU.add).then_inc(oh_ms, 1)
                    if u == step + 1 + hf:
                        dve.wait_ge(oh_pow, at2(lay, 2, hf + 1))
                        for i in range(2):
                            a = nc.vector.tensor_tensor(hv[:, :, 512 * hf + 256 * i:512 * hf + 256 * (i + 1)].rearrange("p t (h d) -> p h t d", d=P),
                                                        wk[b0 + i][:].rearrange("p (h t d) -> p h t d", h=2, t=TT),
                                                        rso[:, 4 * i:4 * i + 4].rearrange("p (h t) -> p h t", t=TT).unsqueeze(3).broadcast_to((P, 2, TT, P)), ALU.mult)
                        a.then_inc(oh_out, 1)
                if u == HG0 + NHG + 4:
                    dve.wait_ge(oh_out, at2(lay, 2, 2))
                    dve.wait_ge(hgs_done, at2(lay, 1, 1))
                    for hf in range(2):
                        g = hgt[:, :, halves(hf)]
                        nc.vector.tensor_tensor(g, g, hv[:, :, halves(hf)], ALU.mult).then_inc(oa_done, 1)
                hd, odd = divmod(u - ATT0 - 1, 2)
                if odd == 0 and 0 <= hd < ATT_HEADS:
                    if hd > 0:
                        dve.wait_ge(dexp_done, at2(lay, ATT_HEADS, hd))
                    for g in range(ATT_GROUPS):
                        dve.wait_ge(dsc_done, at2(lay, 3 * ATT_HEADS, 3 * hd + g + 1))
                        a = nc.vector.scalar_tensor_tensor(sma[:, g, :], wk[g][:, 0:384], DH ** -0.5,
                                                           kblk[:, K2_MASK + 384 * g:K2_MASK + 384 * (g + 1)], ALU.mult, ALU.add)
                    link(dve, a)
                    nc.vector.tensor_reduce(nma[:, 0:1], sma[:, :, 0:P], AX.XY, ALU.max, negate=True)
                    nc.vector.tensor_reduce(nma[:, 1:2], sma[:, :, P:384], AX.XY, ALU.max, negate=True).then_inc(dmax_done, 1)
                if u == 45:
                    for i in range(2):
                        dve.wait_ge(obTh_done, at2(lay, 2, i + 1))
                        nc.vector.tensor_tensor(obTl[:, 2 * i:2 * i + 2, :], wk[i][:].rearrange("p (k n) -> p k n", k=2),
                                                obTh[:, 2 * i:2 * i + 2, :].bitcast(F32), ALU.subtract).then_inc(obTl_done, 1)
                if u in (47, 48):
                    half = u - 47
                    for i in range(2):
                        kt = 4 * half + 2 * i
                        dve.wait_ge(mTh_done2, at2(lay, 4, 2 * half + i + 1))
                        nc.vector.tensor_tensor(xl[:, kt:kt + 2, :], wk[2 * half + i][:].rearrange("p (k n) -> p k n", k=2),
                                                xh[:, kt:kt + 2, :].bitcast(F32), ALU.subtract).then_inc(mTl_done2, 1)

        def mix2_pool(pool, lay):
            split_low(pool, nc.gpsimd, 2, POOLS, lay, mix_use(2))
            norm_pool(pool, lay, 1)
            for u in range(MIX2):
                n = u + 1 - HG0
                if 0 <= n < NHG and 0 < n % LEVELS < LEVELS - 1:
                    hf, lev = divmod(n, LEVELS)
                    L = 1 << (lev - 1)
                    g = gc[:, 4 * hf:4 * hf + 4, :].rearrange("p h (b l) -> p (h b) l", l=2 * L)
                    if lev == 1:
                        pool.wait_ge(g_done, at2(lay, 2, hf + 1))
                    if (LEVELS - 1) * hf + lev > 1:
                        pool.wait_ge(A_done, at2(lay, 2 * (LEVELS - 1), (LEVELS - 1) * hf + lev - 1))
                    nc.gpsimd.tensor_tensor(dl[:].rearrange("p h (b l) -> p (h b) l", l=2 * L), g,
                                            g[:, :, L - 1:L].broadcast_to((P, 4 * SEQ // (2 * L), 2 * L)), ALU.subtract).then_inc(diff_ready, 1)
                if 0 < u < MIX2 - 1 and slot_of(u + 2) == POOLS:
                    split_low(pool, nc.gpsimd, 2, POOLS, lay, mix_use(u + 2))
                for hf, step in ((0, HG0 + LEVELS + 1), (1, HG0 + NHG + 1)):
                    if u == step:
                        pool.wait_ge(oh_ms, at2(lay, 2, hf + 1))
                        nc.gpsimd.tensor_tensor(rso[:], mso[:], neghalf[:, 0:8], ALU.pow).then_inc(oh_pow, 1)
                a, odd = divmod(u - AQ0, 2)
                if odd == 0 and 0 <= a < 6:
                    pool.wait_ge(ams_done, at2(lay, 6, a + 1))
                    nc.gpsimd.tensor_tensor(rsa[:], msa[:], neghalf[:, 0:8], ALU.pow).then_inc(apow_done, 1)

        t_mix = {1: dict(sp=mix1_sp, pe=mix1_pe, act=mix1_act, dve=mix1_dve, pool=mix1_pool),
                 2: dict(sp=mix2_sp, pe=mix2_pe, act=mix2_act, dve=mix2_dve, pool=mix2_pool)}


        block = ctx.enter_context(nc.Block())

        @block.sync
        def _(sp):
            sp.dma_start(X[:, 0, :], t["x"][0:P, :]).then_inc(x_in[0], 16)
            sp.dma_start(konst[:], t["konst"]).then_inc(konst_in, 16)
            sp.dma_start(gain0[:], t["gain0"][0:P, :]).then_inc(gain0_in, 16)
            sp.dma_start(X[:, 1, :], t["x"][P:SEQ, :]).then_inc(x_in[1], 16)
            for blk in (1, 2):
                with sp.Fori((blk - 1) * LAYERS, blk * LAYERS) as lay:
                    l = lay if blk == 1 else lay - LAYERS
                    ffn_sp(sp, blk, lay, 0)
                    sp.wait_ge(x_ready, at(lay, 12, LOADED))
                    sp.dma_start(cols[:, 0:(NC1, NC2)[blk - 1]], t["cols"][blk][bass.ds(l * P, P), :]).then_inc(cols_in, 16)
                    sp.dma_start(kblk[:, 0:(NK1, NK2)[blk - 1]], t["kblk"][blk]).then_inc(kblk_in, 16)
                    post_sp(sp, blk, lay, 0)
                    t_mix[blk]["sp"](sp, lay)
                    sp.wait_ge(x_ready, at(lay, 12, LOADED + 4))
                    sp.dma_start(gain0[:], t["gain0"][bass.ds(lay * P + P, P), :]).then_inc(gain0_in, 16)
                    post_sp(sp, blk, lay, 1)
                    ffn_sp(sp, blk, lay, 1)
                    if blk == 1:
                        sp.wait_ge(x_ready, at(lay, 12, LOADED + 8))
                    post_sp(sp, blk, lay, 2)
            for s in range(SLOTS):
                sp.wait_ge(low_done[s], use(2, s, 2 * LAYERS, 0))
                sp.sem_inc(raw_in[s], 32)
            for tt in range(TT):
                sp.wait_ge(x_ready, LOADED + 12 * 2 * LAYERS - 2 * (TT - 1 - tt))
                sp.dma_start(t["out"][tt * P:(tt + 1) * P, :], X[:, tt, :]).then_inc(out_sent, 16)
            sp.wait_ge(out_sent, TT * 16)

        @block.tensor
        def _(pe):
            for s in range(SLOTS):
                pe.sem_inc(slot_used[s], FREE)
            norm_pe(pe, 0, 0, 0)
            for blk in (1, 2):
                with pe.Fori((blk - 1) * LAYERS, blk * LAYERS) as lay:
                    ffn_pe(pe, blk, lay, 0)
                    t_mix[blk]["pe"](pe, lay)
                    ffn_pe(pe, blk, lay, 1)
            norm_pe(pe, 2 * LAYERS - 1, 3, 1)

        @block.scalar
        def _(act):
            def to_first():
                for s in LEAD + UP[:1]:
                    split_high(act, 1, s, 0, 0)

            norm_act(act, 0, 0, to_first)
            for blk in (1, 2):
                with act.Fori((blk - 1) * LAYERS, blk * LAYERS) as lay:
                    ffn_act(act, blk, lay, 0)
                    post_act(act, blk, lay, 0, 0)
                    split_high(act, blk, LEAD[1], lay, FSTEPS)

                    def to_mixer():
                        post_act(act, blk, lay, 0, 1)
                        split_high(act, blk, slot_of(2), lay, mix_use(2))

                    norm_act(act, lay, 1, to_mixer)
                    t_mix[blk]["act"](act, lay)
                    post_act(act, blk, lay, 1, 0)
                    split_high(act, blk, LEAD[1], lay, ffn_use(blk, 1, LEAD[1]))

                    def to_ffn2():
                        post_act(act, blk, lay, 1, 1)
                        split_high(act, blk, UP[0], lay, ffn_use(blk, 1, UP[0]))

                    norm_act(act, lay, 2, to_ffn2)
                    ffn_act(act, blk, lay, 1)
                    post_act(act, blk, lay, 2, 0)
                    split_high(act, blk, LEAD[1], lay, ffn_use(blk, 1, LEAD[1]) + FSTEPS)

                    def to_next():
                        post_act(act, blk, lay, 2, 1)
                        split_high(act, blk, UP[0], lay, ffn_use(blk, 1, UP[0]) + FSTEPS)

                    norm_act(act, lay, 3, to_next)

        @block.vector
        def _(dve):
            for s in (0, 1):
                dve.sem_inc(low_done[s], FREE)
            dve.sem_inc(x_ready, LOADED)
            norm_dve(dve, 0, 0, 0)
            for s in LEAD:
                split_low(dve, nc.vector, 1, s, 0, 0)
            norm_dve(dve, 0, 0, 1)
            for blk in (1, 2):
                with dve.Fori((blk - 1) * LAYERS, blk * LAYERS) as lay:
                    per = LINKS[blk]
                    chain.update(n=0, lay=lay, per=per, off=0 if blk == 1 else LAYERS * (LINKS[1] - LINKS[2]))

                    def boundary(f):
                        for tt in range(TT):
                            post_dve(dve, blk, lay, f, tt)
                            norm_dve(dve, lay, f + 1, tt)

                    ffn_dve(dve, blk, lay, 0)
                    boundary(0)
                    t_mix[blk]["dve"](dve, lay)
                    boundary(1)
                    ffn_dve(dve, blk, lay, 1)
                    boundary(2)
                links[blk] = chain["n"]

        @block.gpsimd
        def _(pool):
            nc.gpsimd.memset(neghalf[:], -0.5).then_inc(const_set, 1)
            pool.sem_inc(low_done[POOLS], FREE)
            pool.wait_ge(const_set, 1)
            for blk in (1, 2):
                with pool.Fori((blk - 1) * LAYERS, blk * LAYERS) as lay:
                    ffn_pool(pool, blk, lay, 0)
                    post_pool(pool, blk, lay, 0, 0)
                    split_low(pool, nc.gpsimd, blk, LEAD[1], lay, FSTEPS)
                    post_pool(pool, blk, lay, 0, 1)
                    t_mix[blk]["pool"](pool, lay)
                    post_pool(pool, blk, lay, 1, 0)
                    split_low(pool, nc.gpsimd, blk, LEAD[1], lay, ffn_use(blk, 1, LEAD[1]))
                    post_pool(pool, blk, lay, 1, 1)
                    ffn_pool(pool, blk, lay, 1)
                    post_pool(pool, blk, lay, 2, 0)
                    split_low(pool, nc.gpsimd, blk, LEAD[1], lay, ffn_use(blk, 1, LEAD[1]) + FSTEPS)
                    post_pool(pool, blk, lay, 2, 1)
        assert links == LINKS, links


def constants():
    i = np.arange(P)
    konst = np.concatenate([np.eye(P), np.ones((P, P)), i[:, None] >= i[None, :]], 1).astype(np.float32)

    def logit_blocks(ok):
        return np.concatenate([ok[0:P, 0:P], ok[P:SEQ, 0:SEQ]], 1)

    tok = np.arange(SEQ)
    gap = tok[:, None] - tok[None, :]
    causal = np.where(logit_blocks(gap >= 0), 0.0, NEG)
    before = (gap > 0).T
    keep = np.concatenate([before[0:P, :], before[P:SEQ, P:SEQ]], 1)

    def angles(theta, width):
        inv = (np.float32(theta) ** (-np.arange(0, width, 2, dtype=np.float32) / np.float32(width))).astype(np.float32)
        a = (tok.astype(np.float32)[:, None] * inv[None, :]).astype(np.float32)
        return np.cos(a), np.sin(a)

    def by_tile(a):
        return a.reshape(TT, P, -1).transpose(1, 0, 2).reshape(P, -1)

    c1, s1 = angles(500000.0, ROT)
    kb1 = np.concatenate([causal, keep, np.where(keep, 0.0, NEG), by_tile(c1), by_tile(s1)], 1).astype(np.float32)
    c2, s2 = angles(10000.0, DH)
    masks = [np.where(logit_blocks((gap >= 0) & (gap <= w) & (gap % d == 0)), 0.0, NEG) for w, d in PATTERNS]
    levels = [np.eye(P)]
    for n in range(7):
        L = 1 << n
        same = i[:, None] // (2 * L) == i[None, :] // (2 * L)
        levels.append(same & (i[:, None] % (2 * L) < L) & (i[None, :] % (2 * L) >= L))
    kb2 = np.concatenate([by_tile(np.concatenate([c2, c2], 1)), by_tile(np.concatenate([-s2, s2], 1))] + masks + levels, 1).astype(np.float32)
    assert konst.shape[1] == NK0 and kb1.shape[1] == NK1 and kb2.shape[1] == NK2
    return konst, kb1, kb2


WEIGHTS = ["w_in", "w_diff_o", "w_sb_o", "w_moba_o", "w_out", "ffn1_wg", "ffn1_wu", "ffn1_wd", "ffn2_wg", "ffn2_wu", "ffn2_wd",
           "ffn1_w_in_2", "ffn1_w_out_2", "w_in_2", "w_branch_a_2", "w_branch_b_2", "w_out_2", "ffn2_w_in_2", "ffn2_w_out_2"]


def laid_out(inputs):
    arrays = {n: np.ascontiguousarray(inputs[n]) for n in WEIGHTS}
    arrays["x"] = np.ascontiguousarray(inputs["x"]).reshape(SEQ, D)

    def column(a):
        return np.asarray(a).reshape(-1, P).T

    def repeated(a):
        return np.tile(np.asarray(a).reshape(1, -1), (P, 1))

    def const(v):
        return np.full((P, 1), v, np.float32)

    one, two = [], []
    for l in range(LAYERS):
        start = 0.8 - 0.6 * math.exp(-0.3 * l)
        one.append(np.concatenate([column(inputs[n][l]) for n in ("g_ffn1_pre", "g_mix_pre", "g_ffn2_pre", "diff_norm_g")]
                                  + [const(start), const(1.0 - start)]
                                  + [repeated(inputs[n][l]) for n in ("lam_q1", "lam_k1", "lam_q2", "lam_k2")], 1))
        two.append(np.concatenate([column(inputs[n][l]) for n in ("ffn1_norm_2", "mix_norm_2", "ffn2_norm_2", "hgrn_out_norm_2")]
                                  + [column(inputs["hgrn_lb_logits_2"][m]) for m in range(LAYERS)]
                                  + [const(float(l))]
                                  + [repeated(inputs[n][l]) for n in ("attn_q_norm_2", "attn_k_norm_2")], 1))
    first = [inputs["g_ffn1_pre"][l] for l in range(LAYERS)] + [inputs["ffn1_norm_2"][l] for l in range(LAYERS)]
    arrays["gain0"] = np.ascontiguousarray(np.concatenate([column(g) for g in first + first[-1:]], 0))
    arrays["post"] = np.ascontiguousarray(np.concatenate([inputs[n][l:l + 1] for l in range(LAYERS) for n in ("g_ffn1_post", "g_mix_post", "g_ffn2_post")], 0))
    arrays["cols1"] = np.ascontiguousarray(np.concatenate(one, 0))
    arrays["cols2"] = np.ascontiguousarray(np.concatenate(two, 0))
    arrays["konst"], arrays["kblk1"], arrays["kblk2"] = constants()
    return arrays


def program(nc, shapes):
    dram = {n: nc.dram_tensor(f"in_{n}", s, F32, kind="ExternalInput").ap() for n, s in shapes.items()}
    out = nc.dram_tensor("out_x", (SEQ, D), F32, kind="ExternalOutput").ap()
    rows = {n: dram[n].rearrange("l k n -> (l k) n") for n in WEIGHTS }
    build(nc, {
        "x": dram["x"], "out": out, "konst": dram["konst"], "gain0": dram["gain0"], "kblk": {1: dram["kblk1"], 2: dram["kblk2"]},
        "cols": {1: dram["cols1"], 2: dram["cols2"]},
        "post": dram["post"],
        "ffn": {1: [(rows["ffn1_wg"], rows["ffn1_wu"], rows["ffn1_wd"], 0), (rows["ffn2_wg"], rows["ffn2_wu"], rows["ffn2_wd"], 0)],
                2: [(rows["ffn1_w_in_2"], rows["ffn1_w_in_2"], rows["ffn1_w_out_2"], FFN),
                    (rows["ffn2_w_in_2"], rows["ffn2_w_in_2"], rows["ffn2_w_out_2"], FFN)]},
        "w_in": rows["w_in"], "w_o": [rows["w_diff_o"], rows["w_sb_o"], rows["w_moba_o"]], "w_out": rows["w_out"],
        "w_in2": rows["w_in_2"], "w_a": rows["w_branch_a_2"], "w_b": rows["w_branch_b_2"], "w_out2": rows["w_out_2"],
    })


def kernel(**inputs):
    import concourse.bacc as _bacc
    from concourse.bass_utils import run_bass_kernel_spmd as _run

    arrays = laid_out(inputs)
    nc = _bacc.Bacc("TRN2", target_bir_lowering=False, num_devices=1)
    program(nc, {n: a.shape for n, a in arrays.items()})
    r = _run(nc, [{f"in_{n}": a for n, a in arrays.items()}], core_ids=[0])
    return r.results[0]["out_x"].reshape(1, SEQ, D)
```
